# Optimizing a Trainium2 kernel written in Bass

```python
import math
import jax, jax.numpy as jnp
from jax import lax
import numpy as np

D_MODEL = 1024
BATCH = 1
SEQ = 1024
DEPTH = 1
DEC_BATCH = 8
DEC_SEQ = 4
PAST_LEN = 8192
PAGE_SIZE = 128

H_A = 4
DV_A = D_MODEL // H_A
DK_A = DV_A // 2
QK_A = H_A * DK_A
CONV_W = 4
H_B = 4
DV_B = D_MODEL // H_B
DK_B = DV_B // 2
QK_B = H_B * DK_B
GLA_RANK = 16
GLA_TAU = 16.0
CHUNK = 64
D_FF = ((8 * D_MODEL // 3 + 255) // 256) * 256
EPS = 1e-6
SPLIT_SIZES = (2 * QK_A, H_A * DV_A, H_A * DV_A, H_A, H_A,
               QK_B, QK_B, H_B * DV_B, H_B * DV_B, GLA_RANK,
               D_MODEL, D_MODEL)
N_IN = 2 * QK_A + 2 * H_A * DV_A + 2 * H_A + 2 * QK_B + 2 * H_B * DV_B + GLA_RANK + 2 * D_MODEL

kernel_name = "hybrid_mlstm_gla_adaln_step"

def _rmsnorm(x, g):
    xf = x.astype(jnp.float32)
    y = xf * lax.rsqrt(jnp.mean(xf * xf, axis=-1, keepdims=True) + EPS)
    return y.astype(x.dtype) * g

def _to_chunks(a, L):
    B, T = a.shape[:2]
    a = a.reshape((B, T // L, L) + a.shape[2:])
    return jnp.transpose(a, (1, 0, 3, 2) + tuple(range(4, a.ndim)))

def _from_chunks(h, B, T):
    h = jnp.transpose(h, (1, 0, 3, 2, 4))
    return h.reshape(B, T, h.shape[3], h.shape[4])

def _mlstm(q, k, v, ig, lf, C0, n0, m0):
    B, T = q.shape[:2]
    L = math.gcd(T, CHUNK)
    mask = jnp.tril(jnp.ones((L, L), dtype=bool))
    xs = (_to_chunks(q, L), _to_chunks(k, L), _to_chunks(v, L), _to_chunks(ig, L), _to_chunks(lf, L))

    def step(carry, inp):
        C, n, m = carry
        qc, kc, vc, ic, fc = inp
        b = jnp.cumsum(fc, axis=-1)
        D = jnp.where(mask, b[..., :, None] - b[..., None, :] + ic[..., None, :], -jnp.inf)
        inter = b + m[..., None]
        m_t = jnp.maximum(jnp.max(D, axis=-1), inter)
        w = jnp.exp(D - m_t[..., None])
        wi = jnp.exp(inter - m_t)
        s = jnp.einsum('bhtd,bhsd->bhts', qc, kc) * w
        num = jnp.einsum('bhts,bhsv->bhtv', s, vc) + wi[..., None] * jnp.einsum('bhtd,bhdv->bhtv', qc, C)
        den = jnp.sum(s, axis=-1) + wi * jnp.einsum('bhtd,bhd->bht', qc, n)
        h = num / jnp.maximum(jnp.abs(den), jnp.exp(-m_t))[..., None]
        bL = b[..., -1]
        dec = bL[..., None] - b + ic
        m_new = jnp.maximum(bL + m, jnp.max(dec, axis=-1))
        wk = jnp.exp(dec - m_new[..., None])
        wC = jnp.exp(bL + m - m_new)
        C_new = wC[..., None, None] * C + jnp.einsum('bhs,bhsd,bhsv->bhdv', wk, kc, vc)
        n_new = wC[..., None] * n + jnp.einsum('bhs,bhsd->bhd', wk, kc)
        return (C_new, n_new, m_new), h

    (C1, n1, m1), hs = lax.scan(step, (C0, n0, m0), xs)
    return _from_chunks(hs, B, T), C1, n1, m1

def _gla(q, k, v, la, S0):
    B, T = q.shape[:2]
    L = math.gcd(T, CHUNK)
    mask = jnp.tril(jnp.ones((L, L), dtype=bool))[..., None]
    xs = (_to_chunks(q, L), _to_chunks(k, L), _to_chunks(v, L), _to_chunks(la, L))

    def step(S, inp):
        qc, kc, vc, lc = inp
        b = jnp.cumsum(lc, axis=2)
        decay = jnp.exp(jnp.where(mask, b[:, :, :, None, :] - b[:, :, None, :, :], -jnp.inf))
        A = jnp.einsum('bhtd,bhsd,bhtsd->bhts', qc, kc, decay)
        o = jnp.einsum('bhts,bhsv->bhtv', A, vc) + jnp.einsum('bhtd,bhdv->bhtv', qc * jnp.exp(b), S)
        bL = b[:, :, -1, :]
        S_new = jnp.exp(bL)[..., None] * S + jnp.einsum('bhsd,bhsv->bhdv', kc * jnp.exp(bL[:, :, None, :] - b), vc)
        return S_new, o

    S1, os_ = lax.scan(step, S0, xs)
    return _from_chunks(os_, B, T), S1

def _head_norm(h, g):
    hf = h * lax.rsqrt(jnp.mean(h * h, axis=-1, keepdims=True) + EPS)
    return hf * g

def _layer(x, c, state, p):
    conv_buf, C0, n0, m0, S0 = state
    (g_norm1, g_norm2, w_ada, b_ada, w_in, conv_w, conv_b, b_igate, b_fgate, g_head_a,
     w_alpha, b_alpha, g_head_b, w_out, w_ffn_gate, w_ffn_up, w_ffn_down) = p
    B, T, _ = x.shape
    f32 = jnp.float32
    ada = (c @ w_ada + b_ada)[:, None, :]
    shift1, scale1, gate1, shift2, scale2, gate2 = jnp.split(ada, 6, axis=-1)

    h = _rmsnorm(x, g_norm1) * (1.0 + scale1) + shift1
    z = h @ w_in
    idx = list(np.cumsum(SPLIT_SIZES)[:-1])
    qk_a, v_a, o_a, i_a, f_a, q_b, k_b, v_b, r_b, lr_b, g_a, g_b = jnp.split(z, idx, axis=-1)

    xpad = jnp.concatenate([conv_buf.astype(qk_a.dtype), qk_a], axis=1)
    conv = conv_b + sum(xpad[:, j:j + T] * conv_w[j] for j in range(CONV_W))
    new_conv = xpad[:, T:]
    qk = jax.nn.silu(conv).astype(f32)
    qa = qk[..., :QK_A].reshape(B, T, H_A, DK_A) * (DK_A ** -0.5)
    ka = qk[..., QK_A:].reshape(B, T, H_A, DK_A)
    va = v_a.astype(f32).reshape(B, T, H_A, DV_A)
    ig = (i_a + b_igate).astype(f32)
    lf = jax.nn.log_sigmoid((f_a + b_fgate).astype(f32))
    ha, C1, n1, m1 = _mlstm(qa, ka, va, ig, lf, C0.astype(f32), n0.astype(f32), m0.astype(f32))
    ha = _head_norm(ha, g_head_a.astype(f32)).reshape(B, T, D_MODEL).astype(x.dtype) * jax.nn.sigmoid(o_a)

    qb = q_b.astype(f32).reshape(B, T, H_B, DK_B) * (DK_B ** -0.5)
    kb = k_b.astype(f32).reshape(B, T, H_B, DK_B)
    vb = v_b.astype(f32).reshape(B, T, H_B, DV_B)
    la = (jax.nn.log_sigmoid((lr_b @ w_alpha + b_alpha).astype(f32)) / GLA_TAU).reshape(B, T, H_B, DK_B)
    hb, S1 = _gla(qb, kb, vb, la, S0.astype(f32))
    hb = _head_norm(hb, g_head_b.astype(f32)).reshape(B, T, D_MODEL).astype(x.dtype) * jax.nn.silu(r_b)

    y = (jax.nn.sigmoid(g_a) * ha + jax.nn.sigmoid(g_b) * hb) @ w_out
    x = x + gate1 * y

    h2 = _rmsnorm(x, g_norm2) * (1.0 + scale2) + shift2
    ffn = (jax.nn.silu(h2 @ w_ffn_gate) * (h2 @ w_ffn_up)) @ w_ffn_down
    x = x + gate2 * ffn
    dt = x.dtype
    return x, (new_conv.astype(dt), C1.astype(dt), n1.astype(dt), m1.astype(dt), S1.astype(dt))

def setup_inputs(seed: int = 0) -> dict:
    key = jax.random.key(seed)
    ks = jax.random.split(key, 32)
    nrm = jax.random.normal
    D = D_MODEL
    inp = {}
    inp["x_prompt"] = nrm(ks[0], (BATCH, SEQ, D), jnp.float32)
    inp["x_sample"] = nrm(ks[1], (DEC_BATCH, DEC_SEQ, D), jnp.float32)
    inp["state_conv"] = nrm(ks[2], (DEPTH, DEC_BATCH, CONV_W - 1, 2 * QK_A), jnp.float32)
    inp["state_C"] = 0.1 * nrm(ks[3], (DEPTH, DEC_BATCH, H_A, DK_A, DV_A), jnp.float32)
    inp["state_n"] = nrm(ks[4], (DEPTH, DEC_BATCH, H_A, DK_A), jnp.float32)
    inp["state_m"] = 0.5 * nrm(ks[5], (DEPTH, DEC_BATCH, H_A), jnp.float32)
    inp["state_S"] = (DK_B ** -0.5) * nrm(ks[6], (DEPTH, DEC_BATCH, H_B, DK_B, DV_B), jnp.float32)
    inp["c_prompt"] = nrm(ks[7], (BATCH, D), jnp.float32)
    inp["c_sample"] = nrm(ks[8], (DEC_BATCH, D), jnp.float32)
    inp["g_norm1"] = 1.0 + 0.05 * nrm(ks[9], (DEPTH, D), jnp.float32)
    inp["g_norm2"] = 1.0 + 0.05 * nrm(ks[10], (DEPTH, D), jnp.float32)
    inp["w_ada"] = 0.5 * D ** -0.5 * nrm(ks[11], (DEPTH, D, 6 * D), jnp.float32)
    inp["b_ada"] = 0.02 * nrm(ks[12], (DEPTH, 6 * D), jnp.float32)
    inp["w_in"] = D ** -0.5 * nrm(ks[13], (DEPTH, D, N_IN), jnp.float32)
    inp["conv_w"] = 0.5 * nrm(ks[14], (DEPTH, CONV_W, 2 * QK_A), jnp.float32)
    inp["conv_b"] = 0.02 * nrm(ks[15], (DEPTH, 2 * QK_A), jnp.float32)
    inp["b_igate"] = 0.1 * nrm(ks[16], (DEPTH, H_A), jnp.float32)
    inp["b_fgate"] = jnp.linspace(3.0, 6.0, H_A, dtype=jnp.float32)[None, :] + 0.1 * nrm(ks[17], (DEPTH, H_A), jnp.float32)
    inp["g_head_a"] = 1.0 + 0.05 * nrm(ks[18], (DEPTH, H_A, DV_A), jnp.float32)
    inp["w_alpha"] = GLA_RANK ** -0.5 * nrm(ks[19], (DEPTH, GLA_RANK, QK_B), jnp.float32)
    inp["b_alpha"] = 2.0 + 0.1 * nrm(ks[20], (DEPTH, QK_B), jnp.float32)
    inp["g_head_b"] = 1.0 + 0.05 * nrm(ks[21], (DEPTH, H_B, DV_B), jnp.float32)
    inp["w_out"] = D ** -0.5 * nrm(ks[22], (DEPTH, D, D), jnp.float32)
    inp["w_ffn_gate"] = D ** -0.5 * nrm(ks[23], (DEPTH, D, D_FF), jnp.float32)
    inp["w_ffn_up"] = D ** -0.5 * nrm(ks[24], (DEPTH, D, D_FF), jnp.float32)
    inp["w_ffn_down"] = D_FF ** -0.5 * nrm(ks[25], (DEPTH, D_FF, D), jnp.float32)
    inp["g_final"] = 1.0 + 0.05 * nrm(ks[26], (D,), jnp.float32)
    return inp

def reference(x_prompt, x_sample, state_conv, state_C, state_n, state_m, state_S, c_prompt, c_sample,
              g_norm1, g_norm2, w_ada, b_ada, w_in, conv_w, conv_b, b_igate, b_fgate, g_head_a,
              w_alpha, b_alpha, g_head_b, w_out, w_ffn_gate, w_ffn_up, w_ffn_down, g_final):
    xp, xs = x_prompt, x_sample
    Bp = xp.shape[0]
    dt = xp.dtype
    zero_state = (jnp.zeros((Bp, CONV_W - 1, 2 * QK_A), dt), jnp.zeros((Bp, H_A, DK_A, DV_A), dt),
                  jnp.zeros((Bp, H_A, DK_A), dt), jnp.zeros((Bp, H_A), dt), jnp.zeros((Bp, H_B, DK_B, DV_B), dt))
    new_p = [[] for _ in range(5)]
    new_s = [[] for _ in range(5)]
    for l in range(DEPTH):
        p = (g_norm1[l], g_norm2[l], w_ada[l], b_ada[l], w_in[l], conv_w[l], conv_b[l], b_igate[l], b_fgate[l],
             g_head_a[l], w_alpha[l], b_alpha[l], g_head_b[l], w_out[l], w_ffn_gate[l], w_ffn_up[l], w_ffn_down[l])
        xp, st_p = _layer(xp, c_prompt, zero_state, p)
        xs, st_s = _layer(xs, c_sample, (state_conv[l], state_C[l], state_n[l], state_m[l], state_S[l]), p)
        for j in range(5):
            new_p[j].append(st_p[j])
            new_s[j].append(st_s[j])
    y_prompt = _rmsnorm(xp, g_final)
    y_sample = _rmsnorm(xs, g_final)
    conv_p, C_p, n_p, m_p, S_p = [jnp.stack(a, axis=0) for a in new_p]
    conv_s, C_s, n_s, m_s, S_s = [jnp.stack(a, axis=0) for a in new_s]
    return (y_prompt, y_sample, conv_p, C_p, n_p, m_p, S_p, conv_s, C_s, n_s, m_s, S_s)


_drawn_inputs = setup_inputs


def setup_inputs(seed=0):
    import zlib

    import numpy as np

    out = dict(_drawn_inputs(seed))
    spreads = {}
    factors = {'g_head_a': 7.318, 'g_head_b': 5.242, 'g_norm2': 3.851}
    for name, (base, spread) in spreads.items():
        noise = np.random.default_rng([zlib.crc32(name.encode()), seed]).standard_normal(out[name].shape)
        drawn = base * np.exp(spread * noise) if base else spread * noise
        out[name] = __import__('jax').numpy.asarray(drawn.astype(out[name].dtype))
    for name, factor in factors.items():
        out[name] = (out[name] * factor).astype(out[name].dtype)
    return out
```

```python
from contextlib import ExitStack

import concourse.bass as bass
from concourse import mybir

F32 = mybir.dt.float32
F32R = mybir.dt.float32r
BF16 = mybir.dt.bfloat16
U8 = mybir.dt.uint8
ALU = mybir.AluOpType
ACT = mybir.ActivationFunctionType

P = 128
D = 1024
KC = D // P
SEQ = 1024
NSEQ, SLEN = 8, 4
NS = NSEQ * SLEN
T = SEQ + NS
NC = SEQ // P
NT = NC + 1
H, DK, DV = 4, 128, 256
VX = DV + 1
W4 = 4
RANK = 16
FF = 2816
FT = FF // P
EPS = 1e-6
QSCALE = DK ** -0.5
TAU = 16.0
BIG = 1e30
NPC = 3
PC = T // NPC
NCOND = 1 + NSEQ
ZP = SEQ + W4 - 1
ZS = SLEN + W4 - 1
ZN = ZP + NSEQ * ZS
ZO = ZN - (W4 - 1)
KEEP = (W4 - 1) * NCOND

QK = H * DK
C_QA, C_KA = 0, QK
C_VA = 2 * QK
C_OA = C_VA + H * DV
C_IF = C_OA + H * DV
C_QB = C_IF + 2 * H
C_KB = C_QB + QK
C_VB = C_KB + QK
C_RB = C_VB + H * DV
C_LR = C_RB + H * DV
C_GA = C_LR + RANK
C_GB = C_GA + D

V_BADA = 0
V_G1 = V_BADA + 6 * KC
V_G2 = V_G1 + KC
V_CW = V_G2 + KC
V_CB = V_CW + W4 * KC
V_HA = V_CB + KC
V_HB = V_HA + KC
V_AL = V_HB + KC
NV = V_AL + H

LEVELS = [64, 32, 16, 8, 4, 2, 1]
NL = len(LEVELS) + 1

ROW_A, ROW_W, ROW_L = 0, 32, 64


def wait(e, sem, v):
    if not (isinstance(v, int) and v <= 0):
        e.wait_ge(sem, v)


class Steps:

    def __init__(self, engine, sem, per=0):
        self.e, self.sem, self.per, self.base, self.n, self.i = engine, sem, per, None, 0, 0

    def turn(self, i):
        if self.per:
            if self.base is None:
                self.base = self.n
            self.i, self.n = i, 0

    def value(self):
        return self.i * self.per + ((self.base or 0) + self.n)

    def did(self, ins):
        ins.then_inc(self.sem, 1)
        self.n += 1
        return self.n

    def link(self, ins):
        self.did(ins)
        self.e.wait_ge(self.sem, self.value())


def bc(ap, n):
    return ap.to_broadcast(list(ap.shape[:-1]) + [n])


def mid(ap, n):
    return ap.unsqueeze(1).to_broadcast([ap.shape[0], n, ap.shape[1]])


def setup_phase(nc, g, a):
    with ExitStack() as ctx:
        sb = lambda n, s, d=F32: ctx.enter_context(nc.sbuf_tensor(n, s, d))
        sem = lambda n: ctx.enter_context(nc.semaphore(n))
        xs = sb("x_rows", [P, NT, D])
        vr = sb("vec_rows", [P, P])
        cr = sb("c_rows", [NCOND, D])
        nr = sb("n_rows", [NSEQ * H, DK])
        sr = sb("sconv_rows", [NSEQ * (W4 - 1), D])
        NW = 3
        wa = sb("w_ada_ring", [P, NW, KC, 2 * P])
        lmf = sb("level_masks_f", [P, NL, P])
        cT = g.cT
        am = sb("norm1_mult", [P, KC, NCOND])
        junk = sb("junk", [P, D])
        ssq = sb("ssq", [P, NT])
        rstd = sb("rstd", [P, NT])
        NTMP = 3
        tmp = sb("h_tmp", [P, NTMP, 4 * P])
        s_small, s_x = sem("small_loaded"), sem("x_loaded")
        s_wa = [sem(f"w_ada_loaded{i}") for i in range(NW)]
        s_const, s_pool = sem("constants"), sem("pool_steps")
        s_tr, s_trc = sem("small_transposed"), sem("small_copied")
        s_adau, s_ada = sem("w_ada_used"), sem("ada_full")
        s_ssq, s_t, s_sqrt, s_xn = sem("ssq_done"), sem("ms_done"), sem("sqrt_done"), sem("x_normed")
        s_dve = sem("dve_steps")
        s_xt = sem("x_transposed")
        s_ht, s_hi, s_lo = sem("h_affine"), sem("h_hi"), sem("h_lo")
        units = [(k, q) for q in range(3) for k in range(KC)]
        NB = 4
        bank = lambda u: g.ps[u % NB]
        SMALLB, ADAB = g.ps[4], g.ps[5]
        O_V, O_C, O_N, O_S = 0, P, P + KC * NCOND, P + KC * NCOND + NSEQ * H

        def cols(q):
            return (q * 4 * P, 4 * P) if q < 2 else (SEQ, NS)

        with nc.Block() as block:

            @block.sync
            def _(sp):
                def small(dst, src):
                    sp.dma_start(dst, src).then_inc(s_small, 16)
                small(vr[V_BADA:V_G1, :], a["b_ada"].rearrange("o (r c) -> (o r) c", c=P))
                small(vr[V_G1:V_G2, :], a["g_norm1"].rearrange("o (r c) -> (o r) c", c=P))
                small(vr[V_G2:V_CW, :], a["g_norm2"].rearrange("o (r c) -> (o r) c", c=P))
                small(vr[V_CW:V_CB, :], a["conv_w"].rearrange("o j (r c) -> (o j r) c", c=P))
                small(vr[V_CB:V_HA, :], a["conv_b"].rearrange("o (r c) -> (o r) c", c=P))
                small(vr[V_HA:V_HB, :], a["g_head_a"].rearrange("o h (r c) -> (o h r) c", c=P))
                small(vr[V_HB:V_AL, :], a["g_head_b"].rearrange("o h (r c) -> (o h r) c", c=P))
                small(vr[V_AL:NV, :], a["b_alpha"].rearrange("o (r c) -> (o r) c", c=P))
                small(cr[0:1, :], a["c_prompt"])
                small(cr[1:NCOND, :], a["c_sample"])
                small(nr[:, :], a["state_n"].rearrange("o b h d -> (o b h) d"))
                small(sr[:, :], a["state_conv"].rearrange("o b j c -> (o b j) c"))
                wsrc = a["w_ada"][0].rearrange("(k p) n -> p k n", p=P)
                for n in range(KC):
                    if n >= NW:
                        sp.wait_ge(s_adau, n - NW + 1)
                    sp.dma_start(wa[:, n % NW], wsrc[:, :, n * 2 * P:(n + 1) * 2 * P]).then_inc(s_wa[n % NW], 16)
                    if n == 1:
                        sp.dma_start(xs[:, 0:NC, :], a["x_prompt"][0].rearrange("(t p) d -> p t d", p=P)).then_inc(s_x, 16)
                        sp.dma_start(xs[0:NS, NC, :], a["x_sample"].rearrange("b t d -> (b t) d")).then_inc(s_x, 16)

            @block.gpsimd
            def _(pool):
                st = Steps(pool, s_pool)
                ge = ALU.is_ge

                def keep(v, base, pattern, chan, fill=0.0, op=ge):
                    st.link(pool.affine_select(out=v, in_=v, compare_op=op, fill=fill, base=base,
                                               pattern=pattern, channel_multiplier=chan))
                st.link(pool.memset(g.ident[:, :], 0.0))
                keep(g.ident[:, :], 0, [[-1, P]], 1, fill=1.0, op=ALU.not_equal)
                pool.memset(g.ones[:, :], 1.0).then_inc(s_const, 1)
                st.link(pool.memset(g.cmask[:, :], BIG))
                keep(g.cmask[:, :], 0, [[1, P]], -1, fill=-BIG)
                st.link(pool.memset(g.cmask_s[:, :], BIG))
                keep(g.cmask_s[:, :], 0, [[1, NS]], -1, fill=-BIG)
                v = g.cmask_s[:, :].rearrange("s (b r) -> s b r", r=SLEN)
                keep(v, SLEN - 1, [[SLEN, NSEQ], [0, SLEN]], -1, fill=-BIG)
                keep(v, 0, [[-SLEN, NSEQ], [0, SLEN]], 1, fill=-BIG)
                st.link(pool.memset(g.seqcol[:, :], 1.0))
                keep(g.seqcol[:, :], SLEN - 1, [[SLEN, NSEQ]], -1)
                keep(g.seqcol[:, :], 0, [[-SLEN, NSEQ]], 1)
                st.link(pool.memset(g.seqrow[:, :, :], 1.0))
                keep(g.seqrow[:, :, :], SLEN - 1, [[SLEN, NSEQ], [-1, NS]], 0)
                keep(g.seqrow[:, :, :], 0, [[-SLEN, NSEQ], [1, NS]], 0)
                st.link(pool.memset(lmf[:, :, :], 0.0))
                for l, hs in enumerate(LEVELS):
                    n = P // (2 * hs)
                    v = lmf[:, l, :].rearrange("s (n w) -> s n w", w=2 * hs)[:, :, hs:2 * hs]
                    st.link(pool.memset(v, 1.0))
                    keep(v, 0, [[-2 * hs, n], [0, hs]], 1)
                    keep(v, hs - 1, [[2 * hs, n], [0, hs]], -1)
                st.link(pool.tensor_copy(lmf[:, NL - 1, :], g.ident[:, :]))
                st.link(pool.tensor_copy(g.lmask[:, :, :], lmf[:, :, :]))
                st.link(pool.memset(g.reset[:, :], 1.0))
                st.link(pool.memset(g.reset[:, 0:SEQ].rearrange("p (c t) -> p c t", t=P)[:, :, 0:1], 0.0))
                st.link(pool.memset(g.reset[:, SEQ:T].rearrange("p (b t) -> p b t", t=SLEN)[:, :, 0:1], 0.0))
                pool.memset(g.nout[:, :], 0.0).then_inc(s_const, 1)
                for u, (k, q) in enumerate(units):
                    c0, n = cols(q)
                    pool.wait_ge(s_hi, u + 1)
                    pool.tensor_tensor(g.Hl[:, k, c0:c0 + n], tmp[:, u % NTMP, 0:n], g.Hh[:, k, c0:c0 + n].bitcast(F32),
                                       ALU.subtract).then_inc(s_lo, 1)

            @block.tensor
            def _(pe):
                pe.wait_ge(s_small, 12 * 16)
                pe.wait_ge(s_const, 2)
                pe.transpose(SMALLB[:, O_V:O_V + NV], vr[0:NV, :], g.ident[0:NV, 0:NV])
                for k in range(KC):
                    pe.transpose(SMALLB[:, O_C + k * NCOND:O_C + (k + 1) * NCOND], cr[:, k * P:(k + 1) * P],
                                 g.ident[0:NCOND, 0:NCOND])
                pe.transpose(SMALLB[:, O_N:O_N + NSEQ * H], nr[:, :], g.ident[0:NSEQ * H, 0:NSEQ * H])
                m = NSEQ * (W4 - 1)
                last = None
                for k in range(KC):
                    if O_S + (k + 1) * m > 512:
                        raise ValueError("the small transposes outgrow their bank")
                    last = pe.transpose(SMALLB[:, O_S + k * m:O_S + (k + 1) * m], sr[:, k * P:(k + 1) * P], g.ident[0:m, 0:m])
                last.then_inc(s_tr, 1)
                pe.wait_ge(s_trc, 1)
                for n in range(2 * KC):
                    if n % 2 == 0:
                        pe.wait_ge(s_wa[(n // 2) % NW], 16 * (n // 2 // NW + 1))
                    for k in range(KC):
                        last = pe.matmul(ADAB[:, n * NCOND:(n + 1) * NCOND], wa[:, (n // 2) % NW, k, (n % 2) * P:(n % 2 + 1) * P],
                                         cT[:, k, :], start=(k == 0), stop=(k == KC - 1))
                    if n % 2:
                        last.then_inc(s_adau, 1)
                pe.wait_ge(s_xn, NT)
                for u, (k, q) in enumerate(units):
                    if u >= NB:
                        pe.wait_ge(s_ht, u - NB + 1)
                    for t in range(4 * q, min(4 * q + 4, NT)):
                        n = P if t < NC else NS
                        last = pe.transpose(bank(u)[:, (t - 4 * q) * P:(t - 4 * q) * P + n], xs[0:n, t, k * P:(k + 1) * P],
                                            g.ident[0:n, 0:n])
                    last.then_inc(s_xt, 1)

            @block.scalar
            def _(act):
                act.wait_ge(s_x, 32)
                act.wait_ge(s_t, 1)
                for t in range(NT):
                    n = P if t < NC else NS
                    if t:
                        act.wait_ge(s_ssq, t)
                    act.activation(junk[0:n, :], xs[0:n, t, :], ACT.Square, accum_out=ssq[0:n, t:t + 1]).then_inc(s_ssq, 1)
                act.wait_ge(s_t, 2)
                act.activation(rstd[:, :], ssq[:, :], ACT.Sqrt).then_inc(s_sqrt, 1)
                for u, (k, q) in enumerate(units):
                    c0, n = cols(q)
                    act.wait_ge(s_ht, u + 1)
                    act.activation(g.Hh[:, k, c0:c0 + n], tmp[:, u % NTMP, 0:n], ACT.Copy).then_inc(s_hi, 1)

            @block.vector
            def _(dve):
                st = Steps(dve, s_dve)
                dve.memset(ssq[:, :], 1.0).then_inc(s_t, 1)
                dve.wait_ge(s_tr, 1)
                dve.tensor_copy(cT[:, :, :], SMALLB[:, O_C:O_N].rearrange("p (k c) -> p k c", c=NCOND)).then_inc(s_trc, 1)
                st.link(dve.tensor_copy(g.vec[:, 0:NV], SMALLB[:, O_V:O_V + NV]))
                dve.tensor_copy(g.n0T[:, :], SMALLB[:, O_N:O_S])
                m = NSEQ * (W4 - 1)
                dve.tensor_copy(g.sconvT[:, :, :], SMALLB[:, O_S:O_S + KC * m].rearrange("p (k c) -> p k c", c=m))
                st.link(dve.tensor_scalar(g.vec[:, V_HA:V_AL], g.vec[:, V_HA:V_AL], 0.25, None, ALU.mult))
                dve.wait_ge(s_ssq, NT)
                dve.tensor_scalar(ssq[:, :], ssq[:, :], 1.0 / D, EPS, ALU.mult, ALU.add).then_inc(s_t, 1)
                dve.wait_ge(s_sqrt, 1)
                st.link(dve.reciprocal(ssq[:, :], rstd[:, :]))
                for t in range(NT):
                    n = P if t < NC else NS
                    dve.tensor_scalar(xs[0:n, t, :], xs[0:n, t, :], ssq[0:n, t:t + 1], None, ALU.mult).then_inc(s_xn, 1)
                dve.wait_ge(s_adau, KC)
                st.link(dve.tensor_tensor(g.ada[:, 0:2 * KC, :], ADAB[:, 0:2 * KC * NCOND].rearrange("p (n c) -> p n c", c=NCOND),
                                          bc(g.vec[:, 0:2 * KC].unsqueeze(2), NCOND), ALU.add))
                st.link(dve.scalar_tensor_tensor(am[:, :, :], g.ada[:, KC:2 * KC, :], 1.0,
                                                 bc(g.vec[:, V_G1:V_G1 + KC].unsqueeze(2), NCOND), ALU.add, ALU.mult))
                for u, (k, q) in enumerate(units):
                    dve.wait_ge(s_xt, u + 1)
                    if u >= NTMP:
                        dve.wait_ge(s_lo, u - NTMP + 1)
                    if q < 2:
                        dve.tensor_scalar(tmp[:, u % NTMP, :], bank(u)[:, :], am[:, k, 0:1], g.ada[:, k, 0:1],
                                          ALU.mult, ALU.add).then_inc(s_ht, 1)
                    else:
                        v = tmp[:, u % NTMP, 0:NS].rearrange("p (b r) -> p b r", r=SLEN)
                        st.link(dve.tensor_tensor(v, bank(u)[:, 0:NS].rearrange("p (b r) -> p b r", r=SLEN),
                                                  bc(am[:, k, 1:NCOND].unsqueeze(2), SLEN), ALU.mult))
                        dve.tensor_tensor(v, v, bc(g.ada[:, k, 1:NCOND].unsqueeze(2), SLEN), ALU.add).then_inc(s_ht, 1)


TILES = {"S": ["small", "q", "v0", "k", "v1"],
         "A": ["q", "v0", "k", "v1", "o0", "g0", "o1", "g1"],
         "B": ["q", "v0", "k", "v1", "o0", "g0", "o1", "g1"],
         "L": ["o0", "g0", "o1", "g1"]}
NS_TILES, NW_TILES = len(TILES["S"]), len(TILES["A"])
COLUMN = {("A", "q"): (C_QB, DK), ("A", "k"): (C_KB, DK), ("A", "v"): (C_VB, DV), ("A", "o"): (C_OA, DV), ("A", "g"): (C_GA, DV),
          ("B", "q"): (C_QA, DK), ("B", "k"): (C_KA, DK), ("B", "v"): (C_VA, DV), ("B", "o"): (C_RB, DV), ("B", "g"): (C_GB, DV)}
CHAIN = [f"chunk{c}" for c in range(NC)]
SAMPLE = [f"sample{b}" for b in range(NSEQ)]
AT_SLOT = {
    "S": [("rows", 6), ("conv_q", 14), ("silu_q", 17), ("vt0", 19), ("rows_t", 21), ("conv_k", 24), ("silu_k", 28), ("vt1", 29)],
    "A": [("select", 0), ("decay", 1), ("scores", 4), ("interq", 6), ("keys", 8), ("masked", 9), ("vt0", 14), ("vt1", 26)]
    + [(s, 11 + 2 * n) for n, s in enumerate(CHAIN)] + [("sample_out", 28)] + [(s, 29 + n) for n, s in enumerate(SAMPLE)]
    + [("gate0", 37), ("norm", 39), ("turn0", 44), ("gate1", 47), ("turn1", 47)],
    "B": [("alpha", 0), ("sums", 2)] + [(f"level{l}", 4 + 3 * l) for l in range(NL)] + [("keys", 27), ("masked", 28)]
    + [("conv_q", 6), ("silu_q", 10), ("vt0", 14), ("conv_k", 18), ("silu_k", 22), ("vt1", 26), ("gate_r0", 30), ("gate_r1", 42)]
    + [(s, 29 + n) for n, s in enumerate(CHAIN)] + [("sample_out", 37)] + [(s, 38 + n // 3) for n, s in enumerate(SAMPLE)]
    + [("gate0", 37), ("norm", 42), ("turn0", 46), ("gate1", 47), ("turn1", 47)],
}
for _w in "AB":
    AT_SLOT[_w] += [(f"ada_load{q}", 12 * q) for q in range(4)] + [(f"ada{q}", 12 * q + 9) for q in range(4)]
AT_SLOT["L"] = sorted([(s, {"gate_r0": 6, "gate0": 12, "gate_r1": 18, "gate1": 23, "norm": 23, "turn0": 23, "turn1": 23}.get(s, n // 2))
                       for s, n in AT_SLOT["B"] if s not in ("conv_q", "conv_k", "silu_q", "silu_k", "vt0", "vt1")],
                      key=lambda x: x[1])
USES = {"decay": 3, "scores": 3, "interq": 3, "keys": 3, "vt0": 3, "vt1": 3, "sample_out": 1, "turn0": 3, "turn1": 3,
        "alpha": 3, "rows_t": 3, **{s: 2 for s in CHAIN}, **{s: 1 for s in SAMPLE}, **{f"ada{q}": 1 for q in range(4)},
        **{f"level{l}": (3 if l >= NL - 3 else 2) for l in range(NL)}}


def timeline(w):
    out, stages = [], sorted(AT_SLOT[w], key=lambda x: x[1])
    for s in range(6 * len(TILES[w])):
        out.append(("piece", s // 6, s // 3 % 2, s % 3))
        out += [(n,) for n, at in stages if at == s]
    assert len([x for x in out if len(x) == 1]) == len(stages)
    return out


TIMELINE = {w: timeline(w) for w in TILES}
USE = {w: {} for w in TILES}
NUSE = {}
for _w in TILES:
    _n = 0
    for _x in TIMELINE[_w]:
        if len(_x) == 1 and _x[0] in USES:
            USE[_w][_x[0]] = _n
            _n += USES[_x[0]]
    NUSE[_w] = _n
BEGUN = 1
NRB = 4


def uses_before(w, i, n):
    b = n % NRB
    mine = lambda w, m: sum(1 for x in range(m) if x % NRB == b)
    total, own = NUSE["S"], mine("S", NUSE["S"])
    if w == "S":
        return n, mine("S", n)
    total, own = total + i * (NUSE["A"] + NUSE["B"]), own + i * (mine("A", NUSE["A"]) + mine("B", NUSE["B"]))
    if w in "BL":
        total, own = total + NUSE["A"], own + mine("A", NUSE["A"])
    return total + n, own + mine(w, n)


def tile_index(w, i, l):
    return l if w == "S" else i * 2 * NW_TILES + (NS_TILES + l + (NW_TILES if w in "BL" else 0))


def after(w, i, l, h, by):
    l, h = l + (h + by) // 2, (h + by) % 2
    while l >= len(TILES[w]):
        l -= len(TILES[w])
        if w == "L":
            return None
        if w == "B":
            w, i = "A", i + 1
        else:
            w, i = ("A" if w == "S" else "L" if isinstance(i, int) and i == H - 1 else "B"), i
    return w, i, l, h


def static(i, per, k, n):
    assert per % n == 0
    return k % n, i * (per // n) + k // n


def mixer_phase(nc, g, a, loops=True):
    with ExitStack() as ctx:
        sb = lambda n, s, d=F32: ctx.enter_context(nc.sbuf_tensor(n, s, d))
        sem = lambda n: ctx.enter_context(nc.semaphore(n))
        RAW, SPL = 4, 2
        raw = sb("w_raw", [P, RAW, 4, P])
        Wh = sb("w_hi", [P, SPL, 4, P], F32R)
        Wl = sb("w_lo", [P, SPL, 4, P], F32R)
        Q = [sb("q_a", [P, T]), sb("q_b", [P, T])]
        K = [sb("k_a", [P, T]), sb("k_b", [P, T])]
        V = [sb("v_a", [P, NT, VX]), sb("v_b", [P, NT, VX])]
        Z = sb("conv_in", [P, ZN])
        CV = sb("conv_out", [P, ZN])
        VS = sb("v_stage", [P, T])
        G = sb("gate", [P, 2, T])
        TG = sb("gate_t", [P, T])
        AT = sb("scores_t", [P, T])
        QD = sb("q_decayed", [P, T])
        KD = sb("k_decayed", [P, NT * P])
        TA = sb("temp_a", [P, T])
        TB = sb("temp_b", [P, T])
        ST = sb("sample_state", [P, NSEQ, VX])
        SS = sb("state", [P, 2, VX])
        M = sb("mix", [P, 2, T])
        HS = sb("sample_heads", [P, VX])
        QM = sb("q_masked", [P, NSEQ, NS])
        rows = sb("gate_rows", [P, T])
        cols = sb("gate_cols", [P, NT, 3 * H])
        hcol = sb("head_cols", [P, NT, 3])
        wcr = sb("carry_rows", [H, 2 * NC])
        wcs = sb("carry_sel", [H, 2 * NC])
        sdec = sb("state_decay", [P, 2 * NC])
        wal = sb("w_alpha_all", [P, QK])
        walh = sb("w_alpha_head", [P, DK])
        bif = sb("b_if", [H, 2])
        m0 = sb("m0", [H, NSEQ])
        me = sb("m_ends", [H, 4, 2 * NC])
        ssq = sb("head_ssq", [P, NT])
        den = sb("head_den", [P, NT])
        ms = sb("head_ms", [P, NT])
        scl = sb("head_scale", [P, NT])
        wad = sb("w_ada_tile", [P, KC, P])

        s_w = [sem(f"w_loaded{n}") for n in range(RAW)]
        s_zero = sem("w_raw_zeroed")
        s_hi, s_lo, s_used = sem("w_hi_made"), sem("w_lo_made"), sem("w_used")
        s_piece = sem("pieces_full")
        s_pfree = [sem(f"piece_bank_free{n}") for n in range(4)]
        s_full = sem("rec_bank_full")
        s_free = [sem(f"rec_bank_free{n}") for n in range(NRB)]
        s_small, s_init = sem("small_in"), sem("buffers_set")
        s_dve, s_pool = sem("dve_chain"), sem("pool_chain")
        s_r1, s_r2, s_r3, s_rows = sem("rows_x"), sem("rows_exp"), sem("rows_args"), sem("rows_ready")
        s_cols = sem("gate_cols_ready")
        s_cv, s_th, s_silu = sem("conv_done"), sem("conv_tanh"), sem("conv_silu")
        s_sel, s_warg, s_wexp = sem("rows_selected"), sem("decay_args"), sem("decay_exp")
        s_qd, s_km = sem("q_decayed_ready"), sem("sample_masked")
        s_hc = sem("heads_copied")
        s_stl, s_sts = sem("sample_state_loaded"), sem("states_stored")
        s_ms, s_sq, s_hn = sem("head_ms_ready"), sem("head_sqrt"), sem("heads_normed")
        s_gr, s_gate, s_sum = sem("gate_r"), sem("gate_ready"), sem("mixers_summed")
        s_mst = sem("mix_stored")
        s_x, s_nab, s_ln, s_b = sem("alpha_x"), sem("alpha_nab"), sem("alpha_ln"), sem("b_sums")
        s_d, s_E, s_qe, s_ke, s_at0 = sem("level_diff"), sem("level_exp"), sem("level_q"), sem("level_k"), sem("scores_zeroed")
        s_wah = sem("w_alpha_sliced")
        s_kt = sem("k_scaled")
        s_adl = sem("ada_tile_loaded")

        w_in = a["w_in"][0].rearrange("(k p) n -> p k n", p=P)
        w_ada = a["w_ada"][0].rearrange("(k p) n -> p k n", p=P)
        isB = lambda w: w in "BL"

        def half(w, i, l, h):
            per = 4 * NW_TILES
            if w == "S":
                k, j = 2 * l + h, 0
            else:
                k, j = 2 * (NS_TILES + l + (NW_TILES if isB(w) else 0)) + h, i
            r, turns = static(j, per, k, RAW)
            s, _ = static(j, per, k, SPL)
            return r, s, turns, j * per + k

        def piece(w, i, l, c):
            per = 3 * 2 * NW_TILES
            if w == "S":
                k, j = 3 * l + c, 0
            else:
                k, j = 3 * (NS_TILES + l + (NW_TILES if isB(w) else 0)) + c, i
            return static(j, per, k, 4)

        def two(w, i, per=1, first=0):
            return i * (2 * per) + (first + (per if isB(w) else 0))

        def span(c):
            return c * PC, PC

        def wait_piece(e, w, i, l, c):
            if c < 2:
                t = tile_index(w, i, l)
                e.wait_ge(s_piece, t * 2 + (c + 1))
            else:
                e.wait_ge(s_used, half(w, i, l, 1)[3] + 1)

        def wait_evacuated(e, w, i, l):
            b, turns = piece(w, i, l, NPC - 1)
            e.wait_ge(s_pfree[b], turns + 1)

        def wait_use(e, w, i, n):
            e.wait_ge(s_full, uses_before(w, i, n)[0] + 1)

        def apart(e):
            e.nop(nofuse=True)

        def wait_read_use(e, w, i, n):
            e.wait_ge(s_free[n % NRB], uses_before(w, i, n)[1] + 1)

        def wait_read(e, w, i, stage):
            wait_read_use(e, w, i, USE[w][stage] + USES[stage] - 1)

        RB = lambda n: g.ps[4 + n % NRB]
        free = lambda n: s_free[n % NRB]
        PARTS = [(0, 512), (512, 512), (SEQ, NS)]

        def chunks(v):
            return v[:, 0:SEQ].rearrange("p (c t) -> p c t", t=P)

        def seqs(v):
            return v[:, SEQ:T].rearrange("p (b t) -> p b t", t=SLEN)

        def run(engine, turn, body):
            body("S", 0)
            if loops:
                with engine.Fori(0, H - 1) as i:
                    body("A", i)
                    body("B", i)
            else:
                for i in range(H - 1):
                    body("A", i)
                    body("B", i)
            body("A", H - 1)
            body("L", H - 1)

        with nc.Block() as block:

            @block.sync
            def _(sp):
                def load_half(w, i, l, h):
                    r, _, turns, before = half(w, i, l, h)
                    wait(sp, s_lo, before - (RAW - 1))
                    name = TILES[w][l]
                    dst = raw[:, r]
                    if name == "small":
                        sp.wait_ge(s_zero, 1)
                        for c0, n, at in ((C_IF, H, 0), (C_IF + H, H, 32), (C_LR, RANK, 64)):
                            sp.dma_start(dst[:, :, at:at + n], w_in[:, 4 * h:4 * h + 4, c0:c0 + n]).then_inc(s_w[r], 16)
                        return
                    base, step = COLUMN["B" if w in "SL" else w, name[0]]
                    head = 0 if w == "S" else i + 1 if w == "B" and name[0] in "qkv" else i
                    c0 = head * step + (base + (P if name[1:] == "1" else 0))
                    src = w_in[:, 4 * h:4 * h + 4, bass.ds(c0, P)]
                    sp.dma_start(dst, src).then_inc(s_w[r], 16)

                small = [(bif[:, 0:1], a["b_igate"].rearrange("o h -> h o")), (bif[:, 1:2], a["b_fgate"].rearrange("o h -> h o")),
                         (m0[:, :], a["state_m"][0].rearrange("b h -> h b")), (wal[64:64 + RANK, :], a["w_alpha"][0])]
                sp.nop().then_inc(s_sts, BEGUN)
                sp.nop().then_inc(s_mst, BEGUN)
                load_half("S", 0, 0, 0)
                load_half("S", 0, 0, 1)
                for dst, src in small:
                    sp.dma_start(dst, src, allow_slow_non_contiguous=True).then_inc(s_small, 16)
                load_half("S", 0, 1, 0)

                def window(w, i):
                    for x in TIMELINE[w]:
                        if x[0] == "piece":
                            _, l, h, c = x
                            nxt = after(w, i, l, h, RAW - 1)
                            if c == 0 and nxt:
                                load_half(*nxt)
                        elif x[0].startswith("ada_load"):
                            q = int(x[0][-1])
                            n = two(w, i, 4) + q
                            wait_use(sp, w, i, USE[w][f"ada{q - 1}"] if q else 0)
                            sp.dma_start(wad[:, :, :], w_ada[:, :, bass.ds(n * P + 2 * D, P)]).then_inc(s_adl, 16)
                            if q == 0:
                                sp.wait_ge(s_sts, BEGUN + two(w, i, 32))
                                apart(sp)
                                sp.wait_ge(s_ms, BEGUN + two(w, i))
                                src = a["state_S"] if isB(w) else a["state_C"]
                                sp.dma_start(ST[:, :, 0:DV], src[0, :, bass.ds(i, 1)].rearrange("b h d v -> d (h b) v")).then_inc(s_stl, 16)
                        elif x[0] == "norm":
                            wait_read(sp, w, i, SAMPLE[-1])
                            dst = a["S_p"] if isB(w) else a["C_p"]
                            sp.dma_start(dst[0, 0, bass.ds(i, 1)].rearrange("h d v -> d h v"), SS[:, 1:2, 0:DV]).then_inc(s_sts, 16)
                            dst = a["S_s"] if isB(w) else a["C_s"]
                            sp.dma_start(dst[0, :, bass.ds(i, 1)].rearrange("b h d v -> d (h b) v"), ST[:, :, 0:DV]).then_inc(s_sts, 16)
                        elif x[0] == "rows_t":
                            sp.wait_ge(s_rows, 1)
                            sp.dma_start(a["m_p"][0].rearrange("o h -> h o"), me[:, 1, NC - 1:NC], allow_slow_non_contiguous=True).then_inc(s_small, 16)
                            sp.dma_start(a["m_s"][0].rearrange("b h -> h b"), me[:, 1, NC:2 * NC], allow_slow_non_contiguous=True).then_inc(s_small, 16)
                    if isB(w):
                        sp.wait_ge(s_sum, BEGUN + i * 2 + 2)
                        sp.dma_start(g.mix_d[:, bass.ds(i * 2, 2), :], M[:, :, :]).then_inc(s_mst, 16)
                run(sp, None, window)
                sp.wait_ge(s_small, 16 * (len(small) + 2))
                sp.wait_ge(s_sts, BEGUN + 32 * 2 * H)
                sp.wait_ge(s_mst, BEGUN + 16 * H)

            @block.tensor
            def _(pe):
                def mm_piece(w, i, l, h, c):
                    _, s, _, before = half(w, i, l, h)
                    b, turns = piece(w, i, l, c)
                    if c == 0:
                        pe.wait_ge(s_lo, before + 1)
                    if h == 0:
                        wait(pe, s_pfree[b], turns)
                    c0, n = span(c)
                    for k in range(4):
                        for m, (x, y) in enumerate(((Wh, g.Hh), (Wh, g.Hl), (Wl, g.Hh))):
                            last = pe.matmul(g.ps[b][:, 0:n], x[:, s, k, :], y[:, 4 * h + k, c0:c0 + n],
                                             start=(h == 0 and k == 0 and m == 0), stop=(h == 1 and k == 3 and m == 2))
                    if c == 2:
                        last.then_inc(s_used, 1)
                    elif h == 1:
                        last.then_inc(s_piece, 1)

                def window(w, i):
                    hd = 1 if isB(w) else 0
                    vw = DV if isB(w) else VX
                    q, k, v = Q[hd], K[hd], V[hd]

                    def use(n):
                        wait(pe, free(n), uses_before(w, i, n)[1])
                        return RB(n)

                    def full(ins):
                        ins.then_inc(s_full, 1)

                    def scores(n, kk, qq, samples=True):
                        for b in range(2):
                            bank = use(n + b)
                            for c in range(4 * b, 4 * b + 4):
                                last = pe.matmul(bank[:, (c % 4) * P:(c % 4 + 1) * P], kk[:, c * P:(c + 1) * P],
                                                 qq[:, c * P:(c + 1) * P], start=True, stop=True)
                            full(last)
                        if samples:
                            bank = use(n + 2)
                            apart(pe)
                            full(pe.matmul(bank[0:NS, 0:NS], kk[:, SEQ:T], qq[:, SEQ:T], start=True, stop=True))

                    def turned(n, src):
                        for b in range(2):
                            bank = use(n + b)
                            for c in range(4 * b, 4 * b + 4):
                                last = pe.transpose(bank[:, (c % 4) * P:(c % 4 + 1) * P], src[:, c * P:(c + 1) * P], g.ident[:, :])
                            full(last)
                        full(pe.transpose(use(n + 2)[0:NS, 0:P], src[:, SEQ:T], g.ident[:, :]))

                    for x in TIMELINE[w]:
                        if x[0] == "piece":
                            mm_piece(w, i, *x[1:])
                            continue
                        name = x[0]
                        n = USE[w].get(name)
                        if name == "rows_t":
                            pe.wait_ge(s_rows, 1)
                            for b in range(2):
                                bank = use(n + b)
                                for c in range(4 * b, 4 * b + 4):
                                    last = pe.transpose(bank[:, (c % 4) * P:(c % 4) * P + 68], G[0:68, 0, c * P:(c + 1) * P],
                                                        g.ident[0:68, 0:68])
                                full(last)
                            full(pe.transpose(use(n + 2)[0:NS, 0:68], G[0:68, 0, SEQ:T], g.ident[0:68, 0:68]))
                        elif name in ("vt0", "vt1"):
                            wait_evacuated(pe, w, i, TILES[w].index("v" + name[2]))
                            turned(n, VS)
                        elif name == "decay":
                            pe.wait_ge(s_sel, i + 1)
                            for b, (c0, m) in enumerate(PARTS):
                                last = pe.matmul(use(n + b)[:, 0:m], g.ones[0:H, :], TB[0:H, c0:c0 + m], start=True, stop=True)
                                if b < 2:
                                    full(last)
                            full(pe.matmul(RB(n + 2)[:, NS:NS + 2 * NC], g.ones[0:H, :], wcs[:, :], start=True, stop=True))
                        elif name == "scores":
                            pe.wait_ge(s_silu, i * 2 + 2)
                            scores(n, k, q)
                        elif name == "interq":
                            for b, (c0, m) in enumerate(PARTS):
                                full(pe.matmul(use(n + b)[:, 0:m], g.ones[32:32 + H, :], TB[32:32 + H, c0:c0 + m], start=True, stop=True))
                        elif name == "keys":
                            if isB(w):
                                pe.wait_ge(s_kt, i + 1)
                                turned(n, TB)
                            else:
                                turned(n, k)
                        elif name == "alpha":
                            pe.wait_ge(s_wah, i + 1)
                            for b, (c0, m) in enumerate(PARTS):
                                full(pe.matmul(use(n + b)[:, 0:m], walh[64:64 + RANK, :], rows[64:64 + RANK, c0:c0 + m], start=True, stop=True))
                        elif name.startswith("level"):
                            l = int(name[5:])
                            if l < NL - 1:
                                pe.wait_ge(s_qe, i * (NL - 1) + (l + 1))
                                pe.wait_ge(s_ke, i * (NL - 1) + (l + 1))
                                scores(n, KD, QD, samples=USES[name] == 3)
                            else:
                                scores(n, k, q)
                        elif name in CHAIN:
                            c = CHAIN.index(name)
                            if c == 0:
                                wait_read(pe, w, i, "keys")
                                wait_read(pe, w, i, f"level{NL - 1}" if isB(w) else "scores")
                                if isB(w):
                                    pe.wait_ge(s_qd, i + 1)
                                else:
                                    wait_read(pe, w, i, "interq")
                            full(pe.matmul(use(n)[:, 0:vw], KD[:, c * P:(c + 1) * P], v[:, c, 0:vw], start=True, stop=True))
                            bank = use(n + 1)
                            last = pe.matmul(bank[:, 0:vw], AT[:, c * P:(c + 1) * P], v[:, c, 0:vw], start=True, stop=(c == 0))
                            if c:
                                wait_read_use(pe, w, i, USE[w][CHAIN[c - 1]])
                                last = pe.matmul(bank[:, 0:vw], QD[:, c * P:(c + 1) * P], SS[:, (c - 1) % 2, 0:vw], start=False, stop=True)
                            full(last)
                        elif name == "sample_out":
                            pe.wait_ge(s_km, two(w, i) + 1)
                            pe.wait_ge(s_stl, two(w, i, 16) + 16)
                            bank = use(n)
                            apart(pe)
                            pe.matmul(bank[0:NS, 0:vw], AT[0:NS, SEQ:T], v[0:NS, NC, 0:vw], start=True, stop=False)
                            for b in range(NSEQ):
                                last = pe.matmul(bank[0:NS, 0:vw], QM[:, b, :], ST[:, b, 0:vw], start=False, stop=(b == NSEQ - 1))
                            full(last)
                        elif name in SAMPLE:
                            b = SAMPLE.index(name)
                            full(pe.matmul(use(n)[:, 0:vw], TB[0:NS, b * P:(b + 1) * P], v[0:NS, NC, 0:vw], start=True, stop=True))
                        elif name in ("turn0", "turn1"):
                            j = int(name[4])
                            pe.wait_ge(s_hn, two(w, i) + 1)
                            for b in range(2):
                                bank = use(n + b)
                                for c in range(4 * b, 4 * b + 4):
                                    last = pe.transpose(bank[:, (c % 4) * P:(c % 4 + 1) * P], v[:, c, j * P:(j + 1) * P], g.ident[:, :])
                                full(last)
                            bank = use(n + 2)
                            apart(pe)
                            full(pe.transpose(bank[:, 0:NS], HS[0:NS, j * P:(j + 1) * P], g.ident[0:NS, 0:NS]))
                        elif name.startswith("ada") and name[3] != "_":
                            m = two(w, i, 4) + int(name[3])
                            pe.wait_ge(s_adl, m * 16 + 16)
                            bank = use(n)
                            for kc in range(KC):
                                last = pe.matmul(bank[:, 0:NCOND], wad[:, kc, :], g.cT[:, kc, :], start=(kc == 0), stop=(kc == KC - 1))
                            full(last)
                run(pe, None, window)

            @block.scalar
            def _(act):
                def split_hi(w, i, l, h):
                    r, s, turns, before = half(w, i, l, h)
                    act.wait_ge(s_w[r], turns * 16 + (16 + (32 if r < 2 else 0)))
                    wait(act, s_used, before - (SPL - 1))
                    act.activation(Wh[:, s], raw[:, r], ACT.Copy).then_inc(s_hi, 1)

                def evacuate(w, i, l, c):
                    name = TILES[w][l]
                    b, _ = piece(w, i, l, c)
                    c0, n = span(c)
                    src = g.ps[b][:, 0:n]
                    wait_piece(act, w, i, l, c)
                    t = tile_index(w, i, l)
                    last_c = c == NPC - 1
                    cut = SEQ - c0 if last_c else n

                    conv = name in ("q", "k") and w in "SB"
                    if name == "small":
                        act.activation(M[0:H, 0, c0:c0 + n], src[0:H], ACT.Copy)
                        act.activation(M[0:H, 1, c0:c0 + n], src[32:32 + H], ACT.Copy)
                        last = act.activation(rows[64:64 + RANK, c0:c0 + n], src[64:64 + RANK], ACT.Copy)
                    elif conv:
                        if c == 0:
                            nth = (0 if w == "S" else i * 2 + 2) + (1 if name == "k" else 0)
                            wait(act, s_silu, nth)
                        last = act.activation(Z[:, W4 - 1 + c0:W4 - 1 + c0 + cut], src[:, 0:cut], ACT.Copy)
                        if last_c:
                            z = Z[:, ZP:ZN].rearrange("p (b t) -> p b t", t=ZS)[:, :, W4 - 1:ZS]
                            last = act.activation(z, src[:, cut:n].rearrange("p (b t) -> p b t", t=SLEN), ACT.Copy)
                    elif name in ("q", "k"):
                        last = act.activation((Q if name == "q" else K)[1][:, c0:c0 + n], src, ACT.Copy,
                                              scale=QSCALE if name == "q" else 1.0)
                    elif name[0] == "v":
                        last = act.activation(VS[:, c0:c0 + n], src, ACT.Copy)
                    elif name[0] == "o":
                        j = int(name[1])
                        if c == 0:
                            if isB(w):
                                wait_read(act, "A", i, f"turn{j}")
                                act.wait_ge(s_gate, BEGUN + i * 4 + (2 + j))
                            else:
                                act.wait_ge(s_sum, BEGUN + i * 2)
                        last = act.activation(G[:, j, c0:c0 + n], src, ACT.Tanh, scale=0.5)
                        if isB(w):
                            last = act.activation(TG[:, c0:c0 + n], src, ACT.Copy)
                    else:
                        if c == 0:
                            if isB(w):
                                act.wait_ge(s_gr, i * 2 + (int(name[1]) + 1))
                            else:
                                act.wait_ge(s_gate, BEGUN + two(w, i, 2) + int(name[1]))
                        last = act.activation(TG[:, c0:c0 + n], src, ACT.Tanh, scale=0.5)
                    last.then_inc(s_pfree[b], 1)

                split_hi("S", 0, 0, 0)
                def window(w, i):
                    hd = 1 if isB(w) else 0
                    vw = DV if isB(w) else VX
                    v = V[hd]

                    for x in TIMELINE[w]:
                        if x[0] == "piece":
                            _, l, h, c = x
                            nxt = after(w, i, l, h, 1)
                            if c == 0 and nxt:
                                split_hi(*nxt)
                            if h == 1:
                                evacuate(w, i, l, c)
                            continue
                        name = x[0]
                        n = USE[w].get(name)
                        if name == "rows":
                            act.wait_ge(s_r1, 1)
                            act.activation(TB[0:H, :], TB[0:H, :], ACT.Exp).then_inc(s_r2, 1)
                            act.wait_ge(s_r2, 1)
                            act.activation(TB[0:H, :], TB[0:H, :], ACT.Ln, bias=1.0).then_inc(s_r2, 1)
                            act.wait_ge(s_r3, 1)
                            act.activation(rows[32:32 + H, :], TB[0:H, :], ACT.Exp)
                            act.activation(G[32:32 + H, 0, :], VS[0:H, :], ACT.Exp)
                            act.activation(wcr[:, :], me[:, 3, :], ACT.Exp)
                            act.activation(G[64:64 + H, 0, :], TA[0:H, :], ACT.Exp, scale=-1.0).then_inc(s_rows, 1)
                        elif name in ("silu_q", "silu_k"):
                            m = (0 if w == "S" else i * 2 + 2) + (2 if name[-1] == "k" else 1)
                            act.wait_ge(s_cv, m)
                            act.activation(Z[:, 0:ZO], CV[:, 0:ZO], ACT.Tanh, scale=0.5).then_inc(s_th, 1)
                        elif name in ("vt0", "vt1"):
                            j = int(name[2])
                            dst = V[0 if w in "SB" else 1]
                            for b in range(2):
                                wait_use(act, w, i, n + b)
                                act.activation(dst[:, 4 * b:4 * b + 4, j * P:(j + 1) * P],
                                               RB(n + b)[:, :].rearrange("p (c d) -> p c d", d=P), ACT.Copy).then_inc(free(n + b), 1)
                            wait_use(act, w, i, n + 2)
                            act.activation(dst[0:NS, NC, j * P:(j + 1) * P], RB(n + 2)[0:NS, 0:P], ACT.Copy).then_inc(free(n + 2), 1)
                        elif name == "decay":
                            act.wait_ge(s_warg, i + 1)
                            act.activation(TA[:, 0:SEQ], TA[:, 0:SEQ], ACT.Exp)
                            act.activation(TA[0:NS, SEQ:T], TA[0:NS, SEQ:T], ACT.Exp).then_inc(s_wexp, 1)
                        elif name == "alpha":
                            for b, (c0, m) in enumerate(PARTS):
                                wait_use(act, w, i, n + b)
                                last = act.activation(QD[:, c0:c0 + m], RB(n + b)[:, 0:m], ACT.Copy)
                                last.then_inc(free(n + b), 1)
                            act.wait_ge(s_nab, i + 1)
                            act.activation(TB[:, :], TB[:, :], ACT.Exp).then_inc(s_ln, 1)
                            act.wait_ge(s_ln, i * 2 + 1)
                            act.activation(TB[:, :], TB[:, :], ACT.Ln, bias=1.0).then_inc(s_ln, 1)
                        elif name == "sums":
                            level_exp(act, w, i, 0)
                        elif name.startswith("level"):
                            l = int(name[5:])
                            if l + 1 < NL - 1:
                                level_exp(act, w, i, l + 1)
                            elif l == NL - 1:
                                act.wait_ge(s_d, i * NL + NL)
                                act.activation(TB[:, :], TB[:, :], ACT.Exp, scale=1.0 / TAU)
                                act.activation(TA[:, :], TA[:, :], ACT.Exp, scale=1.0 / TAU).then_inc(s_E, 1)
                        elif name == "keys" and isB(w):
                            for b in range(2):
                                wait_use(act, w, i, n + b)
                                act.activation(KD[:, 512 * b:512 * b + 512], RB(n + b)[:, :], ACT.Copy).then_inc(free(n + b), 1)
                            wait_use(act, w, i, n + 2)
                            act.activation(KD[0:NS, SEQ:SEQ + P], RB(n + 2)[0:NS, 0:P], ACT.Copy).then_inc(free(n + 2), 1)
                        elif name in CHAIN or name == "sample_out":
                            c = CHAIN.index(name) if name in CHAIN else NC
                            u = n + 1 if name in CHAIN else n
                            m = P if c < NC else NS
                            dst = v[:, c, 0:vw] if c < NC else HS[0:NS, 0:vw]
                            wait_use(act, w, i, u)
                            act.activation(dst, RB(u)[0:m, 0:vw], ACT.Copy).then_inc(s_hc, 1)
                            act.wait_ge(s_hc, two(w, i, NT) + (c + 1))
                            act.activation(RB(u)[0:m, 0:DV], RB(u)[0:m, 0:DV], ACT.Square,
                                           accum_out=ssq[0:m, c:c + 1]).then_inc(free(u), 1)
                        elif name == "norm":
                            act.wait_ge(s_ms, BEGUN + two(w, i) + 1)
                            act.activation(ms[:, :], ms[:, :], ACT.Sqrt).then_inc(s_sq, 1)

                def level_exp(act, w, i, l):
                    hs = LEVELS[l]
                    top = T if hs <= SLEN // 2 else SEQ
                    act.wait_ge(s_d, i * NL + (l + 1))
                    e = TB[:, 0:top].rearrange("p (n w) -> p n w", w=2 * hs)
                    act.activation(e[:, :, hs:2 * hs], e[:, :, hs:2 * hs], ACT.Exp, scale=1.0 / TAU)
                    act.activation(e[:, :, 0:hs], e[:, :, 0:hs], ACT.Exp, scale=-1.0 / TAU).then_inc(s_E, 1)
                run(act, None, window)

            @block.gpsimd
            def _(pool):
                st = Steps(pool, s_pool)
                pool.memset(raw[:, 0:2], 0.0).then_inc(s_zero, 1)
                for buf, x in ((cols[:, :, :], 0.0), (G[:, 0, :], 0.0), (me[:, :, :], 0.0), (ssq[:, :], 1.0), (ms[:, :], 1.0)):
                    pool.memset(buf, x)
                pool.memset(den[:, :], 1.0).then_inc(s_init, 1)

                def split_lo(w, i, l, h):
                    _, s, _, before = half(w, i, l, h)
                    r = half(w, i, l, h)[0]
                    pool.wait_ge(s_hi, before + 1)
                    wait(pool, s_used, before - (SPL - 1))
                    pool.tensor_tensor(Wl[:, s], raw[:, r], Wh[:, s].bitcast(F32), ALU.subtract).then_inc(s_lo, 1)
                pool.nop().then_inc(s_sum, BEGUN)
                split_lo("S", 0, 0, 0)

                def window(w, i):
                    hd = 1 if isB(w) else 0
                    for x in TIMELINE[w]:
                        if x[0] == "piece":
                            _, l, h, c = x
                            nxt = after(w, i, l, h, 1)
                            if c == 0 and nxt:
                                split_lo(*nxt)
                            continue
                        name = x[0]
                        n = USE[w].get(name)
                        if name.startswith("level") and int(name[5:]) < NL - 1:
                            l = int(name[5:])
                            if l == 0:
                                wait_use(pool, w, i, USE[w]["alpha"])
                                apart(pool)
                                pool.memset(AT[:, :], 0.0).then_inc(s_at0, 1)
                            else:
                                wait_use(pool, w, i, n - 1)
                            pool.wait_ge(s_E, i * NL + (l + 1))
                            top = T if LEVELS[l] <= SLEN // 2 else SEQ
                            pool.tensor_tensor(KD[:, 0:top], K[1][:, 0:top], TB[:, 0:top], ALU.mult).then_inc(s_ke, 1)
                        elif name == "masked":
                            wait_read(pool, w, i, "keys")
                            if isB(w):
                                pool.wait_ge(s_qd, i + 1)
                            else:
                                wait_read(pool, w, i, "interq")
                            pool.tensor_tensor(QM[:, :, :], mid(QD[:, SEQ:T], NSEQ), g.seqrow[:, :, :], ALU.mult)
                            pool.tensor_tensor(TB[0:NS, 0:SEQ].rearrange("p (b d) -> p b d", b=NSEQ), mid(KD[0:NS, SEQ:SEQ + P], NSEQ),
                                               bc(g.seqcol[:, :].unsqueeze(2), P), ALU.mult).then_inc(s_km, 1)
                        elif name in ("turn0", "turn1") and isB(w):
                            j = int(name[4])
                            wait_read(pool, w, i, name)
                            pool.tensor_tensor(M[:, j, :], M[:, j, :], G[:, j, :], ALU.add).then_inc(s_sum, 1)
                run(pool, None, window)

            @block.vector
            def _(dve):
                per = g.dve_per
                st = Steps(dve, s_dve, per=per)
                dve.nop().then_inc(s_ms, BEGUN)
                dve.nop().then_inc(s_gate, BEGUN)
                link, did = st.link, st.did

                def conv(kt):
                    z = Z[:, ZP:ZN].rearrange("p (b t) -> p b t", t=ZS)
                    dve.memset(Z[:, 0:W4 - 1], 0.0)
                    dve.tensor_copy(z[:, :, 0:W4 - 1], g.sconvT[:, bass.ds(kt, 1), :].rearrange("p k (b j) -> p (k b) j", j=W4 - 1))
                    dve.tensor_copy(g.pk[:, bass.ds(kt, 1), 0:W4 - 1].rearrange("p k j -> p (k j)"), Z[:, SEQ:ZP])
                    link(dve.tensor_copy(g.pk[:, bass.ds(kt, 1), W4 - 1:KEEP].rearrange("p k (b j) -> p (k b) j", j=W4 - 1),
                                         z[:, :, SLEN:ZS]))
                    col = lambda v: g.vec[:, bass.ds(v + kt, 1)]
                    link(dve.tensor_scalar(CV[:, 0:ZO], Z[:, 0:ZO], col(V_CW), col(V_CB), ALU.mult, ALU.add))
                    for j in range(1, W4):
                        ins = dve.scalar_tensor_tensor(CV[:, 0:ZO], Z[:, j:j + ZO], col(V_CW + j * KC), CV[:, 0:ZO], ALU.mult, ALU.add)
                        if j < W4 - 1:
                            link(ins)
                    ins.then_inc(s_cv, 1)

                def silu(m, dst, f):
                    dve.wait_ge(s_th, m)
                    link(dve.tensor_scalar(Z[:, 0:ZO], Z[:, 0:ZO], 1.0, 0.5 * f, ALU.add, ALU.mult))
                    dve.tensor_tensor(dst[:, 0:SEQ], Z[:, 0:SEQ], CV[:, 0:SEQ], ALU.mult)
                    tail = lambda v: v[:, ZP:ZN].rearrange("p (b t) -> p b t", t=ZS)[:, :, 0:SLEN]
                    dve.tensor_tensor(seqs(dst), tail(Z), tail(CV), ALU.mult).then_inc(s_silu, 1)

                def window(w, i):
                    hd = 1 if isB(w) else 0
                    vw = DV if isB(w) else VX
                    q, k, v = Q[hd], K[hd], V[hd]
                    if w == "A":
                        st.turn(i)
                    for x in TIMELINE[w]:
                        if x[0] == "piece":
                            continue
                        name = x[0]
                        n = USE[w].get(name)
                        if name == "rows":
                            rows_stage()
                        elif name == "rows_t":
                            for b in range(2):
                                wait_use(dve, w, i, n + b)
                                src = RB(n + b)[:, :].rearrange("p (c r) -> p c r", r=P)
                                for r in range(3):
                                    ins = dve.tensor_copy(cols[:, 4 * b:4 * b + 4, r * H:(r + 1) * H], src[:, :, 32 * r:32 * r + H])
                                ins.then_inc(free(n + b), 1)
                            wait_use(dve, w, i, n + 2)
                            for r in range(3):
                                ins = dve.tensor_copy(cols[0:NS, NC, r * H:(r + 1) * H], RB(n + 2)[0:NS, 32 * r:32 * r + H])
                            ins.then_inc(free(n + 2), 1)
                            dve.wait_ge(free(n + 2), 1)
                        elif name in ("conv_q", "conv_k"):
                            wait_evacuated(dve, w, i, TILES[w].index(name[-1]))
                            conv((4 if name[-1] == "k" else 0) + (0 if w == "S" else i + 1))
                        elif name in ("silu_q", "silu_k"):
                            isk = name[-1] == "k"
                            m = (0 if w == "S" else i * 2 + 2) + (2 if isk else 1)
                            silu(m, (K if isk else Q)[0], 1.0 if isk else QSCALE)
                        elif name == "select":
                            one = g.ident[0:H, bass.ds(i, 1)]
                            dve.tensor_scalar(TB[0:H, :], rows[0:H, :], one, None, ALU.mult)
                            dve.tensor_scalar(TB[32:32 + H, :], rows[32:32 + H, :], g.ident[32:32 + H, bass.ds(i + 32, 1)], None, ALU.mult)
                            dve.tensor_copy(walh[64:64 + RANK, :], wal[64:64 + RANK, bass.ds(i * DK, DK)]).then_inc(s_wah, 1)
                            dve.tensor_scalar(wcs[:, :], wcr[:, :], one, None, ALU.mult).then_inc(s_sel, 1)
                            link(dve.tensor_copy(hcol[:, :, :], cols[:, :, :].rearrange("p c (q h) -> p c q h", h=H)[:, :, :, bass.ds(i, 1)]
                                                 .rearrange("p c q h -> p c (q h)")))
                        elif name == "decay":
                            for b in range(2):
                                wait_use(dve, w, i, n + b)
                                for c in range(4 * b, 4 * b + 4):
                                    ins = dve.scalar_tensor_tensor(TA[:, c * P:(c + 1) * P], RB(n + b)[:, (c % 4) * P:(c % 4 + 1) * P],
                                                                   hcol[:, c, 0:1], g.cmask[:, :], ALU.add, ALU.min)
                                ins.then_inc(free(n + b), 1)
                            wait_use(dve, w, i, n + 2)
                            dve.scalar_tensor_tensor(TA[0:NS, SEQ:T], RB(n + 2)[0:NS, 0:NS], hcol[0:NS, NC, 0:1], g.cmask_s[:, :],
                                                     ALU.add, ALU.min).then_inc(s_warg, 1)
                            dve.tensor_copy(sdec[:, :], RB(n + 2)[:, NS:NS + 2 * NC]).then_inc(free(n + 2), 1)
                        elif name == "scores":
                            dve.wait_ge(s_wexp, i + 1)
                            for b in range(2):
                                wait_use(dve, w, i, n + b)
                                dve.tensor_tensor(AT[:, 512 * b:512 * b + 512], RB(n + b)[:, :], TA[:, 512 * b:512 * b + 512],
                                                  ALU.mult).then_inc(free(n + b), 1)
                            wait_use(dve, w, i, n + 2)
                            dve.tensor_tensor(AT[0:NS, SEQ:T], RB(n + 2)[0:NS, 0:NS], TA[0:NS, SEQ:T], ALU.mult).then_inc(free(n + 2), 1)
                        elif name == "interq":
                            did(dve.memset(V[0][:, :, DV:VX], 1.0))
                            did(dve.tensor_copy(ST[:, :, DV:VX], g.n0T[:, :].rearrange("p (b h) -> p b h", h=H)[:, :, bass.ds(i, 1)]))
                            for b, (c0, m) in enumerate(PARTS):
                                wait_use(dve, w, i, n + b)
                                dve.tensor_tensor(QD[:, c0:c0 + m], RB(n + b)[:, 0:m], q[:, c0:c0 + m], ALU.mult).then_inc(free(n + b), 1)
                        elif name == "keys" and not isB(w):
                            for b in range(2):
                                wait_use(dve, w, i, n + b)
                                dve.tensor_tensor(KD[:, 512 * b:512 * b + 512].rearrange("p (c d) -> p c d", d=P),
                                                  RB(n + b)[:, :].rearrange("p (c d) -> p c d", d=P),
                                                  bc(hcol[:, 4 * b:4 * b + 4, 1:2], P), ALU.mult).then_inc(free(n + b), 1)
                            wait_use(dve, w, i, n + 2)
                            dve.tensor_scalar(KD[0:NS, SEQ:SEQ + P], RB(n + 2)[0:NS, 0:P], hcol[0:NS, NC, 1:2], None,
                                              ALU.mult).then_inc(free(n + 2), 1)
                        elif name == "alpha":
                            wait_read(dve, w, i, "alpha")
                            link(dve.tensor_scalar(QD[:, :], QD[:, :], g.vec[:, bass.ds(V_AL + i, 1)], None, ALU.add))
                            dve.scalar_tensor_tensor(TB[:, :], QD[:, :], -1.0, QD[:, :], ALU.mult, ALU.min).then_inc(s_nab, 1)
                        elif name == "sums":
                            dve.wait_ge(s_ln, i * 2 + 2)
                            link(dve.scalar_tensor_tensor(TB[:, :], QD[:, :], 0.0, TB[:, :], ALU.min, ALU.subtract))
                            link(dve.tensor_tensor_scan(TA[:, :], g.reset[:, :], TB[:, :], 0.0, ALU.mult, ALU.add))
                            level_diff(0, i)
                        elif name.startswith("level"):
                            l = int(name[5:])
                            if l < NL - 1:
                                top = T if LEVELS[l] <= SLEN // 2 else SEQ
                                dve.wait_ge(s_E, i * NL + (l + 1))
                                dve.tensor_tensor(QD[:, 0:top], q[:, 0:top], TB[:, 0:top], ALU.mult).then_inc(s_qe, 1)
                                dve.wait_ge(s_qe, i * (NL - 1) + (l + 1))
                                dve.wait_ge(s_ke, i * (NL - 1) + (l + 1))
                                if l < NL - 2:
                                    level_diff(l + 1, i)
                                else:
                                    e, b = chunks(TB), chunks(TA)
                                    did(dve.tensor_tensor(e, bc(b[:, :, P - 1:P], P), b, ALU.subtract))
                                    e, b = seqs(TB), seqs(TA)
                                    dve.tensor_tensor(e, bc(b[:, :, SLEN - 1:SLEN], SLEN), b, ALU.subtract).then_inc(s_d, 1)
                            if l == 0:
                                dve.wait_ge(s_at0, i + 1)
                            c4 = lambda v: v.rearrange("p (c t) -> p c t", t=P)
                            for b in range(2):
                                wait_use(dve, w, i, n + b)
                                apart(dve)
                                dve.copy_predicated(c4(AT[:, 512 * b:512 * b + 512]), mid(g.lmask[:, l, :], 4),
                                                    c4(RB(n + b)[:, :])).then_inc(free(n + b), 1)
                            if USES[name] == 3:
                                wait_use(dve, w, i, n + 2)
                                apart(dve)
                                dve.copy_predicated(AT[0:NS, SEQ:T], g.lmask[0:NS, l, 0:NS], RB(n + 2)[0:NS, 0:NS]).then_inc(free(n + 2), 1)
                            wait_read(dve, w, i, name)
                            if l == NL - 1:
                                dve.wait_ge(s_E, i * NL + NL)
                                dve.tensor_tensor(TB[:, :], k[:, :], TB[:, :], ALU.mult).then_inc(s_kt, 1)
                                did(dve.tensor_copy(sdec[:, 0:NC], chunks(TA)[:, :, P - 1:P].rearrange("p c t -> p (c t)")))
                                did(dve.tensor_copy(sdec[:, NC:2 * NC], seqs(TA)[:, :, SLEN - 1:SLEN].rearrange("p c t -> p (c t)")))
                                dve.tensor_tensor(QD[:, :], q[:, :], TA[:, :], ALU.mult).then_inc(s_qd, 1)
                        elif name in CHAIN:
                            c = CHAIN.index(name)
                            wait_use(dve, w, i, n)
                            if c == 0:
                                ins = dve.tensor_copy(SS[:, 0, 0:vw], RB(n)[:, 0:vw])
                            else:
                                wait_read_use(dve, w, i, USE[w][CHAIN[c - 1]])
                                if c == 1:
                                    dve.wait_ge(s_sts, BEGUN + two(w, i, 32))
                                ins = dve.scalar_tensor_tensor(SS[:, c % 2, 0:vw], SS[:, (c - 1) % 2, 0:vw], sdec[:, c:c + 1],
                                                               RB(n)[:, 0:vw], ALU.mult, ALU.add)
                            ins.then_inc(free(n), 1)
                            if c == NC - 1 and not isB(w):
                                wait_read_use(dve, w, i, n)
                                did(dve.tensor_copy(g.nout[:, bass.ds(i, 1)], SS[:, 1, DV:VX]))
                        elif name in SAMPLE:
                            b = SAMPLE.index(name)
                            wait_use(dve, w, i, n)
                            if b == 0:
                                dve.wait_ge(s_stl, two(w, i, 16) + 16)
                            dve.scalar_tensor_tensor(ST[:, b, 0:vw], ST[:, b, 0:vw], sdec[:, NC + b:NC + b + 1], RB(n)[:, 0:vw],
                                                     ALU.mult, ALU.add).then_inc(free(n), 1)
                            if b == NSEQ - 1 and not isB(w):
                                wait_read_use(dve, w, i, n)
                                did(dve.tensor_copy(g.nout[:, H:].rearrange("p (b h) -> p b h", h=H)[:, :, bass.ds(i, 1)], ST[:, :, DV:VX]))
                        elif name == "norm":
                            wait_read(dve, w, i, "sample_out")
                            if not isB(w):
                                d = v[:, 0:NC, DV:VX].rearrange("p c o -> p (c o)")
                                did(dve.scalar_tensor_tensor(den[:, 0:NC], d, -1.0, d, ALU.mult, ALU.max))
                                d = HS[0:NS, DV:VX]
                                link(dve.scalar_tensor_tensor(den[0:NS, NC:NT], d, -1.0, d, ALU.mult, ALU.max))
                                link(dve.tensor_tensor(den[:, :], den[:, :], hcol[:, :, 2:3].rearrange("p c o -> p (c o)"), ALU.max))
                                link(dve.reciprocal(den[:, :], den[:, :]))
                                link(dve.tensor_tensor(ms[:, :], ssq[:, :], den[:, :], ALU.mult))
                                link(dve.tensor_tensor(ms[:, :], ms[:, :], den[:, :], ALU.mult))
                                dve.tensor_scalar(ms[:, :], ms[:, :], 1.0 / DV, EPS, ALU.mult, ALU.add).then_inc(s_ms, 1)
                            else:
                                dve.tensor_scalar(ms[:, :], ssq[:, :], 1.0 / DV, EPS, ALU.mult, ALU.add).then_inc(s_ms, 1)
                            dve.wait_ge(s_sq, two(w, i) + 1)
                            link(dve.reciprocal(scl[:, :], ms[:, :]))
                            if not isB(w):
                                link(dve.tensor_tensor(scl[:, :], scl[:, :], den[:, :], ALU.mult))
                            dve.tensor_tensor(v[:, 0:NC, 0:DV], v[:, 0:NC, 0:DV], bc(scl[:, 0:NC].unsqueeze(2), DV), ALU.mult)
                            dve.tensor_scalar(HS[0:NS, 0:DV], HS[0:NS, 0:DV], scl[0:NS, NC:NT], None, ALU.mult).then_inc(s_hn, 1)
                        elif name in ("gate_r0", "gate_r1"):
                            j = int(name[-1])
                            wait_evacuated(dve, w, i, TILES[w].index(f"o{j}"))
                            dve.scalar_tensor_tensor(G[:, j, :], G[:, j, :], 1.0, TG[:, :], ALU.add, ALU.mult).then_inc(s_gr, 1)
                        elif name in ("gate0", "gate1"):
                            j = int(name[-1])
                            wait_evacuated(dve, w, i, TILES[w].index(f"g{j}"))
                            gain = g.vec[:, bass.ds(i * 2 + ((V_HB if isB(w) else V_HA) + j), 1)]
                            link(dve.tensor_scalar(TG[:, :], TG[:, :], 1.0, gain, ALU.add, ALU.mult))
                            if isB(w):
                                dve.wait_ge(s_gr, i * 2 + (j + 1))
                                ins = dve.tensor_tensor(G[:, j, :], G[:, j, :], TG[:, :], ALU.mult)
                            else:
                                ins = dve.scalar_tensor_tensor(G[:, j, :], G[:, j, :], 1.0, TG[:, :], ALU.add, ALU.mult)
                            ins.then_inc(s_gate, 1)
                        elif name in ("turn0", "turn1"):
                            j = int(name[-1])
                            dve.wait_ge(s_gate, BEGUN + two(w, i, 2) + (j + 1))
                            if not isB(w) and j == 0:
                                dve.wait_ge(s_mst, BEGUN + i * 16)
                            for b, (c0, m) in enumerate(PARTS):
                                wait_use(dve, w, i, n + b)
                                dst = G if isB(w) else M
                                dve.tensor_tensor(dst[:, j, c0:c0 + m], RB(n + b)[:, 0:m], G[:, j, c0:c0 + m], ALU.mult).then_inc(free(n + b), 1)
                        elif name.startswith("ada") and name[3] != "_":
                            m = two(w, i, 4) + (int(name[3]) + 2 * KC)
                            wait_use(dve, w, i, n)
                            dve.tensor_scalar(g.ada[:, bass.ds(m, 1), :].rearrange("p o c -> p (o c)"), RB(n)[:, 0:NCOND],
                                              g.vec[:, bass.ds(m, 1)], None, ALU.add).then_inc(free(n), 1)
                    if per and w == "B" and st.n != per:
                        raise ValueError(f"set dve_per to {st.n}")

                def level_diff(l, i):
                    hs = LEVELS[l]
                    top = T if hs <= SLEN // 2 else SEQ
                    b = TA[:, 0:top].rearrange("p (n w) -> p n w", w=2 * hs)
                    dve.tensor_tensor(TB[:, 0:top].rearrange("p (n w) -> p n w", w=2 * hs), b, bc(b[:, :, hs - 1:hs], 2 * hs),
                                      ALU.subtract).then_inc(s_d, 1)

                def rows_stage():
                    I, X, LF, B_, MM = M[0:H, 0, :], M[0:H, 1, :], AT[0:H, :], QD[0:H, :], TA[0:H, :]
                    wait_evacuated(dve, "S", 0, 0)
                    dve.wait_ge(s_small, 64)
                    dve.wait_ge(s_init, 1)
                    did(dve.tensor_scalar(I, I, bif[:, 0:1], None, ALU.add))
                    link(dve.tensor_scalar(X, X, bif[:, 1:2], None, ALU.add))
                    dve.scalar_tensor_tensor(TB[0:H, :], X, -1.0, X, ALU.mult, ALU.min).then_inc(s_r1, 1)
                    dve.wait_ge(s_r2, 2)
                    link(dve.scalar_tensor_tensor(LF, X, 0.0, TB[0:H, :], ALU.min, ALU.subtract))
                    did(dve.tensor_tensor_scan(B_, g.reset[0:H, :], LF, 0.0, ALU.mult, ALU.add))
                    did(dve.tensor_tensor_scan(MM[:, 0:SEQ], LF[:, 0:SEQ], I[:, 0:SEQ], 0.0, ALU.add, ALU.max))
                    for b in range(NSEQ):
                        r = slice(SEQ + b * SLEN, SEQ + (b + 1) * SLEN)
                        did(dve.tensor_tensor_scan(MM[:, r], LF[:, r], I[:, r], m0[:, b:b + 1], ALU.add, ALU.max))
                    dve.wait_ge(s_dve, st.value())
                    ends = lambda v: (chunks(v)[:, :, P - 1:P].rearrange("p c t -> p (c t)"), seqs(v)[:, :, SLEN - 1:SLEN].rearrange("p c t -> p (c t)"))
                    for r, v in ((1, MM), (2, B_)):
                        for j, e in enumerate(ends(v)):
                            did(dve.tensor_copy(me[:, r, j * NC:(j + 1) * NC], e))
                    did(dve.tensor_copy(me[:, 0, NC:2 * NC], m0[:, :]))
                    dve.wait_ge(s_dve, st.value())
                    did(dve.tensor_copy(me[:, 0, 1:NC], me[:, 1, 0:NC - 1]))
                    did(dve.tensor_tensor(me[:, 3, :], me[:, 2, :], me[:, 1, :], ALU.subtract))
                    did(dve.tensor_tensor(rows[0:H, :], B_, MM, ALU.subtract))
                    did(dve.tensor_tensor(G[0:H, 0, :], I, B_, ALU.subtract))
                    dve.wait_ge(s_dve, st.value())
                    for f, col in ((chunks, slice(0, NC)), (seqs, slice(NC, 2 * NC))):
                        m = P if f is chunks else SLEN
                        did(dve.tensor_tensor(f(TB[0:H, :]), f(rows[0:H, :]), bc(me[:, 0, col].unsqueeze(2), m), ALU.add))
                        did(dve.tensor_tensor(f(VS[0:H, :]), f(G[0:H, 0, :]), bc(me[:, 3, col].unsqueeze(2), m), ALU.add))
                    dve.wait_ge(s_dve, st.value())
                    dve.tensor_tensor(me[:, 3, :], me[:, 3, :], me[:, 0, :], ALU.add).then_inc(s_r3, 1)
                run(dve, None, window)


NBLK = FT // 2


def ffn_phase(nc, g, a, loops=True):
    with ExitStack() as ctx:
        sb = lambda n, s, d=F32: ctx.enter_context(nc.sbuf_tensor(n, s, d))
        sem = lambda n: ctx.enter_context(nc.semaphore(n))
        RING = 4
        raw = sb("f_raw", [P, RING, 4, P])
        Wh = sb("f_hi", [P, RING, 4, P], F32R)
        Wl = sb("f_lo", [P, RING, 4, P], F32R)
        X = sb("x_t", [P, KC, T])
        XR = sb("x_tile", [P, 2, D])
        MX = sb("mix_tile", [P, 2, T])
        SQ = sb("squares", [P, T])
        SQT = sb("square", [P, T])
        TH = sb("ffn_tanh", [P, T])
        SG = sb("ffn_silu", [P, T])
        AC = sb("ffn_act", [P, T])
        Ah = sb("act_hi", [P, 2, 2, T], F32R)
        Al = sb("act_lo", [P, 2, 2, T], F32R)
        RD = sb("rstd_rows", [P, P])
        small = sb("norm_small", [P, 4, NT])
        am = sb("norm2_mult", [P, KC, NCOND])
        stm = sb("sample_temp", [P, NS])
        co = AC[0:KEEP, 0:D]
        stn = sb("n_rows_out", [H * NCOND, P])
        fss = sb("final_small", [P, NT, 4])
        OT, GF = MX, SQT

        s_w = [sem(f"f_w_loaded{n}") for n in range(RING)]
        s_hi, s_lo, s_used = sem("f_hi_made"), sem("f_lo_made"), sem("f_used")
        s_piece = sem("f_pieces_full")
        s_pf = [sem(f"f_bank_free{n}") for n in range(4)]
        s_ml, s_xl = [sem("mix_loaded0"), sem("mix_loaded1")], [sem("x_row_loaded0"), sem("x_row_loaded1")]
        s_mh, s_mlo = sem("mix_hi"), sem("mix_lo")
        s_xt, s_xe = sem("x_turned"), sem("x_taken")
        s_sq, s_sum, s_ms, s_rt, s_rd, s_rb = sem("squares_summed"), sem("norm2_sums"), sem("norm2_ms"), sem("norm2_sqrt"), sem("norm2_rows"), sem("norm2_bcast")
        s_h, s_hh, s_hl = sem("h2_ready"), sem("h2_hi"), sem("h2_lo")
        s_th, s_ah, s_al = sem("tanh_ready"), sem("act_hi_made"), sem("act_lo_made")
        s_co, s_cc, s_out = sem("states_turned"), sem("states_copied"), sem("stored")
        s_gf = sem("final_gain")
        s_y = [sem("y_stored0"), sem("y_stored1")]
        s_stm = sem("samples_gated")
        s_ft, s_fs, s_fm, s_fr, s_fo = sem("final_turned"), sem("final_ssq"), sem("final_ms"), sem("final_sqrt"), sem("final_rows")
        s_dve, s_pool = sem("f_dve_chain"), sem("f_pool_chain")

        w_out = a["w_out"][0].rearrange("(k p) n -> p k n", p=P)
        w_gate = a["w_ffn_gate"][0].rearrange("(k p) n -> p k n", p=P)
        w_up = a["w_ffn_up"][0].rearrange("(k p) n -> p k n", p=P)
        w_down = a["w_ffn_down"][0]
        LOOP = (NBLK - 1) // 2

        HALVES = {"out": 2, "proj": 8, "down": 4}
        PIECES = {"out": 3, "proj": 12, "down": 24}
        SIGNAL = {"out": 2, "proj": 8, "down": 22}

        class Place:
            def __init__(self, j, steps_before, in_turn):
                tot = lambda d, names: sum(d[x] for x in names)
                pre = ["out"] * KC + ["proj"]
                turn = ["proj", "down"] * 2
                n = lambda d: (tot(d, turn), tot(d, (pre if in_turn is not None else steps_before)) + tot(d, turn[:in_turn or 0]))
                self.j = j
                self.halves, self.pieces, self.fulls = n(HALVES), n(PIECES), n(SIGNAL)

            def half(self, k):
                per, base = self.halves
                s, turns = static(self.j, per, base + k, RING)
                return s, turns, self.j * per + (base + k)

            def piece(self, k):
                per, base = self.pieces
                return static(self.j, per, base + k, 4)

            def full(self, k):
                per, base = self.fulls
                return self.j * per + (base + k)

        def out_place(n):
            return Place(0, ["out"] * n, None)

        def run(engine, step):
            for n in range(KC):
                step("out", n, 0, out_place(n))
            step("norm2", 0, 0, None)
            step("proj", 0, 0, Place(0, ["out"] * KC, None))

            def turn(j):
                step("proj", j * 2 + 1, 1, Place(j, None, 0))
                step("down", j * 2, 0, Place(j, None, 1))
                step("proj", j * 2 + 2, 0, Place(j, None, 2))
                step("down", j * 2 + 1, 1, Place(j, None, 3))
            if loops:
                with engine.Fori(0, LOOP) as j:
                    turn(j)
            else:
                for j in range(LOOP):
                    turn(j)
            step("down", NBLK - 1, 0, Place(LOOP, None, 0))

        def source(kind, b, k):
            if kind == "out":
                return w_out[:, 4 * k:4 * k + 4, bass.ds(b * P, P)]
            if kind == "proj":
                t, h = k // 2, k % 2
                src = w_gate if t % 2 == 0 else w_up
                return src[:, 4 * h:4 * h + 4, bass.ds(b * (2 * P) + (t // 2) * P, P)]
            n0, f = k // 2, k % 2
            rows = w_down[bass.ds(b * (2 * P) + f * P, P), 512 * n0:512 * n0 + 512]
            return rows.rearrange("p (n c) -> p n c", c=P)

        def span(c):
            return c * PC, PC

        def wait_full(e, kind, pl, k):
            if kind == "down":
                nh, r = k // 12, k % 12
                if r == 11:
                    e.wait_ge(s_used, pl.half(2 * nh + 1)[2] + 1)
                else:
                    e.wait_ge(s_piece, pl.full(11 * nh + r) + 1)
            else:
                t, c = k // 3, k % 3
                if c == 2:
                    e.wait_ge(s_used, pl.half(2 * t + 1)[2] + 1)
                else:
                    e.wait_ge(s_piece, pl.full(2 * t + c) + 1)

        MISC = g.ps[4:8]
        PARTS = [(0, 512), (512, 512), (SEQ, NS)]
        seqv = lambda v: v.rearrange("p (b t) -> p b t", t=SLEN)

        with nc.Block() as block:

            @block.sync
            def _(sp):
                sp.dma_start(raw[:, 0], source("out", 0, 0)).then_inc(s_w[0], 16)

                def step(kind, b, par, pl):
                    if kind == "norm2":
                        return
                    if kind == "out" and b == 1:
                        sp.wait_ge(s_cc, 2)
                        sp.dma_start(a["conv_p"].rearrange("o b j c -> (o b j) c"), co[0:W4 - 1, :]).then_inc(s_out, 16)
                        sp.dma_start(a["conv_s"].rearrange("o b j c -> (o b j) c"), co[W4 - 1:KEEP, :]).then_inc(s_out, 16)
                        sp.dma_start(a["n_p"].rearrange("o b h d -> (o b h) d"), stn[0:H, :]).then_inc(s_out, 16)
                        sp.dma_start(a["n_s"].rearrange("o b h d -> (o b h) d"), stn[H:H * NCOND, :]).then_inc(s_out, 16)
                    for k in range(HALVES[kind]):
                        if kind == "out" and b == 0 and k == 0:
                            for m in range(2):
                                sp.dma_start(MX[:, m], g.mix_d[:, m, :]).then_inc(s_ml[m], 16)
                                sp.dma_start(XR[:, m, :], a["x_prompt"][0, m * P:(m + 1) * P, :]).then_inc(s_xl[m], 16)
                            continue
                        s, turns, before = pl.half(k)
                        wait(sp, s_lo, before - (RING - 1))
                        sp.dma_start(raw[:, s], source(kind, b, k)).then_inc(s_w[s], 16)
                        if kind == "out" and b == 0 and k == 1:
                            for m in range(2, KC):
                                sp.wait_ge(s_mlo, m - 1)
                                sp.dma_start(MX[:, m % 2], g.mix_d[:, m, :]).then_inc(s_ml[m % 2], 16)
                            for t in range(2, NT):
                                sp.wait_ge(s_xt, 2 * (t - 1))
                                n = P if t < NC else NS
                                src = a["x_prompt"][0, t * P:(t + 1) * P, :] if t < NC else a["x_sample"].rearrange("b t d -> (b t) d")
                                sp.dma_start(XR[0:n, t % 2, :], src).then_inc(s_xl[t % 2], 16)
                run(sp, step)
                gf = a["g_final"].unsqueeze(0).to_broadcast([P, D])
                sp.wait_ge(s_hl, KC)
                sp.dma_start(GF[:, 0:D], gf).then_inc(s_gf, 16)
                for t in range(NT):
                    sp.wait_ge(s_fo, t + 1)
                    if t < NC:
                        sp.dma_start(a["y_prompt"][0, t * P:(t + 1) * P, :], OT[:, t % 2, 0:D]).then_inc(s_y[t % 2], 16)
                    else:
                        sp.dma_start(a["y_sample"].rearrange("b t d -> (b t) d"), OT[0:NS, t % 2, 0:D]).then_inc(s_y[t % 2], 16)
                sp.wait_ge(s_out, 16 * 4)
                for m in range(2):
                    sp.wait_ge(s_y[m], 16 * ((NT - m + 1) // 2))

            @block.tensor
            def _(pe):
                def tile3(pl, k, t, rhs_hi, rhs_lo):
                    for h in range(2):
                        s, _, before = pl.half(2 * t + h)
                        pe.wait_ge(s_lo, before + 1)
                        for c in range(NPC):
                            bnk, turns = pl.piece(3 * t + c)
                            if h == 0:
                                wait(pe, s_pf[bnk], turns)
                            c0, n = span(c)
                            for kk in range(4):
                                for m, (x, y) in enumerate(((Wh, rhs_hi), (Wh, rhs_lo), (Wl, rhs_hi))):
                                    last = pe.matmul(g.ps[bnk][:, 0:n], x[:, s, kk, :], y[:, 4 * h + kk, c0:c0 + n],
                                                     start=(h == 0 and kk == 0 and m == 0), stop=(h == 1 and kk == 3 and m == 2))
                            if c == NPC - 1:
                                last.then_inc(s_used, 1)
                            elif h == 1:
                                last.then_inc(s_piece, 1)

                def step(kind, b, par, pl):
                    if kind == "out":
                        if b == 0:
                            pe.wait_ge(s_mlo, KC)
                        tile3(pl, 0, 0, g.Hh, g.Hl)
                    elif kind == "proj":
                        if isinstance(b, int) and b == 0:
                            pe.wait_ge(s_hl, KC)
                        for t in range(4):
                            tile3(pl, 0, t, g.Hh, g.Hl)
                    elif kind == "down":
                        pe.wait_ge(s_al, b * 6 + 6)
                        for nh in range(2):
                            sl = []
                            for f in range(2):
                                s, _, before = pl.half(2 * nh + f)
                                pe.wait_ge(s_lo, before + 1)
                                sl.append(s)
                            for r in range(12):
                                n, c = r // 3, r % 3
                                bnk, turns = pl.piece(12 * nh + r)
                                wait(pe, s_pf[bnk], turns)
                                c0, w = span(c)
                                for f in range(2):
                                    for m, (x, y) in enumerate(((Wh, Ah), (Wh, Al), (Wl, Ah))):
                                        last = pe.matmul(g.ps[bnk][:, 0:w], x[:, sl[f], n, :], y[:, par, f, c0:c0 + w],
                                                         start=(f == 0 and m == 0), stop=(f == 1 and m == 2))
                                if r == 11:
                                    last.then_inc(s_used, 2)
                                else:
                                    last.then_inc(s_piece, 1)
                    elif kind == "norm2":
                        pe.wait_ge(s_sq, KC)
                        pe.wait_ge(s_xe, 2 * NT)
                        for t in range(NT):
                            n = P if t < NC else NS
                            last = pe.matmul(MISC[3][0:n, 64 + 2 * t:65 + 2 * t], SQ[:, t * P:t * P + n], g.ones[:, 0:1], start=True, stop=True)
                        last.then_inc(s_sum, 1)
                        for t in range(NT):
                            pe.wait_ge(s_rd, t + 1)
                            n = P if t < NC else NS
                            dst = MISC[t // 4][:, (t % 4) * P:(t % 4) * P + n]
                            pe.matmul(dst, RD[0:n, :], g.ident[0:n, 0:n], start=True, stop=True).then_inc(s_rb, 1)

                for half_ in range(2):
                    for k in range(4):
                        kk = 4 * half_ + k
                        last = pe.transpose(MISC[half_][0:KEEP, k * P:(k + 1) * P], g.pk[:, kk, :], g.ident[:, :])
                pe.transpose(MISC[2][0:H * NCOND, 0:P], g.nout[:, :], g.ident[:, :]).then_inc(s_co, 1)
                pe.wait_ge(s_cc, 2)
                for t in range(NT):
                    pe.wait_ge(s_xl[t % 2], 16 * (t // 2 + 1))
                    n = P if t < NC else NS
                    for b in range(2):
                        u = 2 * t + b
                        if u >= 4:
                            pe.wait_ge(s_xe, u - 3)
                        for k in range(4):
                            last = pe.transpose(MISC[u % 4][:, k * P:k * P + n], XR[0:n, t % 2, (4 * b + k) * P:(4 * b + k + 1) * P],
                                                g.ident[0:n, 0:n])
                        last.then_inc(s_xt, 1)
                run(pe, step)
                lastp = Place(LOOP, None, 0)
                bnk, turns = lastp.piece(23)
                pe.wait_ge(s_pf[bnk], turns + 1)
                for t in range(NT):
                    n = P if t < NC else NS
                    for b in range(2):
                        u = 2 * t + b
                        if u >= 4:
                            pe.wait_ge(s_fo, (u - 4) // 2 + 1)
                        for k in range(4):
                            last = pe.transpose(MISC[u % 4][0:n, k * P:(k + 1) * P], X[:, 4 * b + k, t * P:t * P + n], g.ident[:, :])
                        last.then_inc(s_ft, 1)

            @block.scalar
            def _(act):
                def hi(kind, pl, k):
                    s, turns, before = pl.half(k)
                    act.wait_ge(s_w[s], turns * 16 + 16)
                    wait(act, s_used, before - (RING - 1))
                    act.activation(Wh[:, s], raw[:, s], ACT.Copy).then_inc(s_hi, 1)

                def step(kind, b, par, pl):
                    if kind == "out":
                        for k in range(2):
                            hi(kind, pl, k)
                    elif kind == "norm2":
                        act.wait_ge(s_ms, 1)
                        act.activation(small[:, 1, :], small[:, 0, :], ACT.Sqrt).then_inc(s_rt, 1)
                        p0 = Place(0, ["out"] * KC, None)
                        for k in range(2):
                            hi("proj", p0, k)
                        for k in range(KC):
                            act.wait_ge(s_h, k + 1)
                            act.activation(g.Hh[:, k, :], (SQT, TH, SG)[k % 3][:, :], ACT.Copy).then_inc(s_hh, 1)
                    elif kind == "proj":
                        first = isinstance(b, int) and b == 0
                        for t in range(4):
                            for k in (2 * t, 2 * t + 1):
                                if not (first and k < 2):
                                    hi(kind, pl, k)
                            if t % 2:
                                up(b, t // 2, par, pl)
                            else:
                                gate(b, t // 2, pl)
                    else:
                        for k in range(4):
                            hi(kind, pl, k)

                def gate(b, f, pl):
                    for c in range(NPC):
                        wait_full(act, "proj", pl, 6 * f + c)
                        bnk, _ = pl.piece(6 * f + c)
                        c0, w = span(c)
                        act.activation(TH[:, c0:c0 + w], g.ps[bnk][:, 0:w], ACT.Tanh, scale=0.5).then_inc(s_th, 1)

                def up(b, f, par, pl):
                    for c in range(NPC):
                        bnk, turns = pl.piece(6 * f + 3 + c)
                        act.wait_ge(s_pf[bnk], turns + 1)
                        c0, w = span(c)
                        act.activation(Ah[:, par, f, c0:c0 + w], AC[:, c0:c0 + w], ACT.Copy).then_inc(s_ah, 1)

                act.wait_ge(s_ml[0], 16)
                for m in range(KC):
                    act.wait_ge(s_ml[m % 2], 16 * (m // 2 + 1))
                    act.activation(g.Hh[:, m, :], MX[:, m % 2, :], ACT.Copy).then_inc(s_mh, 1)
                run(act, step)
                for t in range(NT):
                    n = P if t < NC else NS
                    for b in range(2):
                        act.wait_ge(s_ft, 2 * t + b + 1)
                        if 2 * t + b:
                            act.wait_ge(s_fs, 2 * t + b)
                        act.activation(TH[0:n, 0:512], MISC[(2 * t + b) % 4][0:n, :], ACT.Square,
                                       accum_out=fss[0:n, t, b:b + 1]).then_inc(s_fs, 1)
                    act.wait_ge(s_fm, t + 1)
                    act.activation(fss[:, t, 2:3], fss[:, t, 2:3], ACT.Sqrt).then_inc(s_fr, 1)

            @block.gpsimd
            def _(pool):
                def lo(pl, k):
                    s, _, before = pl.half(k)
                    pool.wait_ge(s_hi, before + 1)
                    wait(pool, s_used, before - (RING - 1))
                    pool.tensor_tensor(Wl[:, s], raw[:, s], Wh[:, s].bitcast(F32), ALU.subtract).then_inc(s_lo, 1)

                def step(kind, b, par, pl):
                    if kind == "out":
                        for k in range(2):
                            lo(pl, k)
                    elif kind == "norm2":
                        p0 = Place(0, ["out"] * KC, None)
                        for n in range(KC):
                            bnk, turns = out_place(n).piece(2)
                            pool.wait_ge(s_pf[bnk], turns + 1)
                            if n == 0:
                                pool.tensor_tensor(SQ[:, :], X[:, 0, :], X[:, 0, :], ALU.mult).then_inc(s_sq, 1)
                            else:
                                pool.wait_ge(s_sq, n)
                                st.link(pool.tensor_tensor(SQT[:, :], X[:, n, :], X[:, n, :], ALU.mult))
                                pool.tensor_tensor(SQ[:, :], SQ[:, :], SQT[:, :], ALU.add).then_inc(s_sq, 1)
                        for k in range(2):
                            lo(p0, k)
                        for k in range(KC):
                            pool.wait_ge(s_hh, k + 1)
                            pool.tensor_tensor(g.Hl[:, k, :], (SQT, TH, SG)[k % 3][:, :], g.Hh[:, k, :].bitcast(F32), ALU.subtract).then_inc(s_hl, 1)
                    elif kind == "proj":
                        first = isinstance(b, int) and b == 0
                        for t in range(4):
                            for k in (2 * t, 2 * t + 1):
                                if not (first and k < 2):
                                    lo(pl, k)
                            if t % 2:
                                n = b * 6 + 3 * (t // 2)
                                for c in range(NPC):
                                    pool.wait_ge(s_ah, n + (c + 1))
                                    c0, w = span(c)
                                    pool.tensor_tensor(Al[:, par, t // 2, c0:c0 + w], AC[:, c0:c0 + w],
                                                       Ah[:, par, t // 2, c0:c0 + w].bitcast(F32), ALU.subtract).then_inc(s_al, 1)
                    else:
                        for k in range(4):
                            lo(pl, k)
                st = Steps(pool, s_pool)
                for m in range(KC):
                    pool.wait_ge(s_mh, m + 1)
                    pool.tensor_tensor(g.Hl[:, m, :], MX[:, m % 2, :], g.Hh[:, m, :].bitcast(F32), ALU.subtract).then_inc(s_mlo, 1)
                run(pool, step)

            @block.vector
            def _(dve):
                st = Steps(dve, s_dve)
                link = st.link

                def step(kind, b, par, pl):
                    if kind == "out":
                        for c in range(NPC):
                            if c == NPC - 1:
                                samples("out", pl, c, b, 2 * KC, b + 1)
                            add_prompt("out", pl, c, b, c, 2 * KC)
                    elif kind == "norm2":
                        dve.wait_ge(s_out, 16 * 4)
                        dve.wait_ge(s_sum, 1)
                        sums = MISC[3][:, 64:64 + 2 * NT].rearrange("p (t o) -> p t o", o=2)
                        dve.tensor_scalar(small[:, 0, 0:NC], sums[:, 0:NC, 0], 1.0 / D, EPS, ALU.mult, ALU.add)
                        dve.tensor_scalar(small[0:NS, 0, NC:NT], sums[0:NS, NC:NT, 0], 1.0 / D, EPS, ALU.mult, ALU.add).then_inc(s_ms, 1)
                        link(dve.scalar_tensor_tensor(am[:, :, :], g.ada[:, 4 * KC:5 * KC, :], 1.0,
                                                      bc(g.vec[:, V_G2:V_G2 + KC].unsqueeze(2), NCOND), ALU.add, ALU.mult))
                        dve.wait_ge(s_rt, 1)
                        link(dve.reciprocal(small[:, 2, :], small[:, 1, :]))
                        for t in range(NT):
                            if t:
                                dve.wait_ge(s_rb, t)
                            dve.tensor_scalar(RD[:, :], g.ones[:, :], small[:, 2, t:t + 1], None, ALU.mult).then_inc(s_rd, 1)
                        dve.wait_ge(s_rb, NT)
                        dve.wait_ge(s_sq, KC)
                        for k in range(KC):
                            t = (SQT, TH, SG)[k % 3]
                            if k >= 3:
                                dve.wait_ge(s_hl, k - 2)
                            for p in range(2):
                                st.did(dve.scalar_tensor_tensor(t[:, 512 * p:512 * p + 512], X[:, k, 512 * p:512 * p + 512], am[:, k, 0:1],
                                                                MISC[p][:, :], ALU.mult, ALU.mult))
                            v = seqv(t[:, SEQ:T])
                            link(dve.tensor_tensor(t[:, SEQ:T], X[:, k, SEQ:T], MISC[2][:, 0:NS], ALU.mult))
                            link(dve.tensor_tensor(v, v, bc(am[:, k, 1:NCOND].unsqueeze(2), SLEN), ALU.mult))
                            dve.tensor_scalar(t[:, 0:SEQ], t[:, 0:SEQ], g.ada[:, 3 * KC + k, 0:1], None, ALU.add)
                            dve.tensor_tensor(v, v, bc(g.ada[:, 3 * KC + k, 1:NCOND].unsqueeze(2), SLEN), ALU.add).then_inc(s_h, 1)
                    elif kind == "proj":
                        for f in range(2):
                            n = b * 6 + 3 * f
                            for c in range(NPC):
                                c0, w = span(c)
                                bnk, _ = pl.piece(6 * f + c)
                                dve.wait_ge(s_th, n + (c + 1))
                                dve.scalar_tensor_tensor(SG[:, c0:c0 + w], TH[:, c0:c0 + w], 1.0, g.ps[bnk][:, 0:w],
                                                         ALU.add, ALU.mult).then_inc(s_pf[bnk], 1)
                            for c in range(NPC):
                                c0, w = span(c)
                                bnk, bt = pl.piece(6 * f + 3 + c)
                                gb, gt = pl.piece(6 * f + c)
                                wait_full(dve, "proj", pl, 6 * f + 3 + c)
                                dve.wait_ge(s_pf[gb], gt + 1)
                                wait(dve, s_al, n - 3 + (c + 1))
                                dve.scalar_tensor_tensor(AC[:, c0:c0 + w], SG[:, c0:c0 + w], 0.5, g.ps[bnk][:, 0:w],
                                                         ALU.mult, ALU.mult).then_inc(s_pf[bnk], 1)
                    else:
                        for k in range(24):
                            n, c = 4 * (k // 12) + k % 12 // 3, k % 3
                            if c == NPC - 1:
                                samples("down", pl, k, n, 5 * KC, b * KC + (KC + n + 1))
                            add_prompt("down", pl, k, n, c, 5 * KC)

                def add_prompt(kind, pl, k, n, c, vec):
                    wait_full(dve, kind, pl, k)
                    bnk, _ = pl.piece(k)
                    c0, w = span(c)
                    m = min(w, SEQ - c0)
                    dve.scalar_tensor_tensor(X[:, n, c0:c0 + m], g.ps[bnk][:, 0:m], g.ada[:, vec + n, 0:1], X[:, n, c0:c0 + m],
                                             ALU.mult, ALU.add).then_inc(s_pf[bnk], 1)

                def samples(kind, pl, k, n, vec, count):
                    wait_full(dve, kind, pl, k)
                    bnk, _ = pl.piece(k)
                    wait(dve, s_stm, count * 2 - 2)
                    dve.tensor_tensor(seqv(stm[:, :]), seqv(g.ps[bnk][:, PC - NS:PC]), bc(g.ada[:, vec + n, 1:NCOND].unsqueeze(2), SLEN),
                                      ALU.mult).then_inc(s_stm, 1)
                    dve.wait_ge(s_stm, count * 2 - 1)
                    dve.tensor_tensor(X[:, n, SEQ:T], X[:, n, SEQ:T], stm[:, :], ALU.add).then_inc(s_stm, 1)

                dve.memset(small[:, 0, :], 1.0)
                dve.memset(fss[:, :, :], 1.0)
                dve.wait_ge(s_co, 1)
                for b in range(2):
                    dve.tensor_copy(co[0:KEEP, 512 * b:512 * b + 512], MISC[b][0:KEEP, :])
                dve.tensor_copy(stn[:, :], MISC[2][0:H * NCOND, 0:P]).then_inc(s_cc, 2)
                for t in range(NT):
                    n = P if t < NC else NS
                    for b in range(2):
                        u = 2 * t + b
                        dve.wait_ge(s_xt, u + 1)
                        dve.tensor_copy(X[:, 4 * b:4 * b + 4, t * P:t * P + n],
                                        MISC[u % 4][:, :].rearrange("p (k t) -> p k t", t=P)[:, :, 0:n]).then_inc(s_xe, 1)
                dve.wait_ge(s_xe, 2 * NT)
                run(dve, step)
                dve.wait_ge(s_gf, 16)
                for t in range(NT):
                    n = P if t < NC else NS
                    dve.wait_ge(s_fs, 2 * t + 2)
                    link(dve.tensor_tensor(fss[0:n, t, 2:3], fss[0:n, t, 0:1], fss[0:n, t, 1:2], ALU.add))
                    dve.tensor_scalar(fss[:, t, 2:3], fss[:, t, 2:3], 1.0 / D, EPS, ALU.mult, ALU.add).then_inc(s_fm, 1)
                    dve.wait_ge(s_fr, t + 1)
                    link(dve.reciprocal(fss[:, t, 3:4], fss[:, t, 2:3]))
                    if t >= 2:
                        dve.wait_ge(s_y[t % 2], 16 * (t // 2))
                    for b in range(2):
                        ins = dve.scalar_tensor_tensor(OT[0:n, t % 2, 512 * b:512 * b + 512], MISC[(2 * t + b) % 4][0:n, :], fss[0:n, t, 3:4],
                                                       GF[0:n, 512 * b:512 * b + 512], ALU.mult, ALU.mult)
                    ins.then_inc(s_fo, 1)


class Shared:
    pass


def build(nc, a, outs, loops=True):
    a = dict(a, **outs)
    g = Shared()
    g.dve_per = DVE_PER
    g.mix_d = nc.dram_tensor("mix_scratch", (P, KC, T), F32, kind="Internal").ap()
    with ExitStack() as ctx:
        sb = lambda n, s, d=F32: ctx.enter_context(nc.sbuf_tensor(n, s, d))
        g.ps = [ctx.enter_context(nc.psum_tensor(f"bank{n}", [P, 512], F32)) for n in range(8)]
        g.Hh = sb("h_hi", [P, KC, T], F32R)
        g.Hl = sb("h_lo", [P, KC, T], F32R)
        g.ident = sb("identity", [P, P])
        g.ones = sb("ones", [P, P])
        g.cmask = sb("causal", [P, P])
        g.cmask_s = sb("causal_samples", [NS, NS])
        g.lmask = sb("level_masks", [P, NL, P], U8)
        g.seqcol = sb("seq_columns", [NS, NSEQ])
        g.seqrow = sb("seq_rows", [P, NSEQ, NS])
        g.reset = sb("resets", [P, T], BF16)
        g.vec = sb("vectors", [P, P])
        g.cT = sb("c_t", [P, KC, NCOND])
        g.ada = sb("ada", [P, 6 * KC, NCOND])
        g.sconvT = sb("state_conv_t", [P, KC, NSEQ * (W4 - 1)])
        g.n0T = sb("state_n_t", [P, NSEQ * H])
        g.pk = sb("conv_keep", [P, KC, KEEP])
        g.nout = sb("n_out", [P, H * NCOND])
        setup_phase(nc, g, a)
        mixer_phase(nc, g, a, loops)
        ffn_phase(nc, g, a, loops)


DVE_PER = 34
LOOPS = True

_INS = ["x_prompt", "x_sample", "state_conv", "state_C", "state_n", "state_m", "state_S", "c_prompt", "c_sample",
        "g_norm1", "g_norm2", "w_ada", "b_ada", "w_in", "conv_w", "conv_b", "b_igate", "b_fgate", "g_head_a",
        "w_alpha", "b_alpha", "g_head_b", "w_out", "w_ffn_gate", "w_ffn_up", "w_ffn_down", "g_final"]
_OUTS = [("y_prompt", (1, SEQ, D)), ("y_sample", (NSEQ, SLEN, D)),
         ("conv_p", (1, 1, W4 - 1, 2 * QK)), ("C_p", (1, 1, H, DK, DV)), ("n_p", (1, 1, H, DK)), ("m_p", (1, 1, H)),
         ("S_p", (1, 1, H, DK, DV)),
         ("conv_s", (1, NSEQ, W4 - 1, 2 * QK)), ("C_s", (1, NSEQ, H, DK, DV)), ("n_s", (1, NSEQ, H, DK)), ("m_s", (1, NSEQ, H)),
         ("S_s", (1, NSEQ, H, DK, DV))]


def kernel(**inputs):
    import numpy as _np
    import concourse.bacc as _bacc
    from concourse.bass_utils import run_bass_kernel_spmd as _run

    nc = _bacc.Bacc("TRN2", target_bir_lowering=False, num_devices=1)
    arrays, args, outs = {}, {}, {}
    for name in _INS:
        x = _np.ascontiguousarray(inputs[name])
        arrays[f"in_{name}"] = x
        args[name] = nc.dram_tensor(f"in_{name}", x.shape, F32, kind="ExternalInput").ap()
    for name, shape in _OUTS:
        outs[name] = nc.dram_tensor(f"out_{name}", shape, F32, kind="ExternalOutput").ap()
    build(nc, args, outs, LOOPS)
    r = _run(nc, [arrays], core_ids=[0])
    return tuple(r.results[0][f"out_{name}"] for name, _ in _OUTS)
```

```python
from contextlib import ExitStack

import concourse.bass as bass
from concourse import mybir

F32 = mybir.dt.float32
F32R = mybir.dt.float32r
BF16 = mybir.dt.bfloat16
U8 = mybir.dt.uint8
ALU = mybir.AluOpType
ACT = mybir.ActivationFunctionType

P = 128
D = 1024
KC = D // P
SEQ = 1024
NSEQ, SLEN = 8, 4
NS = NSEQ * SLEN
T = SEQ + NS
NC = SEQ // P
NT = NC + 1
H, DK, DV = 4, 128, 256
VX = DV + 1
W4 = 4
RANK = 16
FF = 2816
FT = FF // P
EPS = 1e-6
QSCALE = DK ** -0.5
TAU = 16.0
BIG = 1e30
NPC = 3
PC = T // NPC
NCOND = 1 + NSEQ
ZP = SEQ + W4 - 1
ZS = SLEN + W4 - 1
ZN = ZP + NSEQ * ZS
ZO = ZN - (W4 - 1)
KEEP = (W4 - 1) * NCOND

QK = H * DK
C_QA, C_KA = 0, QK
C_VA = 2 * QK
C_OA = C_VA + H * DV
C_IF = C_OA + H * DV
C_QB = C_IF + 2 * H
C_KB = C_QB + QK
C_VB = C_KB + QK
C_RB = C_VB + H * DV
C_LR = C_RB + H * DV
C_GA = C_LR + RANK
C_GB = C_GA + D

V_BADA = 0
V_G1 = V_BADA + 6 * KC
V_G2 = V_G1 + KC
V_CW = V_G2 + KC
V_CB = V_CW + W4 * KC
V_HA = V_CB + KC
V_HB = V_HA + KC
V_AL = V_HB + KC
NV = V_AL + H

LEVELS = [64, 32, 16, 8, 4, 2, 1]
NL = len(LEVELS) + 1

ROW_A, ROW_W, ROW_L = 0, 32, 64


def wait(e, sem, v):
    if not (isinstance(v, int) and v <= 0):
        e.wait_ge(sem, v)


class Steps:

    def __init__(self, engine, sem, per=0):
        self.e, self.sem, self.per, self.base, self.n, self.i = engine, sem, per, None, 0, 0

    def turn(self, i):
        if self.per:
            if self.base is None:
                self.base = self.n
            self.i, self.n = i, 0

    def value(self):
        return self.i * self.per + ((self.base or 0) + self.n)

    def did(self, ins):
        ins.then_inc(self.sem, 1)
        self.n += 1
        return self.n

    def link(self, ins):
        self.did(ins)
        self.e.wait_ge(self.sem, self.value())


def bc(ap, n):
    return ap.to_broadcast(list(ap.shape[:-1]) + [n])


def mid(ap, n):
    return ap.unsqueeze(1).to_broadcast([ap.shape[0], n, ap.shape[1]])


def setup_phase(nc, g, a):
    with ExitStack() as ctx:
        sb = lambda n, s, d=F32: ctx.enter_context(nc.sbuf_tensor(n, s, d))
        sem = lambda n: ctx.enter_context(nc.semaphore(n))
        xs = sb("x_rows", [P, NT, D])
        vr = sb("vec_rows", [P, P])
        cr = sb("c_rows", [NCOND, D])
        nr = sb("n_rows", [NSEQ * H, DK])
        sr = sb("sconv_rows", [NSEQ * (W4 - 1), D])
        NW, KH, NA = 4, 2, 4
        wa = sb("w_ada_ring", [P, NW, KC // KH, 512])
        ar = sb("ada_rows", [NCOND, NA * 512])
        lmf = sb("level_masks_f", [P, NL, P])
        cT = g.cT
        am = sb("norm1_mult", [P, KC, NCOND])
        junk = sb("junk", [P, D])
        ssq = sb("ssq", [P, NT])
        rstd = sb("rstd", [P, NT])
        NTMP = 4
        tmp = sb("h_tmp", [P, NTMP, 4 * P])
        s_small, s_x = sem("small_loaded"), [sem(f"x_loaded{t}") for t in range(NT)]
        s_wa = [sem(f"w_ada_loaded{i}") for i in range(NW)]
        s_const, s_pool = sem("constants"), sem("pool_steps")
        s_tr, s_trc = sem("small_transposed"), sem("small_copied")
        s_adau, s_arow, s_ada = sem("w_ada_used"), sem("ada_rows_copied"), sem("ada_turned")
        s_ssq, s_t, s_sqrt, s_xn = sem("ssq_done"), sem("ms_done"), sem("sqrt_done"), sem("x_normed")
        s_dve = sem("dve_steps")
        s_xt = sem("x_transposed")
        s_ht, s_hi, s_lo, s_lov = sem("h_affine"), sem("h_hi"), sem("h_lo"), sem("h_lo_by_vector")
        units = [(k, q) for q in range(3) for k in range(KC)]
        NB = 4
        bank = lambda u: g.ps[u % NB]
        SMALLB, ADAB = g.ps[4], g.ps[5]
        O_V, O_C, O_N, O_S = 0, P, P + KC * NCOND, P + KC * NCOND + NSEQ * H

        EARLY = (6, 14)
        GROUPS = [(0, 4), (4, 8), (8, NT)]

        def cols(q):
            return (q * 4 * P, 4 * P) if q < 2 else (SEQ, NS)

        with nc.Block() as block:

            @block.sync
            def _(sp):
                def small(dst, src):
                    sp.dma_start(dst, src).then_inc(s_small, 16)
                small(vr[V_BADA:V_G1, :], a["b_ada"].rearrange("o (r c) -> (o r) c", c=P))
                small(vr[V_G1:V_G2, :], a["g_norm1"].rearrange("o (r c) -> (o r) c", c=P))
                small(vr[V_G2:V_CW, :], a["g_norm2"].rearrange("o (r c) -> (o r) c", c=P))
                small(vr[V_CW:V_CB, :], a["conv_w"].rearrange("o j (r c) -> (o j r) c", c=P))
                small(vr[V_CB:V_HA, :], a["conv_b"].rearrange("o (r c) -> (o r) c", c=P))
                small(vr[V_HA:V_HB, :], a["g_head_a"].rearrange("o h (r c) -> (o h r) c", c=P))
                small(vr[V_HB:V_AL, :], a["g_head_b"].rearrange("o h (r c) -> (o h r) c", c=P))
                small(vr[V_AL:NV, :], a["b_alpha"].rearrange("o (r c) -> (o r) c", c=P))
                small(cr[0:1, :], a["c_prompt"])
                small(cr[1:NCOND, :], a["c_sample"])
                small(nr[:, :], a["state_n"].rearrange("o b h d -> (o b h) d"))
                small(sr[:, :], a["state_conv"].rearrange("o b j c -> (o b j) c"))
                wsrc = a["w_ada"][0].rearrange("(k p) n -> p k n", p=P)
                for n in range(NA * KH):
                    if n >= NW:
                        sp.wait_ge(s_adau, n - NW + 1)
                    j, h = n // KH, n % KH
                    src = wsrc[:, h * KC // KH:(h + 1) * KC // KH, j * 512:(j + 1) * 512]
                    sp.dma_start(wa[:, n % NW], src).then_inc(s_wa[n % NW], 16)
                for t in range(NT):
                    if t < NC:
                        sp.dma_start(xs[:, t, :], a["x_prompt"][0, t * P:(t + 1) * P, :]).then_inc(s_x[t], 16)
                    else:
                        sp.dma_start(xs[0:NS, t, :], a["x_sample"].rearrange("b t d -> (b t) d")).then_inc(s_x[t], 16)

            @block.gpsimd
            def _(pool):
                st = Steps(pool, s_pool)
                ge = ALU.is_ge

                def keep(v, base, pattern, chan, fill=0.0, op=ge):
                    st.link(pool.affine_select(out=v, in_=v, compare_op=op, fill=fill, base=base,
                                               pattern=pattern, channel_multiplier=chan))
                st.link(pool.memset(g.ident[:, :], 0.0))
                keep(g.ident[:, :], 0, [[-1, P]], 1, fill=1.0, op=ALU.not_equal)
                pool.memset(g.ones[:, :], 1.0).then_inc(s_const, 1)
                st.link(pool.memset(g.cmask[:, :], BIG))
                keep(g.cmask[:, :], 0, [[1, P]], -1, fill=-BIG)
                st.link(pool.memset(g.cmask_s[:, :], BIG))
                keep(g.cmask_s[:, :], 0, [[1, NS]], -1, fill=-BIG)
                v = g.cmask_s[:, :].rearrange("s (b r) -> s b r", r=SLEN)
                keep(v, SLEN - 1, [[SLEN, NSEQ], [0, SLEN]], -1, fill=-BIG)
                keep(v, 0, [[-SLEN, NSEQ], [0, SLEN]], 1, fill=-BIG)
                st.link(pool.memset(g.seqcol[:, :], 1.0))
                keep(g.seqcol[:, :], SLEN - 1, [[SLEN, NSEQ]], -1)
                keep(g.seqcol[:, :], 0, [[-SLEN, NSEQ]], 1)
                st.link(pool.memset(g.seqrow[:, :, :], 1.0))
                keep(g.seqrow[:, :, :], SLEN - 1, [[SLEN, NSEQ], [-1, NS]], 0)
                keep(g.seqrow[:, :, :], 0, [[-SLEN, NSEQ], [1, NS]], 0)
                st.link(pool.memset(lmf[:, :, :], 0.0))
                for l, hs in enumerate(LEVELS):
                    n = P // (2 * hs)
                    v = lmf[:, l, :].rearrange("s (n w) -> s n w", w=2 * hs)[:, :, hs:2 * hs]
                    st.link(pool.memset(v, 1.0))
                    keep(v, 0, [[-2 * hs, n], [0, hs]], 1)
                    keep(v, hs - 1, [[2 * hs, n], [0, hs]], -1)
                st.link(pool.tensor_copy(lmf[:, NL - 1, :], g.ident[:, :]))
                st.link(pool.tensor_copy(g.lmask[:, :, :], lmf[:, :, :]))
                st.link(pool.memset(g.reset[:, :], 1.0))
                st.link(pool.memset(g.reset[:, 0:SEQ].rearrange("p (c t) -> p c t", t=P)[:, :, 0:1], 0.0))
                st.link(pool.memset(g.reset[:, SEQ:T].rearrange("p (b t) -> p b t", t=SLEN)[:, :, 0:1], 0.0))
                pool.memset(g.nout[:, :], 0.0)
                for u, (k, q) in enumerate(units):
                    if u % 2:
                        continue
                    c0, n = cols(q)
                    pool.wait_ge(s_hi, u + 1)
                    pool.tensor_tensor(g.Hl[:, k, c0:c0 + n], tmp[:, u % NTMP, 0:n], g.Hh[:, k, c0:c0 + n].bitcast(F32),
                                       ALU.subtract).then_inc(s_lo, 1)

            @block.tensor
            def _(pe):
                pe.wait_ge(s_small, 12 * 16)
                pe.wait_ge(s_const, 1)
                pe.transpose(SMALLB[:, O_V:O_V + NV], vr[0:NV, :], g.ident[0:NV, 0:NV])
                for k in range(KC):
                    pe.transpose(SMALLB[:, O_C + k * NCOND:O_C + (k + 1) * NCOND], cr[:, k * P:(k + 1) * P],
                                 g.ident[0:NCOND, 0:NCOND])
                pe.transpose(SMALLB[:, O_N:O_N + NSEQ * H], nr[:, :], g.ident[0:NSEQ * H, 0:NSEQ * H])
                m = NSEQ * (W4 - 1)
                last = None
                for k in range(KC):
                    if O_S + (k + 1) * m > 512:
                        raise ValueError("the small transposes outgrow their bank")
                    last = pe.transpose(SMALLB[:, O_S + k * m:O_S + (k + 1) * m], sr[:, k * P:(k + 1) * P], g.ident[0:m, 0:m])
                last.then_inc(s_tr, 1)
                pe.wait_ge(s_trc, 1)
                for n in range(NA * KH):
                    j, h = n // KH, n % KH
                    pe.wait_ge(s_wa[n % NW], 16 * (n // NW + 1))
                    if h == 0 and j >= 2:
                        pe.wait_ge(s_arow, j - 1)
                    for k in range(KC // KH):
                        last = pe.matmul(g.ps[6 + j % 2][0:NCOND, :], cT[:, h * KC // KH + k, :], wa[:, n % NW, k, :],
                                         start=(h == 0 and k == 0), stop=(h == KH - 1 and k == KC // KH - 1))
                    last.then_inc(s_adau, 1)
                for j in range(NA):
                    pe.wait_ge(s_arow, j + 1)
                    for n in range(4 * j, 4 * j + 4):
                        last = pe.transpose(ADAB[:, n * NCOND:(n + 1) * NCOND], ar[:, n * P:(n + 1) * P], g.ident[0:NCOND, 0:NCOND])
                last.then_inc(s_ada, 1)
                for u, (k, q) in enumerate(units):
                    if k == 0:
                        pe.wait_ge(s_xn, GROUPS[q][1])
                    if u >= NB:
                        pe.wait_ge(s_ht, u - NB + 1)
                    for t in range(4 * q, min(4 * q + 4, NT)):
                        n = P if t < NC else NS
                        last = pe.transpose(bank(u)[:, (t - 4 * q) * P:(t - 4 * q) * P + n], xs[0:n, t, k * P:(k + 1) * P],
                                            g.ident[0:n, 0:n])
                    last.then_inc(s_xt, 1)

            @block.scalar
            def _(act):
                act.wait_ge(s_t, 1)

                def squares(t):
                    n = P if t < NC else NS
                    if t:
                        act.wait_ge(s_ssq, t)
                    act.wait_ge(s_x[t], 16)
                    act.activation(junk[0:n, :], xs[0:n, t, :], ACT.Square, accum_out=ssq[0:n, t:t + 1]).then_inc(s_ssq, 1)

                def root(q):
                    t0, t1 = GROUPS[q]
                    act.wait_ge(s_t, q + 2)
                    act.activation(rstd[:, t0:t1], ssq[:, t0:t1], ACT.Sqrt).then_inc(s_sqrt, 1)
                for t in range(*GROUPS[0]):
                    squares(t)
                root(0)
                for u, (k, q) in enumerate(units):
                    if u in EARLY:
                        root(EARLY.index(u) + 1)
                    c0, n = cols(q)
                    act.wait_ge(s_ht, u + 1)
                    act.activation(g.Hh[:, k, c0:c0 + n], tmp[:, u % NTMP, 0:n], ACT.Copy).then_inc(s_hi, 1)
                    if u < NT - 4:
                        squares(4 + u)

            @block.vector
            def _(dve):
                st = Steps(dve, s_dve)
                dve.memset(ssq[:, :], 1.0).then_inc(s_t, 1)
                dve.wait_ge(s_tr, 1)
                dve.tensor_copy(cT[:, :, :], SMALLB[:, O_C:O_N].rearrange("p (k c) -> p k c", c=NCOND)).then_inc(s_trc, 1)
                st.link(dve.tensor_copy(g.vec[:, 0:NV], SMALLB[:, O_V:O_V + NV]))
                dve.tensor_copy(g.n0T[:, :], SMALLB[:, O_N:O_S])
                m = NSEQ * (W4 - 1)
                dve.tensor_copy(g.sconvT[:, :, :], SMALLB[:, O_S:O_S + KC * m].rearrange("p (k c) -> p k c", c=m))
                st.link(dve.tensor_scalar(g.vec[:, V_HA:V_AL], g.vec[:, V_HA:V_AL], 0.25, None, ALU.mult))
                for j in range(NA):
                    dve.wait_ge(s_adau, KH * (j + 1))
                    dve.tensor_copy(ar[:, j * 512:(j + 1) * 512], g.ps[6 + j % 2][0:NCOND, :]).then_inc(s_arow, 1)
                dve.wait_ge(s_ada, 1)
                st.link(dve.tensor_tensor(g.ada[:, 0:2 * KC, :], ADAB[:, 0:2 * KC * NCOND].rearrange("p (n c) -> p n c", c=NCOND),
                                          bc(g.vec[:, 0:2 * KC].unsqueeze(2), NCOND), ALU.add))
                st.link(dve.scalar_tensor_tensor(am[:, :, :], g.ada[:, KC:2 * KC, :], 1.0,
                                                 bc(g.vec[:, V_G1:V_G1 + KC].unsqueeze(2), NCOND), ALU.add, ALU.mult))

                def normed(q):
                    t0, t1 = GROUPS[q]
                    dve.wait_ge(s_ssq, t1)
                    dve.tensor_scalar(ssq[:, t0:t1], ssq[:, t0:t1], 1.0 / D, EPS, ALU.mult, ALU.add).then_inc(s_t, 1)
                    dve.wait_ge(s_sqrt, q + 1)
                    st.link(dve.reciprocal(ssq[:, t0:t1], rstd[:, t0:t1]))
                    for t in range(t0, t1):
                        n = P if t < NC else NS
                        dve.tensor_scalar(xs[0:n, t, :], xs[0:n, t, :], ssq[0:n, t:t + 1], None, ALU.mult).then_inc(s_xn, 1)

                def lower(u):
                    k, q = units[u]
                    c0, n = cols(q)
                    dve.wait_ge(s_hi, u + 1)
                    dve.tensor_tensor(g.Hl[:, k, c0:c0 + n], tmp[:, u % NTMP, 0:n], g.Hh[:, k, c0:c0 + n].bitcast(F32),
                                      ALU.subtract).then_inc(s_lov, 1)
                for u, (k, q) in enumerate(units):
                    if u == 0:
                        normed(0)
                    if u in EARLY:
                        normed(EARLY.index(u) + 1)
                    dve.wait_ge(s_xt, u + 1)
                    if u >= NTMP:
                        dve.wait_ge(s_lov if u % 2 else s_lo, (u - NTMP) // 2 + 1)
                    if q < 2:
                        dve.tensor_scalar(tmp[:, u % NTMP, :], bank(u)[:, :], am[:, k, 0:1], g.ada[:, k, 0:1],
                                          ALU.mult, ALU.add).then_inc(s_ht, 1)
                    else:
                        v = tmp[:, u % NTMP, 0:NS].rearrange("p (b r) -> p b r", r=SLEN)
                        st.link(dve.tensor_tensor(v, bank(u)[:, 0:NS].rearrange("p (b r) -> p b r", r=SLEN),
                                                  bc(am[:, k, 1:NCOND].unsqueeze(2), SLEN), ALU.mult))
                        dve.tensor_tensor(v, v, bc(g.ada[:, k, 1:NCOND].unsqueeze(2), SLEN), ALU.add).then_inc(s_ht, 1)
                    if u >= 2 and u % 2 == 0:
                        lower(u - 1)
                lower(len(units) - 1)


TILES = {"S": ["small", "q", "v0", "k", "v1"],
         "A": ["q", "v0", "k", "v1", "o0", "g0", "o1", "g1"],
         "B": ["q", "v0", "k", "v1", "o0", "g0", "o1", "g1"],
         "L": ["o0", "g0", "o1", "g1"]}
NS_TILES, NW_TILES = len(TILES["S"]), len(TILES["A"])
COLUMN = {("A", "q"): (C_QB, DK), ("A", "k"): (C_KB, DK), ("A", "v"): (C_VB, DV), ("A", "o"): (C_OA, DV), ("A", "g"): (C_GA, DV),
          ("B", "q"): (C_QA, DK), ("B", "k"): (C_KA, DK), ("B", "v"): (C_VA, DV), ("B", "o"): (C_RB, DV), ("B", "g"): (C_GB, DV)}
CHAIN = [f"chunk{c}" for c in range(NC)]
SAMPLE = [f"sample{b}" for b in range(NSEQ)]
AT_SLOT = {
    "S": [("rows", 6), ("rows_exp", 13), ("conv_q", 14), ("taps_q", 14), ("silu_q", 17), ("rows_t", 21), ("vt0", 21),
          ("conv_k", 25), ("taps_k", 26), ("silu_k", 29), ("vt1", 29)],
    "A": [("select", 0), ("decay", 1), ("ada_load0", 2), ("scores", 4), ("keys", 8), ("interq", 8), ("ada0", 9), ("masked", 9),
          ("chunk0", 11), ("ada_load1", 12), ("chunk1", 13), ("vt0", 14), ("chunk2", 15), ("chunk3", 17), ("chunk4", 19),
          ("ada1", 21), ("chunk5", 23), ("chunk6", 23), ("chunk7", 23), ("ada_load2", 24), ("vt1", 26), ("sample_out", 27),
          ("sample0", 29), ("sample1", 31), ("sample2", 31), ("sample3", 32), ("ada2", 33), ("sample4", 33), ("gate0", 35),
          ("sample5", 35), ("ada_load3", 36), ("sample6", 36), ("sample7", 37), ("alpha", 37), ("norm", 39), ("turn0", 44),
          ("ada3", 45), ("gate1", 47), ("turn1", 47)],
    "B": [("ada_load0", 0), ("sums", 3), ("level0", 5), ("conv_q", 7), ("level1", 7), ("taps_q", 8), ("ada0", 9),
          ("level2", 10), ("silu_q", 10), ("ada_load1", 12), ("level3", 13), ("level4", 16), ("vt0", 17), ("conv_k", 18),
          ("level5", 19), ("taps_k", 19), ("ada1", 21), ("level6", 22), ("silu_k", 22), ("level7", 23), ("ada_load2", 24),
          ("vt1", 26), ("masked", 27), ("keys", 30), ("chunk0", 30), ("chunk1", 30), ("chunk2", 31), ("chunk3", 32),
          ("chunk4", 33), ("ada2", 33), ("chunk5", 33), ("gate_r0", 34), ("chunk6", 35), ("chunk7", 36), ("ada_load3", 36),
          ("sample_out", 36), ("sample0", 36), ("sample1", 36), ("sample2", 38), ("sample3", 38), ("sample4", 39),
          ("sample5", 39), ("gate0", 39), ("sample6", 40), ("sample7", 41), ("norm", 42), ("gate_r1", 44), ("ada3", 45),
          ("gate1", 46), ("turn0", 47), ("turn1", 47)],
    "L": [("sums", 0), ("ada_load0", 2), ("level0", 2), ("level1", 3), ("level2", 4), ("level3", 5), ("gate_r0", 5),
          ("ada0", 6), ("level4", 7), ("ada_load1", 8), ("level5", 8), ("level6", 10), ("level7", 11), ("ada1", 12),
          ("keys", 12), ("masked", 12), ("gate0", 13), ("chunk0", 13), ("ada_load2", 14), ("chunk1", 14), ("chunk2", 14),
          ("chunk3", 15), ("chunk4", 15), ("chunk5", 16), ("chunk6", 16), ("chunk7", 17), ("ada2", 18), ("sample_out", 18),
          ("sample0", 18), ("sample1", 19), ("sample2", 19), ("sample3", 19), ("sample4", 19), ("sample5", 19),
          ("sample6", 19), ("ada_load3", 20), ("sample7", 20), ("gate_r1", 22), ("gate1", 22), ("ada3", 23), ("norm", 23),
          ("turn0", 23), ("turn1", 23)],
}
USES = {"decay": 3, "scores": 3, "interq": 3, "keys": 3, "vt0": 3, "vt1": 3, "sample_out": 1, "turn0": 3, "turn1": 3,
        "alpha": 3, "rows_t": 3, **{s: 2 for s in CHAIN}, **{s: 1 for s in SAMPLE}, **{f"ada{q}": 1 for q in range(4)},
        **{f"level{l}": 1 + (l >= NL - 3) + (l == NL - 1) for l in range(NL)}}


def timeline(w):
    out, stages = [], sorted(AT_SLOT[w], key=lambda x: x[1])
    for s in range(6 * len(TILES[w])):
        out.append(("piece", s // 6, s // 3 % 2, s % 3))
        out += [(n,) for n, at in stages if at == s]
    assert len([x for x in out if len(x) == 1]) == len(stages)
    return out


TIMELINE = {w: timeline(w) for w in TILES}
USE = {w: {} for w in TILES}
NUSE = {}
for _w in TILES:
    _n = 0
    for _x in TIMELINE[_w]:
        if len(_x) == 1 and _x[0] in USES:
            USE[_w][_x[0]] = _n
            _n += USES[_x[0]]
    NUSE[_w] = _n
BEGUN = 1
NRB = 4


def uses_before(w, i, n):
    b = n % NRB
    mine = lambda w, m: sum(1 for x in range(m) if x % NRB == b)
    total, own = NUSE["S"], mine("S", NUSE["S"])
    if w == "S":
        return n, mine("S", n)
    total, own = total + i * (NUSE["A"] + NUSE["B"]), own + i * (mine("A", NUSE["A"]) + mine("B", NUSE["B"]))
    if w in "BL":
        total, own = total + NUSE["A"], own + mine("A", NUSE["A"])
    return total + n, own + mine(w, n)


def tile_index(w, i, l):
    return l if w == "S" else i * 2 * NW_TILES + (NS_TILES + l + (NW_TILES if w in "BL" else 0))


def after(w, i, l, h, by):
    l, h = l + (h + by) // 2, (h + by) % 2
    while l >= len(TILES[w]):
        l -= len(TILES[w])
        if w == "L":
            return None
        if w == "B":
            w, i = "A", i + 1
        else:
            w, i = ("A" if w == "S" else "L" if isinstance(i, int) and i == H - 1 else "B"), i
    return w, i, l, h


def static(i, per, k, n):
    assert per % n == 0
    return k % n, i * (per // n) + k // n


def mixer_phase(nc, g, a, loops=True):
    with ExitStack() as ctx:
        sb = lambda n, s, d=F32: ctx.enter_context(nc.sbuf_tensor(n, s, d))
        sem = lambda n: ctx.enter_context(nc.semaphore(n))
        RAW, SPL = 4, 2
        raw = sb("w_raw", [P, RAW, 4, P])
        Wh = sb("w_hi", [P, SPL, 4, P], F32R)
        Wl = sb("w_lo", [P, SPL, 4, P], F32R)
        Q = [sb("q_a", [P, T]), sb("q_b", [P, T])]
        K = [sb("k_a", [P, T]), sb("k_b", [P, T])]
        V = [sb("v_a", [P, NT, VX]), sb("v_b", [P, NT, VX])]
        Z = sb("conv_in", [P, ZN])
        CV = sb("conv_out", [P, ZN])
        VS = sb("v_stage", [P, T])
        G = sb("gate", [P, 2, T])
        TG = sb("gate_t", [P, T])
        AT = sb("scores_t", [P, T])
        QD = sb("q_decayed", [P, T])
        KD = sb("k_decayed", [P, NT * P])
        TA = sb("temp_a", [P, T])
        TB = sb("temp_b", [P, T])
        ST = sb("sample_state", [P, NSEQ, VX])
        SS = sb("state", [P, 2, VX])
        M = sb("mix", [P, 2, T])
        HS = sb("sample_heads", [P, VX])
        QM = sb("q_masked", [P, NSEQ, NS])
        rows = sb("gate_rows", [P, T])
        cols = sb("gate_cols", [P, NT, 3 * H])
        hcol = sb("head_cols", [P, NT, 3])
        wcr = sb("carry_rows", [H, 2 * NC])
        wcs = sb("carry_sel", [H, 2 * NC])
        sdec = sb("state_decay", [P, 2 * NC])
        wal = sb("w_alpha_all", [P, QK])
        walh = sb("w_alpha_head", [P, DK])
        bif = sb("b_if", [H, 2])
        m0 = sb("m0", [H, NSEQ])
        me = sb("m_ends", [H, 4, 2 * NC])
        ssq = sb("head_ssq", [P, NT])
        den = sb("head_den", [P, NT])
        ms = sb("head_ms", [P, NT])
        scl = sb("head_scale", [P, NT])
        wad = sb("w_ada_tile", [P, KC, P])

        s_w = [sem(f"w_loaded{n}") for n in range(RAW)]
        s_zero = sem("w_raw_zeroed")
        s_hi, s_lo, s_used = sem("w_hi_made"), sem("w_lo_made"), sem("w_used")
        s_piece = sem("pieces_full")
        s_pfree = [sem(f"piece_bank_free{n}") for n in range(4)]
        s_full = sem("rec_bank_full")
        s_free = [sem(f"rec_bank_free{n}") for n in range(NRB)]
        s_small, s_init = sem("small_in"), sem("buffers_set")
        s_dve, s_pool = sem("dve_chain"), sem("pool_chain")
        s_r1, s_r2, s_r3, s_rows = sem("rows_x"), sem("rows_exp"), sem("rows_args"), sem("rows_ready")
        s_cols = sem("gate_cols_ready")
        s_cv, s_th, s_silu = sem("conv_done"), sem("conv_tanh"), sem("conv_silu")
        s_sel, s_warg, s_wexp = sem("rows_selected"), sem("decay_args"), sem("decay_exp")
        s_qd, s_km = sem("q_decayed_ready"), sem("sample_masked")
        s_hc = sem("heads_copied")
        s_stl, s_sts = sem("sample_state_loaded"), sem("states_stored")
        s_ms, s_sq, s_hn = sem("head_ms_ready"), sem("head_sqrt"), sem("heads_normed")
        s_gr, s_gate, s_sum = sem("gate_r"), sem("gate_ready"), sem("mixers_summed")
        s_mst = sem("mix_stored")
        s_x, s_nab, s_ln, s_b = sem("alpha_x"), sem("alpha_nab"), sem("alpha_ln"), sem("b_sums")
        s_d, s_E, s_qe, s_ke, s_at0 = sem("level_diff"), sem("level_exp"), sem("level_q"), sem("level_k"), sem("scores_zeroed")
        s_wah = sem("w_alpha_sliced")
        s_kt = sem("k_scaled")
        s_adl = sem("ada_tile_loaded")

        w_in = a["w_in"][0].rearrange("(k p) n -> p k n", p=P)
        w_ada = a["w_ada"][0].rearrange("(k p) n -> p k n", p=P)
        isB = lambda w: w in "BL"

        def half(w, i, l, h):
            per = 4 * NW_TILES
            if w == "S":
                k, j = 2 * l + h, 0
            else:
                k, j = 2 * (NS_TILES + l + (NW_TILES if isB(w) else 0)) + h, i
            r, turns = static(j, per, k, RAW)
            s, _ = static(j, per, k, SPL)
            return r, s, turns, j * per + k

        def piece(w, i, l, c):
            per = 3 * 2 * NW_TILES
            if w == "S":
                k, j = 3 * l + c, 0
            else:
                k, j = 3 * (NS_TILES + l + (NW_TILES if isB(w) else 0)) + c, i
            return static(j, per, k, 4)

        def two(w, i, per=1, first=0):
            return i * (2 * per) + (first + (per if isB(w) else 0))

        def span(c):
            return c * PC, PC

        def wait_piece(e, w, i, l, c):
            if c < 2:
                t = tile_index(w, i, l)
                e.wait_ge(s_piece, t * 2 + (c + 1))
            else:
                e.wait_ge(s_used, half(w, i, l, 1)[3] + 1)

        def wait_evacuated(e, w, i, l):
            b, turns = piece(w, i, l, NPC - 1)
            e.wait_ge(s_pfree[b], turns + 1)

        def wait_use(e, w, i, n):
            e.wait_ge(s_full, uses_before(w, i, n)[0] + 1)

        def apart(e):
            e.nop(nofuse=True)

        def wait_read_use(e, w, i, n):
            e.wait_ge(s_free[n % NRB], uses_before(w, i, n)[1] + 1)

        def wait_read(e, w, i, stage):
            wait_read_use(e, w, i, USE[w][stage] + USES[stage] - 1)

        RB = lambda n: g.ps[4 + n % NRB]
        free = lambda n: s_free[n % NRB]
        PARTS = [(0, 512), (512, 512), (SEQ, NS)]

        def chunks(v):
            return v[:, 0:SEQ].rearrange("p (c t) -> p c t", t=P)

        HP = P // 2

        def halves(v, l, right):
            hs = LEVELS[l]
            return v.rearrange("p (n w) -> p n w", w=2 * hs)[:, :, hs * right:hs * (1 + right)]

        def seqs(v):
            return v[:, SEQ:T].rearrange("p (b t) -> p b t", t=SLEN)

        def run(engine, turn, body):
            body("S", 0)
            if loops:
                with engine.Fori(0, H - 1) as i:
                    body("A", i)
                    body("B", i)
            else:
                for i in range(H - 1):
                    body("A", i)
                    body("B", i)
            body("A", H - 1)
            body("L", H - 1)

        with nc.Block() as block:

            @block.sync
            def _(sp):
                def load_half(w, i, l, h):
                    r, _, turns, before = half(w, i, l, h)
                    wait(sp, s_lo, before - (RAW - 1))
                    name = TILES[w][l]
                    dst = raw[:, r]
                    if name == "small":
                        sp.wait_ge(s_zero, 1)
                        for c0, n, at in ((C_IF, H, 0), (C_IF + H, H, 32), (C_LR, RANK, 64)):
                            sp.dma_start(dst[:, :, at:at + n], w_in[:, 4 * h:4 * h + 4, c0:c0 + n]).then_inc(s_w[r], 16)
                        return
                    base, step = COLUMN["B" if w in "SL" else w, name[0]]
                    head = 0 if w == "S" else i + 1 if w == "B" and name[0] in "qkv" else i
                    c0 = head * step + (base + (P if name[1:] == "1" else 0))
                    src = w_in[:, 4 * h:4 * h + 4, bass.ds(c0, P)]
                    sp.dma_start(dst, src).then_inc(s_w[r], 16)

                small = [(bif[:, 0:1], a["b_igate"].rearrange("o h -> h o")), (bif[:, 1:2], a["b_fgate"].rearrange("o h -> h o")),
                         (m0[:, :], a["state_m"][0].rearrange("b h -> h b")), (wal[64:64 + RANK, :], a["w_alpha"][0])]
                sp.nop().then_inc(s_sts, BEGUN)
                sp.nop().then_inc(s_mst, BEGUN)
                load_half("S", 0, 0, 0)
                load_half("S", 0, 0, 1)
                for dst, src in small:
                    sp.dma_start(dst, src, allow_slow_non_contiguous=True).then_inc(s_small, 16)
                load_half("S", 0, 1, 0)

                def window(w, i):
                    for x in TIMELINE[w]:
                        if x[0] == "piece":
                            _, l, h, c = x
                            nxt = after(w, i, l, h, RAW - 1)
                            if c == 0 and nxt:
                                load_half(*nxt)
                        elif x[0].startswith("ada_load"):
                            q = int(x[0][-1])
                            n = two(w, i, 4) + q
                            wait_use(sp, w, i, USE[w][f"ada{q - 1}"] if q else 0)
                            sp.dma_start(wad[:, :, :], w_ada[:, :, bass.ds(n * P + 2 * D, P)]).then_inc(s_adl, 16)
                            if q == 0:
                                sp.wait_ge(s_sts, BEGUN + two(w, i, 32))
                                apart(sp)
                                sp.wait_ge(s_ms, BEGUN + two(w, i))
                                src = a["state_S"] if isB(w) else a["state_C"]
                                sp.dma_start(ST[:, :, 0:DV], src[0, :, bass.ds(i, 1)].rearrange("b h d v -> d (h b) v")).then_inc(s_stl, 16)
                        elif x[0] == "norm":
                            wait_read(sp, w, i, SAMPLE[-1])
                            dst = a["S_p"] if isB(w) else a["C_p"]
                            sp.dma_start(dst[0, 0, bass.ds(i, 1)].rearrange("h d v -> d h v"), SS[:, 1:2, 0:DV]).then_inc(s_sts, 16)
                            dst = a["S_s"] if isB(w) else a["C_s"]
                            sp.dma_start(dst[0, :, bass.ds(i, 1)].rearrange("b h d v -> d (h b) v"), ST[:, :, 0:DV]).then_inc(s_sts, 16)
                        elif x[0] == "rows_t":
                            sp.wait_ge(s_rows, 1)
                            sp.dma_start(a["m_p"][0].rearrange("o h -> h o"), me[:, 1, NC - 1:NC], allow_slow_non_contiguous=True).then_inc(s_small, 16)
                            sp.dma_start(a["m_s"][0].rearrange("b h -> h b"), me[:, 1, NC:2 * NC], allow_slow_non_contiguous=True).then_inc(s_small, 16)
                    if isB(w):
                        sp.wait_ge(s_sum, BEGUN + i * 2 + 2)
                        sp.dma_start(g.mix_d[:, bass.ds(i * 2, 2), :], M[:, :, :]).then_inc(s_mst, 16)
                run(sp, None, window)
                sp.wait_ge(s_small, 16 * (len(small) + 2))
                sp.wait_ge(s_sts, BEGUN + 32 * 2 * H)
                sp.wait_ge(s_mst, BEGUN + 16 * H)

            @block.tensor
            def _(pe):
                def mm_piece(w, i, l, h, c):
                    _, s, _, before = half(w, i, l, h)
                    b, turns = piece(w, i, l, c)
                    if c == 0:
                        pe.wait_ge(s_lo, before + 1)
                    if h == 0:
                        wait(pe, s_pfree[b], turns)
                    c0, n = span(c)
                    for k in range(4):
                        for m, (x, y) in enumerate(((Wh, g.Hh), (Wh, g.Hl), (Wl, g.Hh))):
                            last = pe.matmul(g.ps[b][:, 0:n], x[:, s, k, :], y[:, 4 * h + k, c0:c0 + n],
                                             start=(h == 0 and k == 0 and m == 0), stop=(h == 1 and k == 3 and m == 2))
                    if c == 2:
                        last.then_inc(s_used, 1)
                    elif h == 1:
                        last.then_inc(s_piece, 1)

                def window(w, i):
                    hd = 1 if isB(w) else 0
                    vw = DV if isB(w) else VX
                    q, k, v = Q[hd], K[hd], V[hd]

                    def use(n):
                        wait(pe, free(n), uses_before(w, i, n)[1])
                        return RB(n)

                    def full(ins):
                        ins.then_inc(s_full, 1)

                    def scores(n, kk, qq, samples=True):
                        for b in range(2):
                            bank = use(n + b)
                            for c in range(4 * b, 4 * b + 4):
                                last = pe.matmul(bank[:, (c % 4) * P:(c % 4 + 1) * P], kk[:, c * P:(c + 1) * P],
                                                 qq[:, c * P:(c + 1) * P], start=True, stop=True)
                            full(last)
                        if samples:
                            bank = use(n + 2)
                            apart(pe)
                            full(pe.matmul(bank[0:NS, 0:NS], kk[:, SEQ:T], qq[:, SEQ:T], start=True, stop=True))

                    def turned(n, src):
                        for b in range(2):
                            bank = use(n + b)
                            for c in range(4 * b, 4 * b + 4):
                                last = pe.transpose(bank[:, (c % 4) * P:(c % 4 + 1) * P], src[:, c * P:(c + 1) * P], g.ident[:, :])
                            full(last)
                        full(pe.transpose(use(n + 2)[0:NS, 0:P], src[:, SEQ:T], g.ident[:, :]))

                    for x in TIMELINE[w]:
                        if x[0] == "piece":
                            mm_piece(w, i, *x[1:])
                            continue
                        name = x[0]
                        n = USE[w].get(name)
                        if name == "rows_t":
                            pe.wait_ge(s_rows, 1)
                            for b in range(2):
                                bank = use(n + b)
                                for c in range(4 * b, 4 * b + 4):
                                    last = pe.transpose(bank[:, (c % 4) * P:(c % 4) * P + 68], G[0:68, 0, c * P:(c + 1) * P],
                                                        g.ident[0:68, 0:68])
                                full(last)
                            full(pe.transpose(use(n + 2)[0:NS, 0:68], G[0:68, 0, SEQ:T], g.ident[0:68, 0:68]))
                        elif name in ("vt0", "vt1"):
                            wait_evacuated(pe, w, i, TILES[w].index("v" + name[2]))
                            turned(n, VS)
                        elif name == "decay":
                            pe.wait_ge(s_sel, i + 1)
                            for b, (c0, m) in enumerate(PARTS):
                                last = pe.matmul(use(n + b)[:, 0:m], g.ones[0:H, :], TB[0:H, c0:c0 + m], start=True, stop=True)
                                if b < 2:
                                    full(last)
                            full(pe.matmul(RB(n + 2)[:, NS:NS + 2 * NC], g.ones[0:H, :], wcs[:, :], start=True, stop=True))
                        elif name == "scores":
                            pe.wait_ge(s_silu, i * 2 + 2)
                            scores(n, k, q)
                        elif name == "interq":
                            for b, (c0, m) in enumerate(PARTS):
                                full(pe.matmul(use(n + b)[:, 0:m], g.ones[32:32 + H, :], TB[32:32 + H, c0:c0 + m], start=True, stop=True))
                        elif name == "keys":
                            if isB(w):
                                pe.wait_ge(s_kt, i + 1)
                                turned(n, TB)
                            else:
                                turned(n, k)
                        elif name == "alpha":
                            pe.wait_ge(s_wah, i + 1)
                            for b, (c0, m) in enumerate(PARTS):
                                full(pe.matmul(use(n + b)[:, 0:m], walh[64:64 + RANK, :], rows[64:64 + RANK, c0:c0 + m], start=True, stop=True))
                        elif name.startswith("level"):
                            l = int(name[5:])
                            if l < NL - 1:
                                pe.wait_ge(s_qe, i * (NL - 1) + (l + 1))
                                pe.wait_ge(s_ke, i * (NL - 1) + (l + 1))
                                bank = use(n)
                                for c in range(NC):
                                    last = pe.matmul(bank[:, c * HP:(c + 1) * HP], KD[:, c * P:(c + 1) * P],
                                                     halves(QD[:, c * P:(c + 1) * P], l, 1), start=True, stop=True)
                                full(last)
                                if USES[name] == 2:
                                    bank = use(n + 1)
                                    apart(pe)
                                    full(pe.matmul(bank[0:NS, 0:NS], KD[:, SEQ:T], QD[:, SEQ:T], start=True, stop=True))
                            else:
                                scores(n, k, q)
                        elif name in CHAIN:
                            c = CHAIN.index(name)
                            if c == 0:
                                wait_read(pe, w, i, "keys")
                                apart(pe)
                                wait_read(pe, w, i, f"level{NL - 1}" if isB(w) else "scores")
                                apart(pe)
                                if isB(w):
                                    pe.wait_ge(s_qd, i + 1)
                                else:
                                    wait_read(pe, w, i, "interq")
                                    apart(pe)
                            full(pe.matmul(use(n)[:, 0:vw], KD[:, c * P:(c + 1) * P], v[:, c, 0:vw], start=True, stop=True))
                            bank = use(n + 1)
                            last = pe.matmul(bank[:, 0:vw], AT[:, c * P:(c + 1) * P], v[:, c, 0:vw], start=True, stop=(c == 0))
                            if c:
                                wait_read_use(pe, w, i, USE[w][CHAIN[c - 1]])
                                last = pe.matmul(bank[:, 0:vw], QD[:, c * P:(c + 1) * P], SS[:, (c - 1) % 2, 0:vw], start=False, stop=True)
                            full(last)
                        elif name == "sample_out":
                            pe.wait_ge(s_km, two(w, i) + 1)
                            pe.wait_ge(s_stl, two(w, i, 16) + 16)
                            bank = use(n)
                            apart(pe)
                            pe.matmul(bank[0:NS, 0:vw], AT[0:NS, SEQ:T], v[0:NS, NC, 0:vw], start=True, stop=False)
                            for b in range(NSEQ):
                                last = pe.matmul(bank[0:NS, 0:vw], QM[:, b, :], ST[:, b, 0:vw], start=False, stop=(b == NSEQ - 1))
                            full(last)
                        elif name in SAMPLE:
                            b = SAMPLE.index(name)
                            full(pe.matmul(use(n)[:, 0:vw], TB[0:NS, b * P:(b + 1) * P], v[0:NS, NC, 0:vw], start=True, stop=True))
                        elif name in ("turn0", "turn1"):
                            j = int(name[4])
                            pe.wait_ge(s_hn, two(w, i) + 1)
                            for b in range(2):
                                bank = use(n + b)
                                for c in range(4 * b, 4 * b + 4):
                                    last = pe.transpose(bank[:, (c % 4) * P:(c % 4 + 1) * P], v[:, c, j * P:(j + 1) * P], g.ident[:, :])
                                full(last)
                            bank = use(n + 2)
                            apart(pe)
                            full(pe.transpose(bank[:, 0:NS], HS[0:NS, j * P:(j + 1) * P], g.ident[0:NS, 0:NS]))
                        elif name.startswith("ada") and name[3] != "_":
                            m = two(w, i, 4) + int(name[3])
                            pe.wait_ge(s_adl, m * 16 + 16)
                            bank = use(n)
                            for kc in range(KC):
                                last = pe.matmul(bank[:, 0:NCOND], wad[:, kc, :], g.cT[:, kc, :], start=(kc == 0), stop=(kc == KC - 1))
                            full(last)
                run(pe, None, window)

            @block.scalar
            def _(act):
                def split_hi(w, i, l, h):
                    r, s, turns, before = half(w, i, l, h)
                    act.wait_ge(s_w[r], turns * 16 + (16 + (32 if r < 2 else 0)))
                    wait(act, s_used, before - (SPL - 1))
                    act.activation(Wh[:, s], raw[:, r], ACT.Copy).then_inc(s_hi, 1)

                def evacuate(w, i, l, c):
                    name = TILES[w][l]
                    b, _ = piece(w, i, l, c)
                    c0, n = span(c)
                    src = g.ps[b][:, 0:n]
                    wait_piece(act, w, i, l, c)
                    t = tile_index(w, i, l)
                    last_c = c == NPC - 1
                    cut = SEQ - c0 if last_c else n

                    conv = name in ("q", "k") and w in "SB"
                    if name == "small":
                        act.activation(M[0:H, 0, c0:c0 + n], src[0:H], ACT.Copy)
                        act.activation(M[0:H, 1, c0:c0 + n], src[32:32 + H], ACT.Copy)
                        last = act.activation(rows[64:64 + RANK, c0:c0 + n], src[64:64 + RANK], ACT.Copy)
                    elif conv:
                        if c == 0:
                            nth = (0 if w == "S" else i * 2 + 2) + (1 if name == "k" else 0)
                            wait(act, s_silu, nth)
                        last = act.activation(Z[:, W4 - 1 + c0:W4 - 1 + c0 + cut], src[:, 0:cut], ACT.Copy)
                        if last_c:
                            z = Z[:, ZP:ZN].rearrange("p (b t) -> p b t", t=ZS)[:, :, W4 - 1:ZS]
                            last = act.activation(z, src[:, cut:n].rearrange("p (b t) -> p b t", t=SLEN), ACT.Copy)
                    elif name in ("q", "k"):
                        last = act.activation((Q if name == "q" else K)[1][:, c0:c0 + n], src, ACT.Copy,
                                              scale=QSCALE if name == "q" else 1.0)
                    elif name[0] == "v":
                        last = act.activation(VS[:, c0:c0 + n], src, ACT.Copy)
                    elif name[0] == "o":
                        j = int(name[1])
                        if c == 0:
                            if isB(w):
                                wait_read(act, "A", i, f"turn{j}")
                                act.wait_ge(s_gate, BEGUN + i * 4 + (2 + j))
                            else:
                                act.wait_ge(s_sum, BEGUN + i * 2)
                        last = act.activation(G[:, j, c0:c0 + n], src, ACT.Tanh, scale=0.5)
                        if isB(w):
                            last = act.activation(TG[:, c0:c0 + n], src, ACT.Copy)
                    else:
                        if c == 0:
                            if isB(w):
                                act.wait_ge(s_gr, i * 2 + (int(name[1]) + 1))
                            else:
                                act.wait_ge(s_gate, BEGUN + two(w, i, 2) + int(name[1]))
                        last = act.activation(TG[:, c0:c0 + n], src, ACT.Tanh, scale=0.5)
                    last.then_inc(s_pfree[b], 1)

                split_hi("S", 0, 0, 0)
                def window(w, i):
                    hd = 1 if isB(w) else 0
                    vw = DV if isB(w) else VX
                    v = V[hd]

                    for x in TIMELINE[w]:
                        if x[0] == "piece":
                            _, l, h, c = x
                            nxt = after(w, i, l, h, 1)
                            if c == 0 and nxt:
                                split_hi(*nxt)
                            if h == 1:
                                evacuate(w, i, l, c)
                            continue
                        name = x[0]
                        n = USE[w].get(name)
                        if name == "rows":
                            act.wait_ge(s_r1, 1)
                            act.activation(TB[0:H, :], TB[0:H, :], ACT.Exp).then_inc(s_r2, 1)
                            act.wait_ge(s_r2, 1)
                            act.activation(TB[0:H, :], TB[0:H, :], ACT.Ln, bias=1.0).then_inc(s_r2, 1)
                        elif name == "rows_exp":
                            act.wait_ge(s_r3, 1)
                            act.activation(rows[32:32 + H, :], TB[0:H, :], ACT.Exp)
                            act.activation(G[32:32 + H, 0, :], VS[0:H, :], ACT.Exp)
                            act.activation(wcr[:, :], me[:, 3, :], ACT.Exp)
                            act.activation(G[64:64 + H, 0, :], TA[0:H, :], ACT.Exp, scale=-1.0).then_inc(s_rows, 1)
                            act.wait_ge(s_rows, 1)
                        elif name in ("silu_q", "silu_k"):
                            m = (0 if w == "S" else i * 2 + 2) + (2 if name[-1] == "k" else 1)
                            act.wait_ge(s_cv, m)
                            act.activation(Z[:, 0:ZO], CV[:, 0:ZO], ACT.Tanh, scale=0.5).then_inc(s_th, 1)
                        elif name in ("vt0", "vt1"):
                            j = int(name[2])
                            dst = V[0 if w in "SB" else 1]
                            for b in range(2):
                                wait_use(act, w, i, n + b)
                                act.activation(dst[:, 4 * b:4 * b + 4, j * P:(j + 1) * P],
                                               RB(n + b)[:, :].rearrange("p (c d) -> p c d", d=P), ACT.Copy).then_inc(free(n + b), 1)
                            wait_use(act, w, i, n + 2)
                            act.activation(dst[0:NS, NC, j * P:(j + 1) * P], RB(n + 2)[0:NS, 0:P], ACT.Copy).then_inc(free(n + 2), 1)
                        elif name == "decay":
                            act.wait_ge(s_warg, i + 1)
                            act.activation(TA[:, 0:SEQ], TA[:, 0:SEQ], ACT.Exp)
                            act.activation(TA[0:NS, SEQ:T], TA[0:NS, SEQ:T], ACT.Exp).then_inc(s_wexp, 1)
                        elif name == "alpha":
                            for b, (c0, m) in enumerate(PARTS):
                                wait_use(act, w, i, n + b)
                                last = act.activation(QD[:, c0:c0 + m], RB(n + b)[:, 0:m], ACT.Copy)
                                last.then_inc(free(n + b), 1)
                            act.wait_ge(s_nab, i + 1)
                            act.activation(TB[:, :], TB[:, :], ACT.Exp).then_inc(s_ln, 1)
                            act.wait_ge(s_ln, i * 2 + 1)
                            act.activation(TB[:, :], TB[:, :], ACT.Ln, bias=1.0).then_inc(s_ln, 1)
                        elif name == "sums":
                            level_exp(act, w, i, 0)
                        elif name.startswith("level"):
                            l = int(name[5:])
                            if l + 1 < NL - 1:
                                level_exp(act, w, i, l + 1)
                            elif l == NL - 1:
                                act.wait_ge(s_d, i * NL + NL)
                                act.activation(TB[:, :], TB[:, :], ACT.Exp, scale=1.0 / TAU)
                                act.activation(TA[:, :], TA[:, :], ACT.Exp, scale=1.0 / TAU).then_inc(s_E, 1)
                        elif name == "keys" and isB(w):
                            for b in range(2):
                                wait_use(act, w, i, n + b)
                                act.activation(KD[:, 512 * b:512 * b + 512], RB(n + b)[:, :], ACT.Copy).then_inc(free(n + b), 1)
                            wait_use(act, w, i, n + 2)
                            act.activation(KD[0:NS, SEQ:SEQ + P], RB(n + 2)[0:NS, 0:P], ACT.Copy).then_inc(free(n + 2), 1)
                        elif name in CHAIN or name == "sample_out":
                            c = CHAIN.index(name) if name in CHAIN else NC
                            u = n + 1 if name in CHAIN else n
                            m = P if c < NC else NS
                            dst = v[:, c, 0:vw] if c < NC else HS[0:NS, 0:vw]
                            wait_use(act, w, i, u)
                            act.activation(dst, RB(u)[0:m, 0:vw], ACT.Copy).then_inc(s_hc, 1)
                            act.wait_ge(s_hc, two(w, i, NT) + (c + 1))
                            act.activation(RB(u)[0:m, 0:DV], RB(u)[0:m, 0:DV], ACT.Square,
                                           accum_out=ssq[0:m, c:c + 1]).then_inc(free(u), 1)
                        elif name == "norm":
                            act.wait_ge(s_ms, BEGUN + two(w, i) + 1)
                            act.activation(ms[:, :], ms[:, :], ACT.Sqrt).then_inc(s_sq, 1)

                def level_exp(act, w, i, l):
                    hs = LEVELS[l]
                    top = T if hs <= SLEN // 2 else SEQ
                    act.wait_ge(s_d, i * NL + (l + 1))
                    e = TB[:, 0:top].rearrange("p (n w) -> p n w", w=2 * hs)
                    act.activation(e[:, :, hs:2 * hs], e[:, :, hs:2 * hs], ACT.Exp, scale=1.0 / TAU)
                    act.activation(e[:, :, 0:hs], e[:, :, 0:hs], ACT.Exp, scale=-1.0 / TAU).then_inc(s_E, 1)
                run(act, None, window)

            @block.gpsimd
            def _(pool):
                st = Steps(pool, s_pool)
                pool.memset(raw[:, 0:2], 0.0).then_inc(s_zero, 1)
                for buf, x in ((cols[:, :, :], 0.0), (G[:, 0, :], 0.0), (me[:, :, :], 0.0), (KD[:, SEQ:T], 0.0), (ssq[:, :], 1.0), (ms[:, :], 1.0)):
                    pool.memset(buf, x)
                pool.memset(den[:, :], 1.0).then_inc(s_init, 1)

                def split_lo(w, i, l, h):
                    _, s, _, before = half(w, i, l, h)
                    r = half(w, i, l, h)[0]
                    pool.wait_ge(s_hi, before + 1)
                    wait(pool, s_used, before - (SPL - 1))
                    pool.tensor_tensor(Wl[:, s], raw[:, r], Wh[:, s].bitcast(F32), ALU.subtract).then_inc(s_lo, 1)
                pool.nop().then_inc(s_sum, BEGUN)
                split_lo("S", 0, 0, 0)

                def window(w, i):
                    hd = 1 if isB(w) else 0
                    for x in TIMELINE[w]:
                        if x[0] == "piece":
                            _, l, h, c = x
                            nxt = after(w, i, l, h, 1)
                            if c == 0 and nxt:
                                split_lo(*nxt)
                            continue
                        name = x[0]
                        n = USE[w].get(name)
                        if name.startswith("level") and int(name[5:]) < NL - 1:
                            l = int(name[5:])
                            if l == 0:
                                wait_use(pool, "A", i, USE["A"]["alpha"])
                                apart(pool)
                                pool.memset(AT[:, :], 0.0).then_inc(s_at0, 1)
                            else:
                                wait_use(pool, w, i, n - 1)
                            pool.wait_ge(s_E, i * NL + (l + 1))
                            top = T if LEVELS[l] <= SLEN // 2 else SEQ
                            pool.tensor_tensor(halves(KD[:, 0:top], l, 0), halves(K[1][:, 0:top], l, 0), halves(TB[:, 0:top], l, 0),
                                               ALU.mult).then_inc(s_ke, 1)
                        elif name == "masked":
                            wait_read(pool, w, i, "keys")
                            if isB(w):
                                pool.wait_ge(s_qd, i + 1)
                            else:
                                wait_read(pool, w, i, "interq")
                            pool.tensor_tensor(QM[:, :, :], mid(QD[:, SEQ:T], NSEQ), g.seqrow[:, :, :], ALU.mult)
                            pool.tensor_tensor(TB[0:NS, 0:SEQ].rearrange("p (b d) -> p b d", b=NSEQ), mid(KD[0:NS, SEQ:SEQ + P], NSEQ),
                                               bc(g.seqcol[:, :].unsqueeze(2), P), ALU.mult).then_inc(s_km, 1)
                        elif name in ("turn0", "turn1") and isB(w):
                            j = int(name[4])
                            wait_read(pool, w, i, name)
                            pool.tensor_tensor(M[:, j, :], M[:, j, :], G[:, j, :], ALU.add).then_inc(s_sum, 1)
                run(pool, None, window)

            @block.vector
            def _(dve):
                per = g.dve_per
                st = Steps(dve, s_dve, per=per)
                dve.nop().then_inc(s_ms, BEGUN)
                dve.nop().then_inc(s_gate, BEGUN)
                link, did = st.link, st.did

                def conv(kt):
                    z = Z[:, ZP:ZN].rearrange("p (b t) -> p b t", t=ZS)
                    dve.memset(Z[:, 0:W4 - 1], 0.0)
                    dve.tensor_copy(z[:, :, 0:W4 - 1], g.sconvT[:, bass.ds(kt, 1), :].rearrange("p k (b j) -> p (k b) j", j=W4 - 1))
                    dve.tensor_copy(g.pk[:, bass.ds(kt, 1), 0:W4 - 1].rearrange("p k j -> p (k j)"), Z[:, SEQ:ZP])
                    link(dve.tensor_copy(g.pk[:, bass.ds(kt, 1), W4 - 1:KEEP].rearrange("p k (b j) -> p (k b) j", j=W4 - 1),
                                         z[:, :, SLEN:ZS]))
                    col = lambda v: g.vec[:, bass.ds(v + kt, 1)]
                    link(dve.tensor_scalar(CV[:, 0:ZO], Z[:, 0:ZO], col(V_CW), col(V_CB), ALU.mult, ALU.add))
                    did(dve.scalar_tensor_tensor(CV[:, 0:ZO], Z[:, 1:1 + ZO], col(V_CW + KC), CV[:, 0:ZO], ALU.mult, ALU.add))

                def taps(kt):
                    col = lambda v: g.vec[:, bass.ds(v + kt, 1)]
                    dve.wait_ge(s_dve, st.value())
                    link(dve.scalar_tensor_tensor(CV[:, 0:ZO], Z[:, 2:2 + ZO], col(V_CW + 2 * KC), CV[:, 0:ZO], ALU.mult, ALU.add))
                    dve.scalar_tensor_tensor(CV[:, 0:ZO], Z[:, 3:3 + ZO], col(V_CW + 3 * KC), CV[:, 0:ZO], ALU.mult, ALU.add).then_inc(s_cv, 1)

                def silu(m, dst, f):
                    dve.wait_ge(s_th, m)
                    link(dve.tensor_scalar(Z[:, 0:ZO], Z[:, 0:ZO], 1.0, 0.5 * f, ALU.add, ALU.mult))
                    dve.tensor_tensor(dst[:, 0:SEQ], Z[:, 0:SEQ], CV[:, 0:SEQ], ALU.mult)
                    tail = lambda v: v[:, ZP:ZN].rearrange("p (b t) -> p b t", t=ZS)[:, :, 0:SLEN]
                    dve.tensor_tensor(seqs(dst), tail(Z), tail(CV), ALU.mult).then_inc(s_silu, 1)

                def window(w, i):
                    hd = 1 if isB(w) else 0
                    vw = DV if isB(w) else VX
                    q, k, v = Q[hd], K[hd], V[hd]
                    if w == "A":
                        st.turn(i)
                    for x in TIMELINE[w]:
                        if x[0] == "piece":
                            continue
                        name = x[0]
                        n = USE[w].get(name)
                        if name == "rows":
                            rows_stage()
                        elif name == "rows_t":
                            for b in range(2):
                                wait_use(dve, w, i, n + b)
                                src = RB(n + b)[:, :].rearrange("p (c r) -> p c r", r=P)
                                for r in range(3):
                                    ins = dve.tensor_copy(cols[:, 4 * b:4 * b + 4, r * H:(r + 1) * H], src[:, :, 32 * r:32 * r + H])
                                ins.then_inc(free(n + b), 1)
                            wait_use(dve, w, i, n + 2)
                            for r in range(3):
                                ins = dve.tensor_copy(cols[0:NS, NC, r * H:(r + 1) * H], RB(n + 2)[0:NS, 32 * r:32 * r + H])
                            ins.then_inc(free(n + 2), 1)
                            dve.wait_ge(free(n + 2), 1)
                        elif name in ("conv_q", "conv_k"):
                            wait_evacuated(dve, w, i, TILES[w].index(name[-1]))
                            conv((4 if name[-1] == "k" else 0) + (0 if w == "S" else i + 1))
                        elif name in ("taps_q", "taps_k"):
                            taps((4 if name[-1] == "k" else 0) + (0 if w == "S" else i + 1))
                        elif name in ("silu_q", "silu_k"):
                            isk = name[-1] == "k"
                            m = (0 if w == "S" else i * 2 + 2) + (2 if isk else 1)
                            silu(m, (K if isk else Q)[0], 1.0 if isk else QSCALE)
                        elif name == "select":
                            one = g.ident[0:H, bass.ds(i, 1)]
                            dve.tensor_scalar(TB[0:H, :], rows[0:H, :], one, None, ALU.mult)
                            dve.tensor_scalar(TB[32:32 + H, :], rows[32:32 + H, :], g.ident[32:32 + H, bass.ds(i + 32, 1)], None, ALU.mult)
                            dve.tensor_copy(walh[64:64 + RANK, :], wal[64:64 + RANK, bass.ds(i * DK, DK)]).then_inc(s_wah, 1)
                            dve.tensor_scalar(wcs[:, :], wcr[:, :], one, None, ALU.mult).then_inc(s_sel, 1)
                            link(dve.tensor_copy(hcol[:, :, :], cols[:, :, :].rearrange("p c (q h) -> p c q h", h=H)[:, :, :, bass.ds(i, 1)]
                                                 .rearrange("p c q h -> p c (q h)")))
                        elif name == "decay":
                            for b in range(2):
                                wait_use(dve, w, i, n + b)
                                for c in range(4 * b, 4 * b + 4):
                                    ins = dve.scalar_tensor_tensor(TA[:, c * P:(c + 1) * P], RB(n + b)[:, (c % 4) * P:(c % 4 + 1) * P],
                                                                   hcol[:, c, 0:1], g.cmask[:, :], ALU.add, ALU.min)
                                ins.then_inc(free(n + b), 1)
                            wait_use(dve, w, i, n + 2)
                            dve.scalar_tensor_tensor(TA[0:NS, SEQ:T], RB(n + 2)[0:NS, 0:NS], hcol[0:NS, NC, 0:1], g.cmask_s[:, :],
                                                     ALU.add, ALU.min).then_inc(s_warg, 1)
                            dve.tensor_copy(sdec[:, :], RB(n + 2)[:, NS:NS + 2 * NC]).then_inc(free(n + 2), 1)
                        elif name == "scores":
                            dve.wait_ge(s_wexp, i + 1)
                            for b in range(2):
                                wait_use(dve, w, i, n + b)
                                dve.tensor_tensor(AT[:, 512 * b:512 * b + 512], RB(n + b)[:, :], TA[:, 512 * b:512 * b + 512],
                                                  ALU.mult).then_inc(free(n + b), 1)
                            wait_use(dve, w, i, n + 2)
                            dve.tensor_tensor(AT[0:NS, SEQ:T], RB(n + 2)[0:NS, 0:NS], TA[0:NS, SEQ:T], ALU.mult).then_inc(free(n + 2), 1)
                        elif name == "interq":
                            did(dve.memset(V[0][:, :, DV:VX], 1.0))
                            did(dve.tensor_copy(ST[:, :, DV:VX], g.n0T[:, :].rearrange("p (b h) -> p b h", h=H)[:, :, bass.ds(i, 1)]))
                            for b, (c0, m) in enumerate(PARTS):
                                wait_use(dve, w, i, n + b)
                                dve.tensor_tensor(QD[:, c0:c0 + m], RB(n + b)[:, 0:m], q[:, c0:c0 + m], ALU.mult).then_inc(free(n + b), 1)
                        elif name == "keys" and not isB(w):
                            for b in range(2):
                                wait_use(dve, w, i, n + b)
                                dve.tensor_tensor(KD[:, 512 * b:512 * b + 512].rearrange("p (c d) -> p c d", d=P),
                                                  RB(n + b)[:, :].rearrange("p (c d) -> p c d", d=P),
                                                  bc(hcol[:, 4 * b:4 * b + 4, 1:2], P), ALU.mult).then_inc(free(n + b), 1)
                            wait_use(dve, w, i, n + 2)
                            dve.tensor_scalar(KD[0:NS, SEQ:SEQ + P], RB(n + 2)[0:NS, 0:P], hcol[0:NS, NC, 1:2], None,
                                              ALU.mult).then_inc(free(n + 2), 1)
                        elif name == "alpha":
                            wait_read(dve, w, i, "alpha")
                            link(dve.tensor_scalar(QD[:, :], QD[:, :], g.vec[:, bass.ds(V_AL + i, 1)], None, ALU.add))
                            dve.scalar_tensor_tensor(TB[:, :], QD[:, :], -1.0, QD[:, :], ALU.mult, ALU.min).then_inc(s_nab, 1)
                        elif name == "sums":
                            dve.wait_ge(s_ln, i * 2 + 2)
                            link(dve.scalar_tensor_tensor(TB[:, :], QD[:, :], 0.0, TB[:, :], ALU.min, ALU.subtract))
                            link(dve.tensor_tensor_scan(TA[:, :], g.reset[:, :], TB[:, :], 0.0, ALU.mult, ALU.add))
                            level_diff(0, i)
                        elif name.startswith("level"):
                            l = int(name[5:])
                            if l < NL - 1:
                                top = T if LEVELS[l] <= SLEN // 2 else SEQ
                                dve.wait_ge(s_E, i * NL + (l + 1))
                                dve.tensor_tensor(halves(QD[:, 0:top], l, 1), halves(q[:, 0:top], l, 1), halves(TB[:, 0:top], l, 1),
                                                  ALU.mult).then_inc(s_qe, 1)
                                dve.wait_ge(s_qe, i * (NL - 1) + (l + 1))
                                dve.wait_ge(s_ke, i * (NL - 1) + (l + 1))
                                if l < NL - 2:
                                    level_diff(l + 1, i)
                                else:
                                    e, b = chunks(TB), chunks(TA)
                                    did(dve.tensor_tensor(e, bc(b[:, :, P - 1:P], P), b, ALU.subtract))
                                    e, b = seqs(TB), seqs(TA)
                                    dve.tensor_tensor(e, bc(b[:, :, SLEN - 1:SLEN], SLEN), b, ALU.subtract).then_inc(s_d, 1)
                            if l == 0:
                                dve.wait_ge(s_at0, i + 1)
                            if l < NL - 1:
                                hs = LEVELS[l]
                                right = halves(g.lmask[:, l, :], l, 1).unsqueeze(1).to_broadcast([P, NC, HP // hs, hs])
                                wait_use(dve, w, i, n)
                                apart(dve)
                                dve.copy_predicated(AT[:, 0:SEQ].rearrange("p (c n w) -> p c n w", c=NC, w=2 * hs)[:, :, :, hs:2 * hs], right,
                                                    RB(n)[:, :].rearrange("p (c n w) -> p c n w", c=NC, w=hs)).then_inc(free(n), 1)
                            else:
                                c4 = lambda v: v.rearrange("p (c t) -> p c t", t=P)
                                for b in range(2):
                                    wait_use(dve, w, i, n + b)
                                    apart(dve)
                                    dve.copy_predicated(c4(AT[:, 512 * b:512 * b + 512]), mid(g.lmask[:, l, :], 4),
                                                        c4(RB(n + b)[:, :])).then_inc(free(n + b), 1)
                            if l >= NL - 3:
                                m = n + USES[name] - 1
                                wait_use(dve, w, i, m)
                                apart(dve)
                                dve.copy_predicated(AT[0:NS, SEQ:T], g.lmask[0:NS, l, 0:NS], RB(m)[0:NS, 0:NS]).then_inc(free(m), 1)
                            wait_read(dve, w, i, name)
                            if l == NL - 1:
                                dve.wait_ge(s_E, i * NL + NL)
                                dve.tensor_tensor(TB[:, :], k[:, :], TB[:, :], ALU.mult).then_inc(s_kt, 1)
                                did(dve.tensor_copy(sdec[:, 0:NC], chunks(TA)[:, :, P - 1:P].rearrange("p c t -> p (c t)")))
                                did(dve.tensor_copy(sdec[:, NC:2 * NC], seqs(TA)[:, :, SLEN - 1:SLEN].rearrange("p c t -> p (c t)")))
                                dve.tensor_tensor(QD[:, :], q[:, :], TA[:, :], ALU.mult).then_inc(s_qd, 1)
                        elif name in CHAIN:
                            c = CHAIN.index(name)
                            wait_use(dve, w, i, n)
                            if c == 0:
                                ins = dve.tensor_copy(SS[:, 0, 0:vw], RB(n)[:, 0:vw])
                            else:
                                wait_read_use(dve, w, i, USE[w][CHAIN[c - 1]])
                                if c == 1:
                                    dve.wait_ge(s_sts, BEGUN + two(w, i, 32))
                                ins = dve.scalar_tensor_tensor(SS[:, c % 2, 0:vw], SS[:, (c - 1) % 2, 0:vw], sdec[:, c:c + 1],
                                                               RB(n)[:, 0:vw], ALU.mult, ALU.add)
                            ins.then_inc(free(n), 1)
                            if c == NC - 1 and not isB(w):
                                wait_read_use(dve, w, i, n)
                                did(dve.tensor_copy(g.nout[:, bass.ds(i, 1)], SS[:, 1, DV:VX]))
                        elif name in SAMPLE:
                            b = SAMPLE.index(name)
                            wait_use(dve, w, i, n)
                            if b == 0:
                                dve.wait_ge(s_stl, two(w, i, 16) + 16)
                            dve.scalar_tensor_tensor(ST[:, b, 0:vw], ST[:, b, 0:vw], sdec[:, NC + b:NC + b + 1], RB(n)[:, 0:vw],
                                                     ALU.mult, ALU.add).then_inc(free(n), 1)
                            if b == NSEQ - 1 and not isB(w):
                                wait_read_use(dve, w, i, n)
                                did(dve.tensor_copy(g.nout[:, H:].rearrange("p (b h) -> p b h", h=H)[:, :, bass.ds(i, 1)], ST[:, :, DV:VX]))
                        elif name == "norm":
                            wait_read(dve, w, i, "sample_out")
                            if not isB(w):
                                d = v[:, 0:NC, DV:VX].rearrange("p c o -> p (c o)")
                                did(dve.scalar_tensor_tensor(den[:, 0:NC], d, -1.0, d, ALU.mult, ALU.max))
                                d = HS[0:NS, DV:VX]
                                link(dve.scalar_tensor_tensor(den[0:NS, NC:NT], d, -1.0, d, ALU.mult, ALU.max))
                                link(dve.tensor_tensor(den[:, :], den[:, :], hcol[:, :, 2:3].rearrange("p c o -> p (c o)"), ALU.max))
                                link(dve.reciprocal(den[:, :], den[:, :]))
                                link(dve.tensor_tensor(ms[:, :], ssq[:, :], den[:, :], ALU.mult))
                                link(dve.tensor_tensor(ms[:, :], ms[:, :], den[:, :], ALU.mult))
                                dve.tensor_scalar(ms[:, :], ms[:, :], 1.0 / DV, EPS, ALU.mult, ALU.add).then_inc(s_ms, 1)
                            else:
                                dve.tensor_scalar(ms[:, :], ssq[:, :], 1.0 / DV, EPS, ALU.mult, ALU.add).then_inc(s_ms, 1)
                            dve.wait_ge(s_sq, two(w, i) + 1)
                            link(dve.reciprocal(scl[:, :], ms[:, :]))
                            if not isB(w):
                                link(dve.tensor_tensor(scl[:, :], scl[:, :], den[:, :], ALU.mult))
                            dve.tensor_tensor(v[:, 0:NC, 0:DV], v[:, 0:NC, 0:DV], bc(scl[:, 0:NC].unsqueeze(2), DV), ALU.mult)
                            dve.tensor_scalar(HS[0:NS, 0:DV], HS[0:NS, 0:DV], scl[0:NS, NC:NT], None, ALU.mult).then_inc(s_hn, 1)
                        elif name in ("gate_r0", "gate_r1"):
                            j = int(name[-1])
                            wait_evacuated(dve, w, i, TILES[w].index(f"o{j}"))
                            dve.scalar_tensor_tensor(G[:, j, :], G[:, j, :], 1.0, TG[:, :], ALU.add, ALU.mult).then_inc(s_gr, 1)
                        elif name in ("gate0", "gate1"):
                            j = int(name[-1])
                            wait_evacuated(dve, w, i, TILES[w].index(f"g{j}"))
                            gain = g.vec[:, bass.ds(i * 2 + ((V_HB if isB(w) else V_HA) + j), 1)]
                            link(dve.tensor_scalar(TG[:, :], TG[:, :], 1.0, gain, ALU.add, ALU.mult))
                            if isB(w):
                                dve.wait_ge(s_gr, i * 2 + (j + 1))
                                ins = dve.tensor_tensor(G[:, j, :], G[:, j, :], TG[:, :], ALU.mult)
                            else:
                                ins = dve.scalar_tensor_tensor(G[:, j, :], G[:, j, :], 1.0, TG[:, :], ALU.add, ALU.mult)
                            ins.then_inc(s_gate, 1)
                        elif name in ("turn0", "turn1"):
                            j = int(name[-1])
                            dve.wait_ge(s_gate, BEGUN + two(w, i, 2) + (j + 1))
                            if not isB(w) and j == 0:
                                dve.wait_ge(s_mst, BEGUN + i * 16)
                            for b, (c0, m) in enumerate(PARTS):
                                wait_use(dve, w, i, n + b)
                                dst = G if isB(w) else M
                                dve.tensor_tensor(dst[:, j, c0:c0 + m], RB(n + b)[:, 0:m], G[:, j, c0:c0 + m], ALU.mult).then_inc(free(n + b), 1)
                        elif name.startswith("ada") and name[3] != "_":
                            m = two(w, i, 4) + (int(name[3]) + 2 * KC)
                            wait_use(dve, w, i, n)
                            dve.tensor_scalar(g.ada[:, bass.ds(m, 1), :].rearrange("p o c -> p (o c)"), RB(n)[:, 0:NCOND],
                                              g.vec[:, bass.ds(m, 1)], None, ALU.add).then_inc(free(n), 1)
                    if per and w == "B" and st.n != per:
                        raise ValueError(f"set dve_per to {st.n}")

                def level_diff(l, i):
                    hs = LEVELS[l]
                    top = T if hs <= SLEN // 2 else SEQ
                    b = TA[:, 0:top].rearrange("p (n w) -> p n w", w=2 * hs)
                    dve.tensor_tensor(TB[:, 0:top].rearrange("p (n w) -> p n w", w=2 * hs), b, bc(b[:, :, hs - 1:hs], 2 * hs),
                                      ALU.subtract).then_inc(s_d, 1)

                def rows_stage():
                    I, X, LF, B_, MM = M[0:H, 0, :], M[0:H, 1, :], AT[0:H, :], QD[0:H, :], TA[0:H, :]
                    wait_evacuated(dve, "S", 0, 0)
                    dve.wait_ge(s_small, 64)
                    dve.wait_ge(s_init, 1)
                    did(dve.tensor_scalar(I, I, bif[:, 0:1], None, ALU.add))
                    link(dve.tensor_scalar(X, X, bif[:, 1:2], None, ALU.add))
                    dve.scalar_tensor_tensor(TB[0:H, :], X, -1.0, X, ALU.mult, ALU.min).then_inc(s_r1, 1)
                    dve.wait_ge(s_r2, 2)
                    link(dve.scalar_tensor_tensor(LF, X, 0.0, TB[0:H, :], ALU.min, ALU.subtract))
                    did(dve.tensor_tensor_scan(B_, g.reset[0:H, :], LF, 0.0, ALU.mult, ALU.add))
                    did(dve.tensor_tensor_scan(MM[:, 0:SEQ], LF[:, 0:SEQ], I[:, 0:SEQ], 0.0, ALU.add, ALU.max))
                    for b in range(NSEQ):
                        r = slice(SEQ + b * SLEN, SEQ + (b + 1) * SLEN)
                        did(dve.tensor_tensor_scan(MM[:, r], LF[:, r], I[:, r], m0[:, b:b + 1], ALU.add, ALU.max))
                    dve.wait_ge(s_dve, st.value())
                    ends = lambda v: (chunks(v)[:, :, P - 1:P].rearrange("p c t -> p (c t)"), seqs(v)[:, :, SLEN - 1:SLEN].rearrange("p c t -> p (c t)"))
                    for r, v in ((1, MM), (2, B_)):
                        for j, e in enumerate(ends(v)):
                            did(dve.tensor_copy(me[:, r, j * NC:(j + 1) * NC], e))
                    did(dve.tensor_copy(me[:, 0, NC:2 * NC], m0[:, :]))
                    dve.wait_ge(s_dve, st.value())
                    did(dve.tensor_copy(me[:, 0, 1:NC], me[:, 1, 0:NC - 1]))
                    did(dve.tensor_tensor(me[:, 3, :], me[:, 2, :], me[:, 1, :], ALU.subtract))
                    did(dve.tensor_tensor(rows[0:H, :], B_, MM, ALU.subtract))
                    did(dve.tensor_tensor(G[0:H, 0, :], I, B_, ALU.subtract))
                    dve.wait_ge(s_dve, st.value())
                    for f, col in ((chunks, slice(0, NC)), (seqs, slice(NC, 2 * NC))):
                        m = P if f is chunks else SLEN
                        did(dve.tensor_tensor(f(TB[0:H, :]), f(rows[0:H, :]), bc(me[:, 0, col].unsqueeze(2), m), ALU.add))
                        did(dve.tensor_tensor(f(VS[0:H, :]), f(G[0:H, 0, :]), bc(me[:, 3, col].unsqueeze(2), m), ALU.add))
                    dve.wait_ge(s_dve, st.value())
                    dve.tensor_tensor(me[:, 3, :], me[:, 3, :], me[:, 0, :], ALU.add).then_inc(s_r3, 1)
                run(dve, None, window)


NBLK = FT // 2


def ffn_phase(nc, g, a, loops=True):
    with ExitStack() as ctx:
        sb = lambda n, s, d=F32: ctx.enter_context(nc.sbuf_tensor(n, s, d))
        sem = lambda n: ctx.enter_context(nc.semaphore(n))
        RING = 4
        raw = sb("f_raw", [P, RING, 4, P])
        Wh = sb("f_hi", [P, RING, 4, P], F32R)
        Wl = sb("f_lo", [P, RING, 4, P], F32R)
        X = sb("x_t", [P, KC, T])
        NXR = 4
        XR = sb("x_tile", [P, NXR, D])
        SQ = sb("squares", [P, T])
        SQT = sb("square", [P, T])
        TH = sb("ffn_tanh", [P, T])
        SG = sb("ffn_silu", [P, T])
        AC = sb("ffn_act", [P, T])
        Ah = sb("act_hi", [P, 2, 2, T], F32R)
        Al = sb("act_lo", [P, 2, 2, T], F32R)
        small = sb("norm_small", [P, 4, NT])
        am = sb("norm2_mult", [P, KC, NCOND])
        stm = sb("sample_temp", [P, NS])
        co = AC[0:KEEP, 0:D]
        stn = sb("n_rows_out", [H * NCOND, P])
        fss = sb("final_small", [P, NT, 4])
        OT, GF = XR, SQT

        def mixed(m):
            return (Ah, Al)[m // 4][:, m // 2 % 2, m % 2, :]

        s_w = [sem(f"f_w_loaded{n}") for n in range(RING)]
        s_hi, s_lo, s_used = sem("f_hi_made"), sem("f_lo_made"), sem("f_used")
        s_piece = sem("f_pieces_full")
        s_pf = [sem(f"f_bank_free{n}") for n in range(4)]
        s_ml, s_xl = [sem(f"mix_loaded{m}") for m in range(KC)], [sem(f"x_row_loaded{m}") for m in range(NXR)]
        s_mh, s_mlo, s_mlv = sem("mix_hi"), sem("mix_lo"), sem("mix_lo_by_vector")
        s_xt, s_xe = sem("x_turned"), [sem("x_taken_by_vector"), sem("x_taken_by_scalar")]
        s_sq, s_sum, s_ms, s_rt, s_rd, s_rb = sem("squares_summed"), sem("norm2_sums"), sem("norm2_ms"), sem("norm2_sqrt"), sem("norm2_rows"), sem("norm2_bcast")
        s_sql, s_row, s_rowc = sem("last_squares"), sem("norm2_row"), sem("norm2_row_copied")
        s_h, s_hh, s_hl = sem("h2_ready"), sem("h2_hi"), sem("h2_lo")
        s_th, s_ah, s_al = sem("tanh_ready"), sem("act_hi_made"), sem("act_lo_made")
        s_co, s_cc, s_out = sem("states_turned"), sem("states_copied"), sem("stored")
        s_gf = sem("final_gain")
        s_y = [sem(f"y_stored{m}") for m in range(NXR)]
        s_stm = sem("samples_gated")
        s_ft, s_fs, s_fm, s_fr, s_fo = sem("final_turned"), sem("final_ssq"), sem("final_ms"), sem("final_sqrt"), sem("final_rows")
        s_dve, s_pool = sem("f_dve_chain"), sem("f_pool_chain")

        w_out = a["w_out"][0].rearrange("(k p) n -> p k n", p=P)
        w_gate = a["w_ffn_gate"][0].rearrange("(k p) n -> p k n", p=P)
        w_up = a["w_ffn_up"][0].rearrange("(k p) n -> p k n", p=P)
        w_down = a["w_ffn_down"][0]
        LOOP = (NBLK - 1) // 2

        HALVES = {"out": 2, "proj": 8, "down": 4}
        PIECES = {"out": 3, "proj": 12, "down": 24}
        SIGNAL = {"out": 2, "proj": 8, "down": 22}

        class Place:
            def __init__(self, j, steps_before, in_turn):
                tot = lambda d, names: sum(d[x] for x in names)
                pre = ["out"] * KC + ["proj"]
                turn = ["proj", "down"] * 2
                n = lambda d: (tot(d, turn), tot(d, (pre if in_turn is not None else steps_before)) + tot(d, turn[:in_turn or 0]))
                self.j = j
                self.halves, self.pieces, self.fulls = n(HALVES), n(PIECES), n(SIGNAL)

            def half(self, k):
                per, base = self.halves
                s, turns = static(self.j, per, base + k, RING)
                return s, turns, self.j * per + (base + k)

            def piece(self, k):
                per, base = self.pieces
                return static(self.j, per, base + k, 4)

            def full(self, k):
                per, base = self.fulls
                return self.j * per + (base + k)

        def out_place(n):
            return Place(0, ["out"] * n, None)

        def run(engine, step):
            for n in range(KC):
                step("out", n, 0, out_place(n))
            step("norm2", 0, 0, None)
            step("proj", 0, 0, Place(0, ["out"] * KC, None))

            def turn(j):
                step("proj", j * 2 + 1, 1, Place(j, None, 0))
                step("down", j * 2, 0, Place(j, None, 1))
                step("proj", j * 2 + 2, 0, Place(j, None, 2))
                step("down", j * 2 + 1, 1, Place(j, None, 3))
            if loops:
                with engine.Fori(0, LOOP) as j:
                    turn(j)
            else:
                for j in range(LOOP):
                    turn(j)
            step("down", NBLK - 1, 0, Place(LOOP, None, 0))

        def source(kind, b, k):
            if kind == "out":
                return w_out[:, 4 * k:4 * k + 4, bass.ds(b * P, P)]
            if kind == "proj":
                t, h = k // 2, k % 2
                src = w_gate if t % 2 == 0 else w_up
                return src[:, 4 * h:4 * h + 4, bass.ds(b * (2 * P) + (t // 2) * P, P)]
            n0, f = k // 2, k % 2
            rows = w_down[bass.ds(b * (2 * P) + f * P, P), 512 * n0:512 * n0 + 512]
            return rows.rearrange("p (n c) -> p n c", c=P)

        def span(c):
            return c * PC, PC

        def ahead(split, pl, t):
            for k in (2 * t, 2 * t + 1):
                split(pl, k)

        def is_last(b):
            return isinstance(b, int) and b == NBLK - 1

        def wait_full(e, kind, pl, k):
            if kind == "down":
                nh, r = k // 12, k % 12
                if r == 11:
                    e.wait_ge(s_used, pl.half(2 * nh + 1)[2] + 1)
                else:
                    e.wait_ge(s_piece, pl.full(11 * nh + r) + 1)
            else:
                t, c = k // 3, k % 3
                if c == 2:
                    e.wait_ge(s_used, pl.half(2 * t + 1)[2] + 1)
                else:
                    e.wait_ge(s_piece, pl.full(2 * t + c) + 1)

        MISC = g.ps[4:8]

        def turned_x(t, b):
            n = P if t < NC else NS
            return MISC[(2 * t + b) % 4][:, :].rearrange("p (k t) -> p k t", t=P)[:, :, 0:n]
        ENDB = g.ps[4:8] + g.ps[0:4]
        NE = len(ENDB) // 2
        PARTS = [(0, 512), (512, 512), (SEQ, NS)]
        seqv = lambda v: v.rearrange("p (b t) -> p b t", t=SLEN)

        with nc.Block() as block:

            @block.sync
            def _(sp):
                def load_x(t):
                    n = P if t < NC else NS
                    src = a["x_prompt"][0, t * P:(t + 1) * P, :] if t < NC else a["x_sample"].rearrange("b t d -> (b t) d")
                    sp.dma_start(XR[0:n, t % NXR, :], src).then_inc(s_xl[t % NXR], 16)
                for k in range(2):
                    sp.dma_start(raw[:, k], source("out", 0, k)).then_inc(s_w[k], 16)
                for m in range(NXR):
                    load_x(m)
                    sp.dma_start(mixed(m).bitcast(F32), g.mix_d[:, m, :]).then_inc(s_ml[m], 16)
                for m in range(NXR, KC):
                    sp.dma_start(mixed(m).bitcast(F32), g.mix_d[:, m, :]).then_inc(s_ml[m], 16)
                for t in range(NXR, NT):
                    sp.wait_ge(s_xt, 2 * (t - NXR + 1))
                    load_x(t)

                def step(kind, b, par, pl):
                    if kind == "norm2":
                        return
                    if kind == "out" and b == 1:
                        sp.wait_ge(s_cc, 2)
                        sp.dma_start(a["conv_p"].rearrange("o b j c -> (o b j) c"), co[0:W4 - 1, :]).then_inc(s_out, 16)
                        sp.dma_start(a["conv_s"].rearrange("o b j c -> (o b j) c"), co[W4 - 1:KEEP, :]).then_inc(s_out, 16)
                        sp.dma_start(a["n_p"].rearrange("o b h d -> (o b h) d"), stn[0:H, :]).then_inc(s_out, 16)
                        sp.dma_start(a["n_s"].rearrange("o b h d -> (o b h) d"), stn[H:H * NCOND, :]).then_inc(s_out, 16)
                    for k in range(HALVES[kind]):
                        if kind == "out" and b == 0:
                            continue
                        s, turns, before = pl.half(k)
                        wait(sp, s_lo, before - (RING - 1))
                        sp.dma_start(raw[:, s], source(kind, b, k)).then_inc(s_w[s], 16)
                run(sp, step)
                gf = a["g_final"].unsqueeze(0).to_broadcast([P, D])
                sp.wait_ge(s_hl, KC)
                sp.dma_start(GF[:, 0:D], gf).then_inc(s_gf, 16)
                for t in range(NT):
                    sp.wait_ge(s_fo, t + 1)
                    if t < NC:
                        sp.dma_start(a["y_prompt"][0, t * P:(t + 1) * P, :], OT[:, t % NXR, 0:D]).then_inc(s_y[t % NXR], 16)
                    else:
                        sp.dma_start(a["y_sample"].rearrange("b t d -> (b t) d"), OT[0:NS, t % NXR, 0:D]).then_inc(s_y[t % NXR], 16)
                sp.wait_ge(s_out, 16 * 4)
                for m in range(NXR):
                    sp.wait_ge(s_y[m], 16 * len(range(m, NT, NXR)))

            @block.tensor
            def _(pe):
                def tile3(pl, t, mix=False, first=False):
                    for h in range(2):
                        s, _, before = pl.half(2 * t + h)
                        pe.wait_ge(s_lo, before + 1)
                        if mix:
                            pe.wait_ge(s_mlo, len([m for m in range(4 * h + 4) if m % 3 != 1]))
                            pe.wait_ge(s_mlv, len([m for m in range(4 * h + 4) if m % 3 == 1]))
                        if first:
                            pe.wait_ge(s_hl, 4 * h + 4)
                        for c in range(NPC):
                            bnk, turns = pl.piece(3 * t + c)
                            if h == 0:
                                wait(pe, s_pf[bnk], turns)
                            c0, n = span(c)
                            for kk in range(4):
                                for m, (x, y) in enumerate(((Wh, g.Hh), (Wh, g.Hl), (Wl, g.Hh))):
                                    last = pe.matmul(g.ps[bnk][:, 0:n], x[:, s, kk, :], y[:, 4 * h + kk, c0:c0 + n],
                                                     start=(h == 0 and kk == 0 and m == 0), stop=(h == 1 and kk == 3 and m == 2))
                            if c == NPC - 1:
                                last.then_inc(s_used, 1)
                            elif h == 1:
                                last.then_inc(s_piece, 1)

                def step(kind, b, par, pl):
                    if kind == "out":
                        tile3(pl, 0, mix=(b == 0))
                    elif kind == "proj":
                        for t in range(4):
                            tile3(pl, t, first=(t == 0 and isinstance(b, int) and b == 0))
                    elif kind == "down":
                        pe.wait_ge(s_al, b * 6 + 6)
                        for nh in range(2):
                            sl = []
                            for f in range(2):
                                s, _, before = pl.half(2 * nh + f)
                                pe.wait_ge(s_lo, before + 1)
                                sl.append(s)
                            for r in range(12):
                                n, c = r // 3, r % 3
                                bnk, turns = pl.piece(12 * nh + r)
                                wait(pe, s_pf[bnk], turns)
                                c0, w = span(c)
                                for f in range(2):
                                    for m, (x, y) in enumerate(((Wh, Ah), (Wh, Al), (Wl, Ah))):
                                        last = pe.matmul(g.ps[bnk][:, 0:w], x[:, sl[f], n, :], y[:, par, f, c0:c0 + w],
                                                         start=(f == 0 and m == 0), stop=(f == 1 and m == 2))
                                if r == 11:
                                    last.then_inc(s_used, 2)
                                else:
                                    last.then_inc(s_piece, 1)
                    elif kind == "norm2":
                        pe.wait_ge(s_sq, KC - 1)
                        pe.wait_ge(s_sql, 1)
                        for b in range(2):
                            pe.wait_ge(s_xe[b], NT)
                        for b, (c0, m) in enumerate(PARTS):
                            pe.matmul(MISC[b][0:1, 0:m], g.ones[:, 0:1], SQ[:, c0:c0 + m], start=True, stop=False)
                            pe.matmul(MISC[b][0:1, 0:m], g.ones[:, 0:1], SG[:, c0:c0 + m], start=False, stop=True).then_inc(s_row, 1)
                        pe.wait_ge(s_rowc, len(PARTS))
                        for t in range(NT):
                            n = P if t < NC else NS
                            last = pe.transpose(MISC[3][0:n, 64 + 2 * t:65 + 2 * t], TH[0:1, t * P:t * P + n], g.ident[0:1, 0:1])
                        last.then_inc(s_sum, 1)
                        pe.wait_ge(s_rd, 1)
                        for b, (c0, m) in enumerate(PARTS):
                            n = P if b < 2 else NS
                            pe.matmul(MISC[b][:, 0:m], g.ones[0:n, :], SQ[0:n, c0:c0 + m], start=True, stop=True).then_inc(s_rb, 1)

                for half_ in range(2):
                    for k in range(4):
                        kk = 4 * half_ + k
                        last = pe.transpose(MISC[half_][0:KEEP, k * P:(k + 1) * P], g.pk[:, kk, :], g.ident[:, :])
                pe.transpose(MISC[2][0:H * NCOND, 0:P], g.nout[:, :], g.ident[:, :]).then_inc(s_co, 1)
                pe.wait_ge(s_cc, 2)
                for t in range(NT):
                    pe.wait_ge(s_xl[t % NXR], 16 * (t // NXR + 1))
                    n = P if t < NC else NS
                    for b in range(2):
                        u = 2 * t + b
                        if u >= 4:
                            pe.wait_ge(s_xe[b], t - 1)
                        for k in range(4):
                            last = pe.transpose(MISC[u % 4][:, k * P:k * P + n], XR[0:n, t % NXR, (4 * b + k) * P:(4 * b + k + 1) * P],
                                                g.ident[0:n, 0:n])
                        last.then_inc(s_xt, 1)
                run(pe, step)
                lastp = Place(LOOP, None, 0)
                bnk, turns = lastp.piece(23)
                pe.wait_ge(s_pf[bnk], turns + 1)
                for t in range(NT):
                    n = P if t < NC else NS
                    for b in range(2):
                        if t >= NE and b == 0:
                            pe.wait_ge(s_fo, t - NE + 1)
                        for k in range(4):
                            last = pe.transpose(ENDB[2 * (t % NE) + b][0:n, k * P:(k + 1) * P], X[:, 4 * b + k, t * P:t * P + n], g.ident[:, :])
                        last.then_inc(s_ft, 1)

            @block.scalar
            def _(act):
                def hi(pl, k):
                    s, turns, before = pl.half(k)
                    act.wait_ge(s_w[s], turns * 16 + 16)
                    wait(act, s_used, before - (RING - 1))
                    act.activation(Wh[:, s], raw[:, s], ACT.Copy).then_inc(s_hi, 1)

                def step(kind, b, par, pl):
                    if kind == "out":
                        ahead(hi, pl, 1)
                    elif kind == "norm2":
                        for b, (c0, m) in enumerate(PARTS):
                            act.wait_ge(s_row, b + 1)
                            act.activation(TH[0:1, c0:c0 + m], MISC[b][0:1, 0:m], ACT.Copy).then_inc(s_rowc, 1)
                        act.wait_ge(s_ms, 1)
                        act.activation(small[:, 1, :], small[:, 0, :], ACT.Sqrt).then_inc(s_rt, 1)
                        for k in range(KC):
                            act.wait_ge(s_h, k + 1)
                            act.activation(g.Hh[:, k, :], (SQT, TH, SG)[k % 3][:, :], ACT.Copy).then_inc(s_hh, 1)
                    elif kind == "proj":
                        for t in range(4):
                            ahead(hi, pl, t + 1)
                            if t % 2:
                                up(b, t // 2, par, pl)
                            else:
                                gate(b, t // 2, pl)
                    else:
                        ahead(hi, pl, 1)
                        if not is_last(b):
                            ahead(hi, pl, 2)

                def gate(b, f, pl):
                    for c in range(NPC):
                        wait_full(act, "proj", pl, 6 * f + c)
                        bnk, _ = pl.piece(6 * f + c)
                        c0, w = span(c)
                        act.activation(TH[:, c0:c0 + w], g.ps[bnk][:, 0:w], ACT.Tanh, scale=0.5).then_inc(s_th, 1)

                def up(b, f, par, pl):
                    for c in range(NPC):
                        bnk, turns = pl.piece(6 * f + 3 + c)
                        act.wait_ge(s_pf[bnk], turns + 1)
                        c0, w = span(c)
                        act.activation(Ah[:, par, f, c0:c0 + w], AC[:, c0:c0 + w], ACT.Copy).then_inc(s_ah, 1)

                ahead(hi, out_place(0), 0)
                for m in range(NT):
                    if m < KC:
                        act.wait_ge(s_ml[m], 16)
                        act.activation(g.Hh[:, m, :], mixed(m).bitcast(F32), ACT.Copy).then_inc(s_mh, 1)
                    n = P if m < NC else NS
                    act.wait_ge(s_xt, 2 * m + 2)
                    act.activation(X[:, 4:8, m * P:m * P + n], turned_x(m, 1), ACT.Copy).then_inc(s_xe[1], 1)
                run(act, step)
                for t in range(NT + 1):
                    n = P if t < NC else NS
                    for b in range(2):
                        if t < NT:
                            act.wait_ge(s_ft, 2 * t + b + 1)
                            if 2 * t + b:
                                act.wait_ge(s_fs, 2 * t + b)
                            act.activation(TH[0:n, 0:512], ENDB[2 * (t % NE) + b][0:n, :], ACT.Square,
                                           accum_out=fss[0:n, t, b:b + 1]).then_inc(s_fs, 1)
                    if t:
                        act.wait_ge(s_fm, t)
                        act.activation(fss[:, t - 1, 2:3], fss[:, t - 1, 2:3], ACT.Sqrt).then_inc(s_fr, 1)

            @block.gpsimd
            def _(pool):
                def lo(pl, k):
                    s, _, before = pl.half(k)
                    pool.wait_ge(s_hi, before + 1)
                    wait(pool, s_used, before - (RING - 1))
                    pool.tensor_tensor(Wl[:, s], raw[:, s], Wh[:, s].bitcast(F32), ALU.subtract).then_inc(s_lo, 1)

                def squares(n):
                    bnk, turns = out_place(n).piece(2)
                    pool.wait_ge(s_pf[bnk], turns + 1)
                    if n == 0:
                        pool.tensor_tensor(SQ[:, :], X[:, 0, :], X[:, 0, :], ALU.mult).then_inc(s_sq, 1)
                    else:
                        pool.wait_ge(s_sq, n)
                        st.link(pool.tensor_tensor(SQT[:, :], X[:, n, :], X[:, n, :], ALU.mult))
                        pool.tensor_tensor(SQ[:, :], SQ[:, :], SQT[:, :], ALU.add).then_inc(s_sq, 1)

                def step(kind, b, par, pl):
                    if kind == "out":
                        ahead(lo, pl, 1)
                        if b:
                            squares(b - 1)
                    elif kind == "norm2":
                        for k in range(KC):
                            pool.wait_ge(s_hh, k + 1)
                            pool.tensor_tensor(g.Hl[:, k, :], (SQT, TH, SG)[k % 3][:, :], g.Hh[:, k, :].bitcast(F32), ALU.subtract).then_inc(s_hl, 1)
                    elif kind == "proj":
                        for t in range(4):
                            ahead(lo, pl, t + 1)
                            if t % 2:
                                n = b * 6 + 3 * (t // 2)
                                for c in range(NPC):
                                    pool.wait_ge(s_ah, n + (c + 1))
                                    c0, w = span(c)
                                    pool.tensor_tensor(Al[:, par, t // 2, c0:c0 + w], AC[:, c0:c0 + w],
                                                       Ah[:, par, t // 2, c0:c0 + w].bitcast(F32), ALU.subtract).then_inc(s_al, 1)
                    else:
                        ahead(lo, pl, 1)
                        if not is_last(b):
                            ahead(lo, pl, 2)
                st = Steps(pool, s_pool)
                ahead(lo, out_place(0), 0)
                for m in range(KC):
                    if m % 3 != 1:
                        pool.wait_ge(s_mh, m + 1)
                        pool.tensor_tensor(g.Hl[:, m, :], mixed(m).bitcast(F32), g.Hh[:, m, :].bitcast(F32), ALU.subtract).then_inc(s_mlo, 1)
                run(pool, step)

            @block.vector
            def _(dve):
                st = Steps(dve, s_dve)
                link, did = st.link, st.did

                def step(kind, b, par, pl):
                    if kind == "out":
                        for c in range(NPC):
                            if c == NPC - 1:
                                samples("out", pl, c, b, 2 * KC, b + 1)
                            add_prompt("out", pl, c, b, c, 2 * KC)
                    elif kind == "norm2":
                        dve.wait_ge(s_stm, 2 * KC)
                        bnk, turns = out_place(KC - 1).piece(NPC - 1)
                        dve.wait_ge(s_pf[bnk], turns + 1)
                        dve.tensor_tensor(SG[:, :], X[:, KC - 1, :], X[:, KC - 1, :], ALU.mult).then_inc(s_sql, 1)
                        dve.wait_ge(s_out, 16 * 4)
                        dve.wait_ge(s_sum, 1)
                        sums = MISC[3][:, 64:64 + 2 * NT].rearrange("p (t o) -> p t o", o=2)
                        dve.tensor_scalar(small[:, 0, 0:NC], sums[:, 0:NC, 0], 1.0 / D, EPS, ALU.mult, ALU.add)
                        dve.tensor_scalar(small[0:NS, 0, NC:NT], sums[0:NS, NC:NT, 0], 1.0 / D, EPS, ALU.mult, ALU.add).then_inc(s_ms, 1)
                        link(dve.scalar_tensor_tensor(am[:, :, :], g.ada[:, 4 * KC:5 * KC, :], 1.0,
                                                      bc(g.vec[:, V_G2:V_G2 + KC].unsqueeze(2), NCOND), ALU.add, ALU.mult))
                        dve.wait_ge(s_rt, 1)
                        link(dve.reciprocal(small[:, 2, :], small[:, 1, :]))
                        did(dve.tensor_tensor(SQ[:, 0:SEQ].rearrange("p (c t) -> p c t", t=P), mid(g.ident[:, :], NC),
                                              bc(small[:, 2, 0:NC].unsqueeze(2), P), ALU.mult))
                        dve.tensor_scalar(SQ[0:NS, SEQ:T], g.ident[0:NS, 0:NS], small[0:NS, 2, NC:NT], None, ALU.mult).then_inc(s_rd, 1)
                        dve.wait_ge(s_rb, len(PARTS))
                        for k in range(KC):
                            t = (SQT, TH, SG)[k % 3]
                            if k >= 3:
                                dve.wait_ge(s_hl, k - 2)
                            for p in range(2):
                                st.did(dve.scalar_tensor_tensor(t[:, 512 * p:512 * p + 512], X[:, k, 512 * p:512 * p + 512], am[:, k, 0:1],
                                                                MISC[p][:, :], ALU.mult, ALU.mult))
                            v = seqv(t[:, SEQ:T])
                            link(dve.tensor_tensor(t[:, SEQ:T], X[:, k, SEQ:T], MISC[2][:, 0:NS], ALU.mult))
                            link(dve.tensor_tensor(v, v, bc(am[:, k, 1:NCOND].unsqueeze(2), SLEN), ALU.mult))
                            dve.tensor_scalar(t[:, 0:SEQ], t[:, 0:SEQ], g.ada[:, 3 * KC + k, 0:1], None, ALU.add)
                            dve.tensor_tensor(v, v, bc(g.ada[:, 3 * KC + k, 1:NCOND].unsqueeze(2), SLEN), ALU.add).then_inc(s_h, 1)
                    elif kind == "proj":
                        for f in range(2):
                            n = b * 6 + 3 * f
                            for c in range(NPC):
                                c0, w = span(c)
                                bnk, _ = pl.piece(6 * f + c)
                                dve.wait_ge(s_th, n + (c + 1))
                                dve.scalar_tensor_tensor(SG[:, c0:c0 + w], TH[:, c0:c0 + w], 1.0, g.ps[bnk][:, 0:w],
                                                         ALU.add, ALU.mult).then_inc(s_pf[bnk], 1)
                            for c in range(NPC):
                                c0, w = span(c)
                                bnk, bt = pl.piece(6 * f + 3 + c)
                                gb, gt = pl.piece(6 * f + c)
                                wait_full(dve, "proj", pl, 6 * f + 3 + c)
                                dve.wait_ge(s_pf[gb], gt + 1)
                                wait(dve, s_al, n - 3 + (c + 1))
                                dve.scalar_tensor_tensor(AC[:, c0:c0 + w], SG[:, c0:c0 + w], 0.5, g.ps[bnk][:, 0:w],
                                                         ALU.mult, ALU.mult).then_inc(s_pf[bnk], 1)
                    else:
                        for k in range(24):
                            n, c = 4 * (k // 12) + k % 12 // 3, k % 3
                            if c == NPC - 1:
                                samples("down", pl, k, n, 5 * KC, b * KC + (KC + n + 1))
                            add_prompt("down", pl, k, n, c, 5 * KC)

                def add_prompt(kind, pl, k, n, c, vec):
                    wait_full(dve, kind, pl, k)
                    bnk, _ = pl.piece(k)
                    c0, w = span(c)
                    m = min(w, SEQ - c0)
                    dve.scalar_tensor_tensor(X[:, n, c0:c0 + m], g.ps[bnk][:, 0:m], g.ada[:, vec + n, 0:1], X[:, n, c0:c0 + m],
                                             ALU.mult, ALU.add).then_inc(s_pf[bnk], 1)

                def samples(kind, pl, k, n, vec, count):
                    wait_full(dve, kind, pl, k)
                    bnk, _ = pl.piece(k)
                    wait(dve, s_stm, count * 2 - 2)
                    dve.tensor_tensor(seqv(stm[:, :]), seqv(g.ps[bnk][:, PC - NS:PC]), bc(g.ada[:, vec + n, 1:NCOND].unsqueeze(2), SLEN),
                                      ALU.mult).then_inc(s_stm, 1)
                    dve.wait_ge(s_stm, count * 2 - 1)
                    dve.tensor_tensor(X[:, n, SEQ:T], X[:, n, SEQ:T], stm[:, :], ALU.add).then_inc(s_stm, 1)

                def rows_out(t):
                    n = P if t < NC else NS
                    dve.wait_ge(s_fr, t + 1)
                    link(dve.reciprocal(fss[:, t, 3:4], fss[:, t, 2:3]))
                    if t >= NXR:
                        dve.wait_ge(s_y[t % NXR], 16 * (t // NXR))
                    for b in range(2):
                        ins = dve.scalar_tensor_tensor(OT[0:n, t % NXR, 512 * b:512 * b + 512], ENDB[2 * (t % NE) + b][0:n, :], fss[0:n, t, 3:4],
                                                       GF[0:n, 512 * b:512 * b + 512], ALU.mult, ALU.mult)
                    ins.then_inc(s_fo, 1)

                dve.memset(small[:, 0, :], 1.0)
                dve.memset(fss[:, :, :], 1.0)
                dve.wait_ge(s_co, 1)
                for b in range(2):
                    dve.tensor_copy(co[0:KEEP, 512 * b:512 * b + 512], MISC[b][0:KEEP, :])
                dve.tensor_copy(stn[:, :], MISC[2][0:H * NCOND, 0:P]).then_inc(s_cc, 2)
                for t in range(NT):
                    n = P if t < NC else NS
                    dve.wait_ge(s_xt, 2 * t + 1)
                    dve.tensor_copy(X[:, 0:4, t * P:t * P + n], turned_x(t, 0)).then_inc(s_xe[0], 1)
                    if t % 3 == 1:
                        dve.wait_ge(s_mh, t + 1)
                        dve.tensor_tensor(g.Hl[:, t, :], mixed(t).bitcast(F32), g.Hh[:, t, :].bitcast(F32), ALU.subtract).then_inc(s_mlv, 1)
                for b in range(2):
                    dve.wait_ge(s_xe[b], NT)
                run(dve, step)
                dve.wait_ge(s_gf, 16)
                for t in range(NT + 1):
                    if t < NT:
                        n = P if t < NC else NS
                        dve.wait_ge(s_fs, 2 * t + 2)
                        link(dve.tensor_tensor(fss[0:n, t, 2:3], fss[0:n, t, 0:1], fss[0:n, t, 1:2], ALU.add))
                        dve.tensor_scalar(fss[:, t, 2:3], fss[:, t, 2:3], 1.0 / D, EPS, ALU.mult, ALU.add).then_inc(s_fm, 1)
                    if t:
                        rows_out(t - 1)


class Shared:
    pass


def build(nc, a, outs, loops=True):
    a = dict(a, **outs)
    g = Shared()
    g.dve_per = DVE_PER
    g.mix_d = nc.dram_tensor("mix_scratch", (P, KC, T), F32, kind="Internal").ap()
    with ExitStack() as ctx:
        sb = lambda n, s, d=F32: ctx.enter_context(nc.sbuf_tensor(n, s, d))
        g.ps = [ctx.enter_context(nc.psum_tensor(f"bank{n}", [P, 512], F32)) for n in range(8)]
        g.Hh = sb("h_hi", [P, KC, T], F32R)
        g.Hl = sb("h_lo", [P, KC, T], F32R)
        g.ident = sb("identity", [P, P])
        g.ones = sb("ones", [P, P])
        g.cmask = sb("causal", [P, P])
        g.cmask_s = sb("causal_samples", [NS, NS])
        g.lmask = sb("level_masks", [P, NL, P], U8)
        g.seqcol = sb("seq_columns", [NS, NSEQ])
        g.seqrow = sb("seq_rows", [P, NSEQ, NS])
        g.reset = sb("resets", [P, T], BF16)
        g.vec = sb("vectors", [P, P])
        g.cT = sb("c_t", [P, KC, NCOND])
        g.ada = sb("ada", [P, 6 * KC, NCOND])
        g.sconvT = sb("state_conv_t", [P, KC, NSEQ * (W4 - 1)])
        g.n0T = sb("state_n_t", [P, NSEQ * H])
        g.pk = sb("conv_keep", [P, KC, KEEP])
        g.nout = sb("n_out", [P, H * NCOND])
        setup_phase(nc, g, a)
        mixer_phase(nc, g, a, loops)
        ffn_phase(nc, g, a, loops)


DVE_PER = 34
LOOPS = True

_INS = ["x_prompt", "x_sample", "state_conv", "state_C", "state_n", "state_m", "state_S", "c_prompt", "c_sample",
        "g_norm1", "g_norm2", "w_ada", "b_ada", "w_in", "conv_w", "conv_b", "b_igate", "b_fgate", "g_head_a",
        "w_alpha", "b_alpha", "g_head_b", "w_out", "w_ffn_gate", "w_ffn_up", "w_ffn_down", "g_final"]
_OUTS = [("y_prompt", (1, SEQ, D)), ("y_sample", (NSEQ, SLEN, D)),
         ("conv_p", (1, 1, W4 - 1, 2 * QK)), ("C_p", (1, 1, H, DK, DV)), ("n_p", (1, 1, H, DK)), ("m_p", (1, 1, H)),
         ("S_p", (1, 1, H, DK, DV)),
         ("conv_s", (1, NSEQ, W4 - 1, 2 * QK)), ("C_s", (1, NSEQ, H, DK, DV)), ("n_s", (1, NSEQ, H, DK)), ("m_s", (1, NSEQ, H)),
         ("S_s", (1, NSEQ, H, DK, DV))]


def kernel(**inputs):
    import numpy as _np
    import concourse.bacc as _bacc
    from concourse.bass_utils import run_bass_kernel_spmd as _run

    nc = _bacc.Bacc("TRN2", target_bir_lowering=False, num_devices=1)
    arrays, args, outs = {}, {}, {}
    for name in _INS:
        x = _np.ascontiguousarray(inputs[name])
        arrays[f"in_{name}"] = x
        args[name] = nc.dram_tensor(f"in_{name}", x.shape, F32, kind="ExternalInput").ap()
    for name, shape in _OUTS:
        outs[name] = nc.dram_tensor(f"out_{name}", shape, F32, kind="ExternalOutput").ap()
    build(nc, args, outs, LOOPS)
    r = _run(nc, [arrays], core_ids=[0])
    return tuple(r.results[0][f"out_{name}"] for name, _ in _OUTS)
```

```python
from contextlib import ExitStack

import concourse.bass as bass
from concourse import mybir

F32 = mybir.dt.float32
F32R = mybir.dt.float32r
BF16 = mybir.dt.bfloat16
U8 = mybir.dt.uint8
ALU = mybir.AluOpType
ACT = mybir.ActivationFunctionType

P = 128
D = 1024
KC = D // P
SEQ = 1024
NSEQ, SLEN = 8, 4
NS = NSEQ * SLEN
T = SEQ + NS
NC = SEQ // P
NT = NC + 1
H, DK, DV = 4, 128, 256
VX = DV + 1
W4 = 4
RANK = 16
FF = 2816
FT = FF // P
EPS = 1e-6
QSCALE = DK ** -0.5
TAU = 16.0
BIG = 1e30
NPC = 3
PC = T // NPC
NCOND = 1 + NSEQ
ZP = SEQ + W4 - 1
ZS = SLEN + W4 - 1
ZN = ZP + NSEQ * ZS
ZO = ZN - (W4 - 1)
KEEP = (W4 - 1) * NCOND

QK = H * DK
C_QA, C_KA = 0, QK
C_VA = 2 * QK
C_OA = C_VA + H * DV
C_IF = C_OA + H * DV
C_QB = C_IF + 2 * H
C_KB = C_QB + QK
C_VB = C_KB + QK
C_RB = C_VB + H * DV
C_LR = C_RB + H * DV
C_GA = C_LR + RANK
C_GB = C_GA + D

V_BADA = 0
V_G1 = V_BADA + 6 * KC
V_G2 = V_G1 + KC
V_CW = V_G2 + KC
V_CB = V_CW + W4 * KC
V_HA = V_CB + KC
V_HB = V_HA + KC
V_AL = V_HB + KC
NV = V_AL + H

LEVELS = [64, 32, 16, 8, 4, 2, 1]
NL = len(LEVELS) + 1

ROW_A, ROW_W, ROW_L = 0, 32, 64


def wait(e, sem, v):
    if not (isinstance(v, int) and v <= 0):
        e.wait_ge(sem, v)


class Steps:

    def __init__(self, engine, sem, per=0):
        self.e, self.sem, self.per, self.base, self.n, self.i = engine, sem, per, None, 0, 0

    def turn(self, i):
        if self.per:
            if self.base is None:
                self.base = self.n
            self.i, self.n = i, 0

    def value(self):
        return self.i * self.per + ((self.base or 0) + self.n)

    def did(self, ins):
        ins.then_inc(self.sem, 1)
        self.n += 1
        return self.n

    def link(self, ins):
        self.did(ins)
        self.e.wait_ge(self.sem, self.value())


def bc(ap, n):
    return ap.to_broadcast(list(ap.shape[:-1]) + [n])


def mid(ap, n):
    return ap.unsqueeze(1).to_broadcast([ap.shape[0], n, ap.shape[1]])


def setup_phase(nc, g, a):
    with ExitStack() as ctx:
        sb = lambda n, s, d=F32: ctx.enter_context(nc.sbuf_tensor(n, s, d))
        sem = lambda n: ctx.enter_context(nc.semaphore(n))
        NX = 4
        xs = sb("x_rows", [P, NX, D])
        X = sb("x_turned_rows", [P, KC, T])
        vr = sb("vec_rows", [P, P])
        cr = sb("c_rows", [NCOND, D])
        nr = sb("n_rows", [NSEQ * H, DK])
        sr = sb("sconv_rows", [NSEQ * (W4 - 1), D])
        NW, KH, NA = 3, 2, 4
        wa = sb("w_ada_ring", [P, NW, KC // KH, 512])
        ar = sb("ada_rows", [NCOND, NA * 512])
        lmf = sb("level_masks_f", [P, NL, P])
        cT = g.cT
        am = sb("norm1_mult", [P, KC, NCOND])
        junk = sb("junk", [P, D])
        ssq = sb("ssq", [P, NT])
        rstd = sb("rstd", [P, NT])
        NTMP = 4
        tmp = g.early[:, 0:NTMP, 0:T]
        dg = g.early[:, NTMP, 0:T]
        s_small, s_x = sem("small_loaded"), [sem(f"x_loaded{t}") for t in range(NX)]
        s_wa = [sem(f"w_ada_loaded{i}") for i in range(NW)]
        s_const, s_pool = sem("constants"), sem("pool_steps")
        s_zero = sem("w_raw_zeroed")
        s_tr, s_trc = sem("small_transposed"), sem("small_copied")
        s_adau, s_arow, s_ada = sem("w_ada_used"), sem("ada_rows_copied"), sem("ada_turned")
        s_ssq, s_t, s_sqrt, s_xn = sem("ssq_done"), sem("ms_done"), sem("sqrt_done"), sem("x_normed")
        s_xc, s_dg, s_r, s_xst = [sem("x_taken_v"), sem("x_taken_s")], sem("diagonals_ready"), sem("rstd_spread"), sem("x_stored")
        s_dve = sem("dve_steps")
        s_xt = sem("x_transposed")
        s_ht, s_hi, s_lo, s_lov = sem("h_affine"), sem("h_hi"), sem("h_lo"), sem("h_lo_by_vector")
        SMALLB, ADAB = g.ps[4], g.ps[5]
        O_V, O_C, O_N, O_S = 0, P, P + KC * NCOND, P + KC * NCOND + NSEQ * H


        def turned(t, b):
            n = P if t < NC else NS
            return g.ps[(2 * t + b) % 4][:, :].rearrange("p (k t) -> p k t", t=P)[:, :, 0:n]
        JO = (0, 2, 1, 3)
        PARTS = [(0, 512), (512, 512), (SEQ, NS)]

        with nc.Block() as block:

            @block.sync
            def _(sp):
                def small(dst, src):
                    sp.dma_start(dst, src).then_inc(s_small, 16)
                small(vr[V_BADA:V_G1, :], a["b_ada"].rearrange("o (r c) -> (o r) c", c=P))
                small(vr[V_G1:V_G2, :], a["g_norm1"].rearrange("o (r c) -> (o r) c", c=P))
                small(vr[V_G2:V_CW, :], a["g_norm2"].rearrange("o (r c) -> (o r) c", c=P))
                small(vr[V_CW:V_CB, :], a["conv_w"].rearrange("o j (r c) -> (o j r) c", c=P))
                small(vr[V_CB:V_HA, :], a["conv_b"].rearrange("o (r c) -> (o r) c", c=P))
                small(vr[V_HA:V_HB, :], a["g_head_a"].rearrange("o h (r c) -> (o h r) c", c=P))
                small(vr[V_HB:V_AL, :], a["g_head_b"].rearrange("o h (r c) -> (o h r) c", c=P))
                small(vr[V_AL:NV, :], a["b_alpha"].rearrange("o (r c) -> (o r) c", c=P))
                small(cr[0:1, :], a["c_prompt"])
                small(cr[1:NCOND, :], a["c_sample"])
                small(nr[:, :], a["state_n"].rearrange("o b h d -> (o b h) d"))
                small(sr[:, :], a["state_conv"].rearrange("o b j c -> (o b j) c"))
                wsrc = a["w_ada"][0].rearrange("(k p) n -> p k n", p=P)
                for t in range(NT):
                    if t >= NX:
                        sp.wait_ge(s_xt, 2 * (t - NX) + 2)
                        sp.wait_ge(s_ssq, t - NX + 1)
                    n = P if t < NC else NS
                    src = a["x_prompt"][0, t * P:(t + 1) * P, :] if t < NC else a["x_sample"].rearrange("b t d -> (b t) d")
                    sp.dma_start(xs[0:n, t % NX, :], src).then_inc(s_x[t % NX], 16)
                for n in range(NA * KH):
                    if n >= NW:
                        sp.wait_ge(s_adau, n - NW + 1)
                    j, h = JO[n // KH], n % KH
                    src = wsrc[:, h * KC // KH:(h + 1) * KC // KH, j * 512:(j + 1) * 512]
                    sp.dma_start(wa[:, n % NW], src).then_inc(s_wa[n % NW], 16)
                for b in range(2):
                    sp.wait_ge(s_xc[b], NT)
                w_in = a["w_in"][0].rearrange("(k p) n -> p k n", p=P)
                sp.wait_ge(s_zero, 1)
                for h in range(2):
                    for c0, n, at in ((C_IF, H, 0), (C_IF + H, H, 32), (C_LR, RANK, 64)):
                        sp.dma_start(g.raw[:, h, :, at:at + n], w_in[:, 4 * h:4 * h + 4, c0:c0 + n]).then_inc(g.s_w[h], 16)
                for h in range(2):
                    sp.dma_start(g.raw[:, 2 + h], w_half(w_in, "S", 0, 1, h)).then_inc(g.s_w[2 + h], 16)
                sp.dma_start(g.x_d, X[:, :, :]).then_inc(s_xst, 16)
                sp.wait_ge(s_xst, 16)

            @block.gpsimd
            def _(pool):
                st = Steps(pool, s_pool)
                ge = ALU.is_ge

                def keep(v, base, pattern, chan, fill=0.0, op=ge):
                    st.link(pool.affine_select(out=v, in_=v, compare_op=op, fill=fill, base=base,
                                               pattern=pattern, channel_multiplier=chan))
                st.link(pool.memset(g.ident[:, :], 0.0))
                keep(g.ident[:, :], 0, [[-1, P]], 1, fill=1.0, op=ALU.not_equal)
                pool.memset(g.ones[:, :], 1.0).then_inc(s_const, 1)
                st.link(pool.memset(g.cmask[:, :], BIG))
                keep(g.cmask[:, :], 0, [[1, P]], -1, fill=-BIG)
                st.link(pool.memset(g.cmask_s[:, :], BIG))
                keep(g.cmask_s[:, :], 0, [[1, NS]], -1, fill=-BIG)
                v = g.cmask_s[:, :].rearrange("s (b r) -> s b r", r=SLEN)
                keep(v, SLEN - 1, [[SLEN, NSEQ], [0, SLEN]], -1, fill=-BIG)
                keep(v, 0, [[-SLEN, NSEQ], [0, SLEN]], 1, fill=-BIG)
                st.link(pool.memset(g.seqcol[:, :], 1.0))
                keep(g.seqcol[:, :], SLEN - 1, [[SLEN, NSEQ]], -1)
                keep(g.seqcol[:, :], 0, [[-SLEN, NSEQ]], 1)
                st.link(pool.memset(g.seqrow[:, :, :], 1.0))
                keep(g.seqrow[:, :, :], SLEN - 1, [[SLEN, NSEQ], [-1, NS]], 0)
                keep(g.seqrow[:, :, :], 0, [[-SLEN, NSEQ], [1, NS]], 0)
                st.link(pool.memset(lmf[:, :, :], 0.0))
                for l, hs in enumerate(LEVELS):
                    n = P // (2 * hs)
                    v = lmf[:, l, :].rearrange("s (n w) -> s n w", w=2 * hs)[:, :, hs:2 * hs]
                    st.link(pool.memset(v, 1.0))
                    keep(v, 0, [[-2 * hs, n], [0, hs]], 1)
                    keep(v, hs - 1, [[2 * hs, n], [0, hs]], -1)
                st.link(pool.tensor_copy(lmf[:, NL - 1, :], g.ident[:, :]))
                st.link(pool.tensor_copy(g.lmask[:, :, :], lmf[:, :, :]))
                st.link(pool.memset(g.reset[:, :], 1.0))
                st.link(pool.memset(g.reset[:, 0:SEQ].rearrange("p (c t) -> p c t", t=P)[:, :, 0:1], 0.0))
                st.link(pool.memset(g.reset[:, SEQ:T].rearrange("p (b t) -> p b t", t=SLEN)[:, :, 0:1], 0.0))
                pool.memset(g.nout[:, :], 0.0)
                pool.memset(g.raw[:, 0:2], 0.0).then_inc(s_zero, 1)
                for k in range(0, KC, 2):
                    pool.wait_ge(s_hi, k + 1)
                    pool.tensor_tensor(g.Hl[:, k, :], tmp[:, k % NTMP, :], g.Hh[:, k, :].bitcast(F32), ALU.subtract).then_inc(s_lo, 1)

            @block.tensor
            def _(pe):
                pe.wait_ge(s_small, 12 * 16)
                pe.wait_ge(s_const, 1)
                pe.transpose(SMALLB[:, O_V:O_V + NV], vr[0:NV, :], g.ident[0:NV, 0:NV])
                for k in range(KC):
                    pe.transpose(SMALLB[:, O_C + k * NCOND:O_C + (k + 1) * NCOND], cr[:, k * P:(k + 1) * P],
                                 g.ident[0:NCOND, 0:NCOND])
                pe.transpose(SMALLB[:, O_N:O_N + NSEQ * H], nr[:, :], g.ident[0:NSEQ * H, 0:NSEQ * H])
                m = NSEQ * (W4 - 1)
                last = None
                for k in range(KC):
                    if O_S + (k + 1) * m > 512:
                        raise ValueError("the small transposes outgrow their bank")
                    last = pe.transpose(SMALLB[:, O_S + k * m:O_S + (k + 1) * m], sr[:, k * P:(k + 1) * P], g.ident[0:m, 0:m])
                last.then_inc(s_tr, 1)
                for t in range(NT):
                    n = P if t < NC else NS
                    pe.wait_ge(s_x[t % NX], 16 * (t // NX + 1))
                    for b in range(2):
                        if t >= 2:
                            pe.wait_ge(s_xc[b], t - 1)
                        for k in range(4):
                            last = pe.transpose(g.ps[(2 * t + b) % 4][:, k * P:k * P + n],
                                                xs[0:n, t % NX, (4 * b + k) * P:(4 * b + k + 1) * P], g.ident[0:n, 0:n])
                        last.then_inc(s_xt, 1)

                def ada_columns(j):
                    pe.wait_ge(s_arow, JO.index(j) + 1)
                    for n in range(4 * j, 4 * j + 4):
                        last = pe.transpose(ADAB[:, n * NCOND:(n + 1) * NCOND], ar[:, n * P:(n + 1) * P], g.ident[0:NCOND, 0:NCOND])
                    return last
                pe.wait_ge(s_trc, 1)
                for n in range(NA * KH):
                    j, h = n // KH, n % KH
                    pe.wait_ge(s_wa[n % NW], 16 * (n // NW + 1))
                    if h == 0 and j >= 2:
                        pe.wait_ge(s_arow, j - 1)
                    for k in range(KC // KH):
                        last = pe.matmul(g.ps[6 + j % 2][0:NCOND, :], cT[:, h * KC // KH + k, :], wa[:, n % NW, k, :],
                                         start=(h == 0 and k == 0), stop=(h == KH - 1 and k == KC // KH - 1))
                    last.then_inc(s_adau, 1)
                    if n == 1:
                        pe.wait_ge(s_dg, 1)
                        for b in range(2):
                            pe.wait_ge(s_xc[b], NT)
                        for b, (c0, m) in enumerate(PARTS):
                            q = P if b < 2 else NS
                            last = pe.matmul(g.ps[b][:, 0:m], g.ones[0:q, :], dg[0:q, c0:c0 + m], start=True, stop=True)
                        last.then_inc(s_r, 1)
                    if n == 4:
                        ada_columns(JO[0])
                        ada_columns(JO[1]).then_inc(s_ada, 1)
                ada_columns(JO[2])
                ada_columns(JO[3]).then_inc(s_ada, 1)

            @block.scalar
            def _(act):
                act.wait_ge(s_t, 1)
                for t in range(NT):
                    n = P if t < NC else NS
                    if t:
                        act.wait_ge(s_ssq, t)
                    act.wait_ge(s_x[t % NX], 16 * (t // NX + 1))
                    act.activation(junk[0:n, :], xs[0:n, t % NX, :], ACT.Square, accum_out=ssq[0:n, t:t + 1]).then_inc(s_ssq, 1)
                    act.wait_ge(s_xt, 2 * t + 2)
                    act.activation(X[:, 4:8, t * P:t * P + n], turned(t, 1), ACT.Copy).then_inc(s_xc[1], 1)
                act.wait_ge(s_t, 2)
                act.activation(rstd[:, :], ssq[:, :], ACT.Sqrt).then_inc(s_sqrt, 1)
                for k in range(KC):
                    act.wait_ge(s_ht, k + 1)
                    act.activation(g.Hh[:, k, :], tmp[:, k % NTMP, :], ACT.Copy).then_inc(s_hi, 1)

            @block.vector
            def _(dve):
                st = Steps(dve, s_dve)
                dve.memset(ssq[:, :], 1.0).then_inc(s_t, 1)
                dve.wait_ge(s_tr, 1)
                dve.tensor_copy(cT[:, :, :], SMALLB[:, O_C:O_N].rearrange("p (k c) -> p k c", c=NCOND)).then_inc(s_trc, 1)
                st.link(dve.tensor_copy(g.vec[:, 0:NV], SMALLB[:, O_V:O_V + NV]))
                dve.tensor_copy(g.n0T[:, :], SMALLB[:, O_N:O_S])
                m = NSEQ * (W4 - 1)
                dve.tensor_copy(g.sconvT[:, :, :], SMALLB[:, O_S:O_S + KC * m].rearrange("p (k c) -> p k c", c=m))
                st.link(dve.tensor_scalar(g.vec[:, V_HA:V_AL], g.vec[:, V_HA:V_AL], 0.25, None, ALU.mult))
                for t in range(NT):
                    n = P if t < NC else NS
                    dve.wait_ge(s_xt, 2 * t + 1)
                    dve.tensor_copy(X[:, 0:4, t * P:t * P + n], turned(t, 0)).then_inc(s_xc[0], 1)
                dve.wait_ge(s_ssq, NT)
                dve.tensor_scalar(ssq[:, :], ssq[:, :], 1.0 / D, EPS, ALU.mult, ALU.add).then_inc(s_t, 1)
                dve.wait_ge(s_sqrt, 1)
                st.link(dve.reciprocal(ssq[:, :], rstd[:, :]))
                dve.tensor_tensor(dg[:, 0:SEQ].rearrange("p (c t) -> p c t", t=P), mid(g.ident[:, :], NC),
                                  bc(ssq[:, 0:NC].unsqueeze(2), P), ALU.mult)
                dve.tensor_scalar(dg[0:NS, SEQ:T], g.ident[0:NS, 0:NS], ssq[0:NS, NC:NT], None, ALU.mult).then_inc(s_dg, 1)

                def row(n):
                    dve.wait_ge(s_adau, KH * (n + 1))
                    dve.tensor_copy(ar[:, JO[n] * 512:(JO[n] + 1) * 512], g.ps[6 + n % 2][0:NCOND, :]).then_inc(s_arow, 1)

                def normed(k):
                    if k >= NTMP:
                        dve.wait_ge(s_lov if k % 2 else s_lo, (k - NTMP) // 2 + 1)
                    for b, (c0, m) in enumerate(PARTS):
                        ins = dve.tensor_tensor(tmp[:, k % NTMP, c0:c0 + m], X[:, k, c0:c0 + m], g.ps[b][:, 0:m], ALU.mult)
                    ins.then_inc(s_xn, 1)

                def affine(c):
                    dve.wait_ge(s_ada, c + 1)
                    four = slice(4 * c, 4 * c + 4)
                    for base in (0, KC):
                        n0 = base + 4 * c
                        st.did(dve.tensor_tensor(g.ada[:, n0:n0 + 4, :], ADAB[:, n0 * NCOND:(n0 + 4) * NCOND].rearrange("p (n c) -> p n c", c=NCOND),
                                                 bc(g.vec[:, n0:n0 + 4].unsqueeze(2), NCOND), ALU.add))
                    dve.wait_ge(s_dve, st.value())
                    st.link(dve.scalar_tensor_tensor(am[:, four, :], g.ada[:, KC + 4 * c:KC + 4 * c + 4, :], 1.0,
                                                     bc(g.vec[:, V_G1 + 4 * c:V_G1 + 4 * c + 4].unsqueeze(2), NCOND), ALU.add, ALU.mult))

                def lower(k):
                    dve.wait_ge(s_hi, k + 1)
                    dve.tensor_tensor(g.Hl[:, k, :], tmp[:, k % NTMP, :], g.Hh[:, k, :].bitcast(F32), ALU.subtract).then_inc(s_lov, 1)

                def shifted(k):
                    dve.wait_ge(s_xn, k + 1)
                    h = tmp[:, k % NTMP, :]
                    v = h[:, SEQ:T].rearrange("p (b r) -> p b r", r=SLEN)
                    st.did(dve.tensor_tensor(v, v, bc(am[:, k, 1:NCOND].unsqueeze(2), SLEN), ALU.mult))
                    st.did(dve.tensor_scalar(h[:, 0:SEQ], h[:, 0:SEQ], am[:, k, 0:1], g.ada[:, k, 0:1], ALU.mult, ALU.add))
                    dve.wait_ge(s_dve, st.value())
                    dve.tensor_tensor(v, v, bc(g.ada[:, k, 1:NCOND].unsqueeze(2), SLEN), ALU.add).then_inc(s_ht, 1)

                dve.wait_ge(s_xc[0], NT)
                dve.wait_ge(s_xc[1], NT)
                row(0)
                dve.wait_ge(s_r, 1)
                for k in range(NTMP):
                    normed(k)
                row(1)
                affine(0)
                for k in range(NTMP):
                    shifted(k)
                    if k == 1:
                        row(2)
                    if k == 2:
                        lower(1)
                normed(4)
                lower(3)
                for k in range(5, KC):
                    normed(k)
                row(3)
                affine(1)
                for k in range(4, KC):
                    shifted(k)
                    if k == 6:
                        lower(5)
                lower(7)


TILES = {"S": ["small", "q", "v0", "k", "v1"],
         "A": ["q", "v0", "k", "v1", "o0", "g0", "o1", "g1"],
         "B": ["q", "v0", "k", "v1", "o0", "g0", "o1", "g1"],
         "L": ["o0", "g0", "o1", "g1"]}
NS_TILES, NW_TILES = len(TILES["S"]), len(TILES["A"])
COLUMN = {("A", "q"): (C_QB, DK), ("A", "k"): (C_KB, DK), ("A", "v"): (C_VB, DV), ("A", "o"): (C_OA, DV), ("A", "g"): (C_GA, DV),
          ("B", "q"): (C_QA, DK), ("B", "k"): (C_KA, DK), ("B", "v"): (C_VA, DV), ("B", "o"): (C_RB, DV), ("B", "g"): (C_GB, DV)}
CHAIN = [f"chunk{c}" for c in range(NC)]
SAMPLE = [f"sample{b}" for b in range(NSEQ)]
AT_SLOT = {
    "S": [("rows", 8), ("rows_exp", 14), ("conv_q", 16), ("taps_q", 16), ("silu_q", 17), ("rows_t", 21), ("vt0", 21),
          ("conv_k", 23), ("taps_k", 24), ("silu_k", 25), ("vt1", 29)],
    "A": [("select", 0), ("decay", 1), ("ada_load0", 2), ("scores", 6), ("keys", 6), ("interq", 8), ("ada0", 9),
          ("masked", 12), ("ada_load1", 12), ("chunk0", 13), ("chunk1", 13), ("chunk2", 13), ("vt0", 14), ("chunk3", 15),
          ("chunk4", 19), ("chunk5", 19), ("ada1", 21), ("chunk6", 21), ("chunk7", 21), ("sample_out", 23), ("ada_load2", 24),
          ("sample0", 31), ("vt1", 31), ("sample1", 31), ("sample2", 31), ("ada2", 33), ("sample3", 34), ("sample4", 35),
          ("sample5", 35), ("sample6", 35), ("gate0", 36), ("ada_load3", 36), ("sample7", 37), ("alpha", 37), ("norm", 39),
          ("turn0", 44), ("ada3", 45), ("gate1", 47), ("turn1", 47)],
    "B": [("ada_load0", 3), ("sums", 3), ("level0", 5), ("conv_q", 7), ("level1", 7), ("taps_q", 7), ("level2", 10),
          ("silu_q", 10), ("ada0", 12), ("level3", 14), ("ada_load1", 15), ("level4", 16), ("vt0", 17), ("conv_k", 20),
          ("level5", 20), ("level6", 22), ("taps_k", 24), ("ada1", 24), ("level7", 26), ("ada_load2", 27), ("vt1", 27),
          ("silu_k", 30), ("masked", 30), ("keys", 30), ("chunk0", 31), ("chunk1", 31), ("chunk2", 32), ("chunk3", 32),
          ("chunk4", 32), ("gate_r0", 33), ("chunk5", 33), ("chunk6", 34), ("gate0", 35), ("chunk7", 35), ("ada2", 36),
          ("ada_load3", 39), ("sample_out", 39), ("sample0", 39), ("sample1", 41), ("sample2", 42), ("sample3", 42),
          ("sample4", 42), ("sample5", 43), ("norm", 43), ("sample6", 43), ("gate_r1", 44), ("sample7", 44), ("gate1", 47),
          ("ada3", 47), ("turn0", 47), ("turn1", 47)],
    "L": [("sums", 0), ("ada_load0", 2), ("level0", 2), ("level1", 3), ("level2", 4), ("level3", 5), ("ada0", 6),
          ("level4", 8), ("ada_load1", 8), ("level5", 8), ("gate_r0", 9), ("level6", 10), ("level7", 11), ("ada1", 12),
          ("keys", 12), ("masked", 13), ("chunk0", 13), ("chunk1", 13), ("ada_load2", 14), ("chunk2", 14), ("gate0", 14),
          ("chunk3", 15), ("chunk4", 15), ("chunk5", 16), ("chunk6", 16), ("chunk7", 17), ("ada2", 18), ("sample_out", 18),
          ("gate_r1", 18), ("sample0", 19), ("sample1", 19), ("sample2", 19), ("sample3", 19), ("sample4", 19),
          ("sample5", 20), ("sample6", 20), ("ada_load3", 20), ("gate1", 21), ("sample7", 23), ("ada3", 23), ("norm", 23),
          ("turn0", 23), ("turn1", 23)],
}
USES = {"decay": 3, "scores": 3, "interq": 3, "keys": 3, "vt0": 3, "vt1": 3, "sample_out": 1, "turn0": 3, "turn1": 3,
        "alpha": 3, "rows_t": 3, **{s: 2 for s in CHAIN}, **{s: 1 for s in SAMPLE}, **{f"ada{q}": 1 for q in range(4)},
        **{f"level{l}": 1 + (l >= NL - 3) + (l == NL - 1) for l in range(NL)}}


def timeline(w):
    out, stages = [], sorted(AT_SLOT[w], key=lambda x: x[1])
    for s in range(6 * len(TILES[w])):
        out.append(("piece", s // 6, s // 3 % 2, s % 3))
        out += [(n,) for n, at in stages if at == s]
    assert len([x for x in out if len(x) == 1]) == len(stages)
    return out


TIMELINE = {w: timeline(w) for w in TILES}
USE = {w: {} for w in TILES}
NUSE = {}
for _w in TILES:
    _n = 0
    for _x in TIMELINE[_w]:
        if len(_x) == 1 and _x[0] in USES:
            USE[_w][_x[0]] = _n
            _n += USES[_x[0]]
    NUSE[_w] = _n
BEGUN = 1
NRB = 4


def uses_before(w, i, n):
    b = n % NRB
    mine = lambda w, m: sum(1 for x in range(m) if x % NRB == b)
    total, own = NUSE["S"], mine("S", NUSE["S"])
    if w == "S":
        return n, mine("S", n)
    total, own = total + i * (NUSE["A"] + NUSE["B"]), own + i * (mine("A", NUSE["A"]) + mine("B", NUSE["B"]))
    if w in "BL":
        total, own = total + NUSE["A"], own + mine("A", NUSE["A"])
    return total + n, own + mine(w, n)


def tile_index(w, i, l):
    return l if w == "S" else i * 2 * NW_TILES + (NS_TILES + l + (NW_TILES if w in "BL" else 0))


def after(w, i, l, h, by):
    l, h = l + (h + by) // 2, (h + by) % 2
    while l >= len(TILES[w]):
        l -= len(TILES[w])
        if w == "L":
            return None
        if w == "B":
            w, i = "A", i + 1
        else:
            w, i = ("A" if w == "S" else "L" if isinstance(i, int) and i == H - 1 else "B"), i
    return w, i, l, h


def static(i, per, k, n):
    assert per % n == 0
    return k % n, i * (per // n) + k // n


NEARLY = 5
RAW = 4


def w_half(w_in, w, i, l, h):
    name = TILES[w][l]
    base, step = COLUMN["B" if w in "SL" else w, name[0]]
    head = 0 if w == "S" else i + 1 if w == "B" and name[0] in "qkv" else i
    return w_in[:, 4 * h:4 * h + 4, bass.ds(head * step + (base + (P if name[1:] == "1" else 0)), P)]


def mixer_phase(nc, g, a, loops=True):
    with ExitStack() as ctx:
        sb = lambda n, s, d=F32: ctx.enter_context(nc.sbuf_tensor(n, s, d))
        sem = lambda n: ctx.enter_context(nc.semaphore(n))
        SPL = 2
        raw = g.raw
        Wh = sb("w_hi", [P, SPL, 4, P], F32R)
        Wl = sb("w_lo", [P, SPL, 4, P], F32R)
        Q = [g.early[:, 0, 0:T], sb("q_b", [P, T])]
        K = [g.early[:, 1, 0:T], sb("k_b", [P, T])]
        V = [sb("v_a", [P, NT, VX]), sb("v_b", [P, NT, VX])]
        VS, Z, CV = g.early[:, 2, 0:T], g.early[:, 3, :], g.early[:, 4, :]
        G = sb("gate", [P, 2, T])
        TG = sb("gate_t", [P, T])
        AT = sb("scores_t", [P, T])
        QD = sb("q_decayed", [P, T])
        KD = sb("k_decayed", [P, NT * P])
        TA = sb("temp_a", [P, T])
        TB = sb("temp_b", [P, T])
        ST = sb("sample_state", [P, NSEQ, VX])
        SS = sb("state", [P, 2, VX])
        M = sb("mix", [P, 2, T])
        HS = sb("sample_heads", [P, VX])
        QM = sb("q_masked", [P, NSEQ, NS])
        rows = sb("gate_rows", [P, T])
        cols = sb("gate_cols", [P, NT, 3 * H])
        hcol = sb("head_cols", [P, NT, 3])
        wcr = sb("carry_rows", [H, 2 * NC])
        wcs = sb("carry_sel", [H, 2 * NC])
        sdec = sb("state_decay", [P, 2 * NC])
        wal = sb("w_alpha_all", [P, QK])
        walh = sb("w_alpha_head", [P, DK])
        bif = sb("b_if", [H, 2])
        m0 = sb("m0", [H, NSEQ])
        me = sb("m_ends", [H, 4, 2 * NC])
        ssq = sb("head_ssq", [P, NT])
        den = sb("head_den", [P, NT])
        ms = sb("head_ms", [P, NT])
        scl = sb("head_scale", [P, NT])
        wad = sb("w_ada_tile", [P, KC, P])

        s_w = g.s_w
        s_hi, s_lo, s_used = sem("w_hi_made"), sem("w_lo_made"), sem("w_used")
        s_piece = sem("pieces_full")
        s_pfree = [sem(f"piece_bank_free{n}") for n in range(4)]
        s_full = sem("rec_bank_full")
        s_free = [sem(f"rec_bank_free{n}") for n in range(NRB)]
        s_small, s_init = sem("small_in"), sem("buffers_set")
        s_dve, s_pool = sem("dve_chain"), sem("pool_chain")
        s_r1, s_r2, s_r3, s_rows = sem("rows_x"), sem("rows_exp"), sem("rows_args"), sem("rows_ready")
        s_cv, s_th, s_silu = sem("conv_done"), sem("conv_tanh"), sem("conv_silu")
        s_sel, s_warg, s_wexp = sem("rows_selected"), sem("decay_args"), sem("decay_exp")
        s_qd, s_km = sem("q_decayed_ready"), sem("sample_masked")
        s_hc = sem("heads_copied")
        s_stl, s_sts = sem("sample_state_loaded"), sem("states_stored")
        s_ms, s_sq, s_hn = sem("head_ms_ready"), sem("head_sqrt"), sem("heads_normed")
        s_gr, s_gate, s_sum = sem("gate_r"), sem("gate_ready"), sem("mixers_summed")
        s_mst = sem("mix_stored")
        s_nab, s_ln = sem("alpha_nab"), sem("alpha_ln")
        s_d, s_E, s_qe, s_ke, s_at0 = sem("level_diff"), sem("level_exp"), sem("level_q"), sem("level_k"), sem("scores_zeroed")
        s_wah = sem("w_alpha_sliced")
        s_kt = sem("k_scaled")
        s_adl = sem("ada_tile_loaded")

        w_in = a["w_in"][0].rearrange("(k p) n -> p k n", p=P)
        w_ada = a["w_ada"][0].rearrange("(k p) n -> p k n", p=P)
        isB = lambda w: w in "BL"

        def half(w, i, l, h):
            per = 4 * NW_TILES
            if w == "S":
                k, j = 2 * l + h, 0
            else:
                k, j = 2 * (NS_TILES + l + (NW_TILES if isB(w) else 0)) + h, i
            r, turns = static(j, per, k, RAW)
            s, _ = static(j, per, k, SPL)
            return r, s, turns, j * per + k

        def piece(w, i, l, c):
            per = 3 * 2 * NW_TILES
            if w == "S":
                k, j = 3 * l + c, 0
            else:
                k, j = 3 * (NS_TILES + l + (NW_TILES if isB(w) else 0)) + c, i
            return static(j, per, k, 4)

        def two(w, i, per=1, first=0):
            return i * (2 * per) + (first + (per if isB(w) else 0))

        def span(c):
            return c * PC, PC

        def wait_piece(e, w, i, l, c):
            if c < 2:
                t = tile_index(w, i, l)
                e.wait_ge(s_piece, t * 2 + (c + 1))
            else:
                e.wait_ge(s_used, half(w, i, l, 1)[3] + 1)

        def wait_evacuated(e, w, i, l):
            b, turns = piece(w, i, l, NPC - 1)
            e.wait_ge(s_pfree[b], turns + 1)

        def wait_use(e, w, i, n):
            e.wait_ge(s_full, uses_before(w, i, n)[0] + 1)

        def apart(e):
            e.nop(nofuse=True)

        def wait_read_use(e, w, i, n):
            e.wait_ge(s_free[n % NRB], uses_before(w, i, n)[1] + 1)

        def wait_read(e, w, i, stage):
            wait_read_use(e, w, i, USE[w][stage] + USES[stage] - 1)

        RB = lambda n: g.ps[4 + n % NRB]
        free = lambda n: s_free[n % NRB]
        PARTS = [(0, 512), (512, 512), (SEQ, NS)]

        def chunks(v):
            return v[:, 0:SEQ].rearrange("p (c t) -> p c t", t=P)

        HP = P // 2

        def halves(v, l, right):
            hs = LEVELS[l]
            return v.rearrange("p (n w) -> p n w", w=2 * hs)[:, :, hs * right:hs * (1 + right)]

        def seqs(v):
            return v[:, SEQ:T].rearrange("p (b t) -> p b t", t=SLEN)

        def run(engine, turn, body):
            body("S", 0)
            if loops:
                with engine.Fori(0, H - 1) as i:
                    body("A", i)
                    body("B", i)
            else:
                for i in range(H - 1):
                    body("A", i)
                    body("B", i)
            body("A", H - 1)
            body("L", H - 1)

        with nc.Block() as block:

            @block.sync
            def _(sp):
                def load_half(w, i, l, h):
                    r, _, turns, before = half(w, i, l, h)
                    sp.wait_ge(s_lo, before - (RAW - 1))
                    sp.dma_start(raw[:, r], w_half(w_in, w, i, l, h)).then_inc(s_w[r], 16)

                small = [(bif[:, 0:1], a["b_igate"].rearrange("o h -> h o")), (bif[:, 1:2], a["b_fgate"].rearrange("o h -> h o")),
                         (m0[:, :], a["state_m"][0].rearrange("b h -> h b")), (wal[64:64 + RANK, :], a["w_alpha"][0])]
                sp.nop().then_inc(s_sts, BEGUN)
                sp.nop().then_inc(s_mst, BEGUN)
                for dst, src in small:
                    sp.dma_start(dst, src, allow_slow_non_contiguous=True).then_inc(s_small, 16)

                def window(w, i):
                    for x in TIMELINE[w]:
                        if x[0] == "piece":
                            _, l, h, c = x
                            nxt = after(w, i, l, h, RAW)
                            if c == 0 and nxt:
                                load_half(*nxt)
                        elif x[0].startswith("ada_load"):
                            q = int(x[0][-1])
                            n = two(w, i, 4) + q
                            wait_use(sp, w, i, USE[w][f"ada{q - 1}"] if q else 0)
                            sp.dma_start(wad[:, :, :], w_ada[:, :, bass.ds(n * P + 2 * D, P)]).then_inc(s_adl, 16)
                            if q == 0:
                                sp.wait_ge(s_sts, BEGUN + two(w, i, 32))
                                apart(sp)
                                sp.wait_ge(s_ms, BEGUN + two(w, i))
                                src = a["state_S"] if isB(w) else a["state_C"]
                                sp.dma_start(ST[:, :, 0:DV], src[0, :, bass.ds(i, 1)].rearrange("b h d v -> d (h b) v")).then_inc(s_stl, 16)
                        elif x[0] == "level1" and w == "L":
                            wait_use(sp, w, i, USE[w]["level1"])
                            sp.wait_ge(s_mst, BEGUN + 16 * (H - 1))
                            sp.dma_start(g.early[:, :, 0:T], g.mix_d[:, 0:NEARLY, :]).then_inc(g.s_early, 16)
                        elif x[0] == "norm":
                            wait_read(sp, w, i, SAMPLE[-1])
                            dst = a["S_p"] if isB(w) else a["C_p"]
                            sp.dma_start(dst[0, 0, bass.ds(i, 1)].rearrange("h d v -> d h v"), SS[:, 1:2, 0:DV]).then_inc(s_sts, 16)
                            dst = a["S_s"] if isB(w) else a["C_s"]
                            sp.dma_start(dst[0, :, bass.ds(i, 1)].rearrange("b h d v -> d (h b) v"), ST[:, :, 0:DV]).then_inc(s_sts, 16)
                        elif x[0] == "rows_t":
                            sp.wait_ge(s_rows, 1)
                            sp.dma_start(a["m_p"][0].rearrange("o h -> h o"), me[:, 1, NC - 1:NC], allow_slow_non_contiguous=True).then_inc(s_small, 16)
                            sp.dma_start(a["m_s"][0].rearrange("b h -> h b"), me[:, 1, NC:2 * NC], allow_slow_non_contiguous=True).then_inc(s_small, 16)
                    if w == "L":
                        for j in range(2):
                            sp.wait_ge(s_sum, BEGUN + i * 2 + (j + 1))
                            sp.dma_start(g.mix_d[:, 2 * i + j, :], M[:, j, :]).then_inc(s_mst, 16)
                    elif isB(w):
                        sp.wait_ge(s_sum, BEGUN + i * 2 + 2)
                        sp.dma_start(g.mix_d[:, bass.ds(i * 2, 2), :], M[:, :, :]).then_inc(s_mst, 16)
                run(sp, None, window)
                sp.wait_ge(s_small, 16 * (len(small) + 2))
                sp.wait_ge(s_sts, BEGUN + 32 * 2 * H)
                sp.wait_ge(s_mst, BEGUN + 16 * (H + 1))

            @block.tensor
            def _(pe):
                def mm_piece(w, i, l, h, c):
                    _, s, _, before = half(w, i, l, h)
                    b, turns = piece(w, i, l, c)
                    if c == 0:
                        pe.wait_ge(s_lo, before + 1)
                    if h == 0:
                        wait(pe, s_pfree[b], turns)
                    c0, n = span(c)
                    for k in range(4):
                        for m, (x, y) in enumerate(((Wh, g.Hh), (Wh, g.Hl), (Wl, g.Hh))):
                            last = pe.matmul(g.ps[b][:, 0:n], x[:, s, k, :], y[:, 4 * h + k, c0:c0 + n],
                                             start=(h == 0 and k == 0 and m == 0), stop=(h == 1 and k == 3 and m == 2))
                    if c == 2:
                        last.then_inc(s_used, 1)
                    elif h == 1:
                        last.then_inc(s_piece, 1)

                def window(w, i):
                    hd = 1 if isB(w) else 0
                    vw = DV if isB(w) else VX
                    q, k, v = Q[hd], K[hd], V[hd]

                    def use(n):
                        wait(pe, free(n), uses_before(w, i, n)[1])
                        return RB(n)

                    def full(ins):
                        ins.then_inc(s_full, 1)

                    def scores(n, kk, qq, samples=True):
                        for b in range(2):
                            bank = use(n + b)
                            for c in range(4 * b, 4 * b + 4):
                                last = pe.matmul(bank[:, (c % 4) * P:(c % 4 + 1) * P], kk[:, c * P:(c + 1) * P],
                                                 qq[:, c * P:(c + 1) * P], start=True, stop=True)
                            full(last)
                        if samples:
                            bank = use(n + 2)
                            apart(pe)
                            full(pe.matmul(bank[0:NS, 0:NS], kk[:, SEQ:T], qq[:, SEQ:T], start=True, stop=True))

                    def turned(n, src):
                        for b in range(2):
                            bank = use(n + b)
                            for c in range(4 * b, 4 * b + 4):
                                last = pe.transpose(bank[:, (c % 4) * P:(c % 4 + 1) * P], src[:, c * P:(c + 1) * P], g.ident[:, :])
                            full(last)
                        full(pe.transpose(use(n + 2)[0:NS, 0:P], src[:, SEQ:T], g.ident[:, :]))

                    for x in TIMELINE[w]:
                        if x[0] == "piece":
                            mm_piece(w, i, *x[1:])
                            continue
                        name = x[0]
                        n = USE[w].get(name)
                        if name == "rows_t":
                            pe.wait_ge(s_rows, 1)
                            for b in range(2):
                                bank = use(n + b)
                                for c in range(4 * b, 4 * b + 4):
                                    last = pe.transpose(bank[:, (c % 4) * P:(c % 4) * P + 68], G[0:68, 0, c * P:(c + 1) * P],
                                                        g.ident[0:68, 0:68])
                                full(last)
                            full(pe.transpose(use(n + 2)[0:NS, 0:68], G[0:68, 0, SEQ:T], g.ident[0:68, 0:68]))
                        elif name in ("vt0", "vt1"):
                            wait_evacuated(pe, w, i, TILES[w].index("v" + name[2]))
                            turned(n, VS)
                        elif name == "decay":
                            pe.wait_ge(s_sel, i + 1)
                            for b, (c0, m) in enumerate(PARTS):
                                last = pe.matmul(use(n + b)[:, 0:m], g.ones[0:H, :], TB[0:H, c0:c0 + m], start=True, stop=True)
                                if b < 2:
                                    full(last)
                            full(pe.matmul(RB(n + 2)[:, NS:NS + 2 * NC], g.ones[0:H, :], wcs[:, :], start=True, stop=True))
                        elif name == "scores":
                            pe.wait_ge(s_silu, i * 2 + 2)
                            scores(n, k, q)
                        elif name == "interq":
                            for b, (c0, m) in enumerate(PARTS):
                                full(pe.matmul(use(n + b)[:, 0:m], g.ones[32:32 + H, :], TB[32:32 + H, c0:c0 + m], start=True, stop=True))
                        elif name == "keys":
                            if isB(w):
                                pe.wait_ge(s_kt, i + 1)
                                turned(n, TB)
                            else:
                                turned(n, k)
                        elif name == "alpha":
                            pe.wait_ge(s_wah, i + 1)
                            for b, (c0, m) in enumerate(PARTS):
                                full(pe.matmul(use(n + b)[:, 0:m], walh[64:64 + RANK, :], rows[64:64 + RANK, c0:c0 + m], start=True, stop=True))
                        elif name.startswith("level"):
                            l = int(name[5:])
                            if l < NL - 1:
                                pe.wait_ge(s_qe, i * (NL - 1) + (l + 1))
                                pe.wait_ge(s_ke, i * (NL - 1) + (l + 1))
                                bank = use(n)
                                for c in range(NC):
                                    last = pe.matmul(bank[:, c * HP:(c + 1) * HP], KD[:, c * P:(c + 1) * P],
                                                     halves(QD[:, c * P:(c + 1) * P], l, 1), start=True, stop=True)
                                full(last)
                                if USES[name] == 2:
                                    bank = use(n + 1)
                                    apart(pe)
                                    full(pe.matmul(bank[0:NS, 0:NS], KD[:, SEQ:T], QD[:, SEQ:T], start=True, stop=True))
                            else:
                                scores(n, k, q)
                        elif name in CHAIN:
                            c = CHAIN.index(name)
                            if c == 0:
                                wait_read(pe, w, i, "keys")
                                apart(pe)
                                wait_read(pe, w, i, f"level{NL - 1}" if isB(w) else "scores")
                                apart(pe)
                                if isB(w):
                                    pe.wait_ge(s_qd, i + 1)
                                else:
                                    wait_read(pe, w, i, "interq")
                                    apart(pe)
                            full(pe.matmul(use(n)[:, 0:vw], KD[:, c * P:(c + 1) * P], v[:, c, 0:vw], start=True, stop=True))
                            bank = use(n + 1)
                            last = pe.matmul(bank[:, 0:vw], AT[:, c * P:(c + 1) * P], v[:, c, 0:vw], start=True, stop=(c == 0))
                            if c:
                                wait_read_use(pe, w, i, USE[w][CHAIN[c - 1]])
                                last = pe.matmul(bank[:, 0:vw], QD[:, c * P:(c + 1) * P], SS[:, (c - 1) % 2, 0:vw], start=False, stop=True)
                            full(last)
                        elif name == "sample_out":
                            pe.wait_ge(s_km, two(w, i) + 1)
                            pe.wait_ge(s_stl, two(w, i, 16) + 16)
                            bank = use(n)
                            apart(pe)
                            pe.matmul(bank[0:NS, 0:vw], AT[0:NS, SEQ:T], v[0:NS, NC, 0:vw], start=True, stop=False)
                            for b in range(NSEQ):
                                last = pe.matmul(bank[0:NS, 0:vw], QM[:, b, :], ST[:, b, 0:vw], start=False, stop=(b == NSEQ - 1))
                            full(last)
                        elif name in SAMPLE:
                            b = SAMPLE.index(name)
                            full(pe.matmul(use(n)[:, 0:vw], TB[0:NS, b * P:(b + 1) * P], v[0:NS, NC, 0:vw], start=True, stop=True))
                        elif name in ("turn0", "turn1"):
                            j = int(name[4])
                            pe.wait_ge(s_hn, two(w, i) + 1)
                            for b in range(2):
                                bank = use(n + b)
                                for c in range(4 * b, 4 * b + 4):
                                    last = pe.transpose(bank[:, (c % 4) * P:(c % 4 + 1) * P], v[:, c, j * P:(j + 1) * P], g.ident[:, :])
                                full(last)
                            bank = use(n + 2)
                            apart(pe)
                            full(pe.transpose(bank[:, 0:NS], HS[0:NS, j * P:(j + 1) * P], g.ident[0:NS, 0:NS]))
                        elif name.startswith("ada") and name[3] != "_":
                            m = two(w, i, 4) + int(name[3])
                            pe.wait_ge(s_adl, m * 16 + 16)
                            bank = use(n)
                            for kc in range(KC):
                                last = pe.matmul(bank[:, 0:NCOND], wad[:, kc, :], g.cT[:, kc, :], start=(kc == 0), stop=(kc == KC - 1))
                            full(last)
                run(pe, None, window)

            @block.scalar
            def _(act):
                def split_hi(w, i, l, h):
                    r, s, turns, before = half(w, i, l, h)
                    act.wait_ge(s_w[r], turns * 16 + (16 + (32 if r < 2 else 0)))
                    wait(act, s_used, before - (SPL - 1))
                    act.activation(Wh[:, s], raw[:, r], ACT.Copy).then_inc(s_hi, 1)

                def evacuate(w, i, l, c):
                    name = TILES[w][l]
                    b, _ = piece(w, i, l, c)
                    c0, n = span(c)
                    src = g.ps[b][:, 0:n]
                    wait_piece(act, w, i, l, c)
                    t = tile_index(w, i, l)
                    last_c = c == NPC - 1
                    cut = SEQ - c0 if last_c else n

                    conv = name in ("q", "k") and w in "SB"
                    if name == "small":
                        act.activation(M[0:H, 0, c0:c0 + n], src[0:H], ACT.Copy)
                        act.activation(M[0:H, 1, c0:c0 + n], src[32:32 + H], ACT.Copy)
                        last = act.activation(rows[64:64 + RANK, c0:c0 + n], src[64:64 + RANK], ACT.Copy)
                    elif conv:
                        if c == 0:
                            nth = (0 if w == "S" else i * 2 + 2) + (1 if name == "k" else 0)
                            wait(act, s_silu, nth)
                        last = act.activation(Z[:, W4 - 1 + c0:W4 - 1 + c0 + cut], src[:, 0:cut], ACT.Copy)
                        if last_c:
                            z = Z[:, ZP:ZN].rearrange("p (b t) -> p b t", t=ZS)[:, :, W4 - 1:ZS]
                            last = act.activation(z, src[:, cut:n].rearrange("p (b t) -> p b t", t=SLEN), ACT.Copy)
                    elif name in ("q", "k"):
                        last = act.activation((Q if name == "q" else K)[1][:, c0:c0 + n], src, ACT.Copy,
                                              scale=QSCALE if name == "q" else 1.0)
                    elif name[0] == "v":
                        last = act.activation(VS[:, c0:c0 + n], src, ACT.Copy)
                    elif name[0] == "o":
                        j = int(name[1])
                        if c == 0:
                            if isB(w):
                                wait_read(act, "A", i, f"turn{j}")
                                act.wait_ge(s_gate, BEGUN + i * 4 + (2 + j))
                            else:
                                act.wait_ge(s_sum, BEGUN + i * 2)
                        last = act.activation(G[:, j, c0:c0 + n], src, ACT.Tanh, scale=0.5)
                        if isB(w):
                            last = act.activation(TG[:, c0:c0 + n], src, ACT.Copy)
                    else:
                        if c == 0:
                            if isB(w):
                                act.wait_ge(s_gr, i * 2 + (int(name[1]) + 1))
                            else:
                                act.wait_ge(s_gate, BEGUN + two(w, i, 2) + int(name[1]))
                        last = act.activation(TG[:, c0:c0 + n], src, ACT.Tanh, scale=0.5)
                    last.then_inc(s_pfree[b], 1)

                split_hi("S", 0, 0, 0)
                def window(w, i):
                    hd = 1 if isB(w) else 0
                    vw = DV if isB(w) else VX
                    v = V[hd]

                    for x in TIMELINE[w]:
                        if x[0] == "piece":
                            _, l, h, c = x
                            nxt = after(w, i, l, h, 1)
                            if c == 0 and nxt:
                                split_hi(*nxt)
                            if h == 1:
                                evacuate(w, i, l, c)
                            continue
                        name = x[0]
                        n = USE[w].get(name)
                        if name == "rows":
                            act.wait_ge(s_r1, 1)
                            act.activation(TB[0:H, :], TB[0:H, :], ACT.Exp).then_inc(s_r2, 1)
                            act.wait_ge(s_r2, 1)
                            act.activation(TB[0:H, :], TB[0:H, :], ACT.Ln, bias=1.0).then_inc(s_r2, 1)
                        elif name == "rows_exp":
                            act.wait_ge(s_r3, 1)
                            act.activation(rows[32:32 + H, :], TB[0:H, :], ACT.Exp)
                            act.activation(G[32:32 + H, 0, :], VS[0:H, :], ACT.Exp)
                            act.activation(wcr[:, :], me[:, 3, :], ACT.Exp)
                            act.activation(G[64:64 + H, 0, :], TA[0:H, :], ACT.Exp, scale=-1.0).then_inc(s_rows, 1)
                            act.wait_ge(s_rows, 1)
                        elif name in ("silu_q", "silu_k"):
                            m = (0 if w == "S" else i * 2 + 2) + (2 if name[-1] == "k" else 1)
                            act.wait_ge(s_cv, m)
                            act.activation(Z[:, 0:ZO], CV[:, 0:ZO], ACT.Tanh, scale=0.5).then_inc(s_th, 1)
                        elif name in ("vt0", "vt1"):
                            j = int(name[2])
                            dst = V[0 if w in "SB" else 1]
                            for b in range(2):
                                wait_use(act, w, i, n + b)
                                act.activation(dst[:, 4 * b:4 * b + 4, j * P:(j + 1) * P],
                                               RB(n + b)[:, :].rearrange("p (c d) -> p c d", d=P), ACT.Copy).then_inc(free(n + b), 1)
                            wait_use(act, w, i, n + 2)
                            act.activation(dst[0:NS, NC, j * P:(j + 1) * P], RB(n + 2)[0:NS, 0:P], ACT.Copy).then_inc(free(n + 2), 1)
                        elif name == "decay":
                            act.wait_ge(s_warg, i + 1)
                            act.activation(TA[:, 0:SEQ], TA[:, 0:SEQ], ACT.Exp)
                            act.activation(TA[0:NS, SEQ:T], TA[0:NS, SEQ:T], ACT.Exp).then_inc(s_wexp, 1)
                        elif name == "alpha":
                            for b, (c0, m) in enumerate(PARTS):
                                wait_use(act, w, i, n + b)
                                last = act.activation(QD[:, c0:c0 + m], RB(n + b)[:, 0:m], ACT.Copy)
                                last.then_inc(free(n + b), 1)
                            act.wait_ge(s_nab, i + 1)
                            act.activation(TB[:, :], TB[:, :], ACT.Exp).then_inc(s_ln, 1)
                            act.wait_ge(s_ln, i * 2 + 1)
                            act.activation(TB[:, :], TB[:, :], ACT.Ln, bias=1.0).then_inc(s_ln, 1)
                        elif name == "sums":
                            level_exp(act, w, i, 0)
                        elif name.startswith("level"):
                            l = int(name[5:])
                            if l + 1 < NL - 1:
                                level_exp(act, w, i, l + 1)
                            elif l == NL - 1:
                                act.wait_ge(s_d, i * NL + NL)
                                act.activation(TB[:, :], TB[:, :], ACT.Exp, scale=1.0 / TAU)
                                act.activation(TA[:, :], TA[:, :], ACT.Exp, scale=1.0 / TAU).then_inc(s_E, 1)
                        elif name == "keys" and isB(w):
                            for b in range(2):
                                wait_use(act, w, i, n + b)
                                act.activation(KD[:, 512 * b:512 * b + 512], RB(n + b)[:, :], ACT.Copy).then_inc(free(n + b), 1)
                            wait_use(act, w, i, n + 2)
                            act.activation(KD[0:NS, SEQ:SEQ + P], RB(n + 2)[0:NS, 0:P], ACT.Copy).then_inc(free(n + 2), 1)
                        elif name in CHAIN or name == "sample_out":
                            c = CHAIN.index(name) if name in CHAIN else NC
                            u = n + 1 if name in CHAIN else n
                            m = P if c < NC else NS
                            dst = v[:, c, 0:vw] if c < NC else HS[0:NS, 0:vw]
                            wait_use(act, w, i, u)
                            act.activation(dst, RB(u)[0:m, 0:vw], ACT.Copy).then_inc(s_hc, 1)
                            act.wait_ge(s_hc, two(w, i, NT) + (c + 1))
                            act.activation(RB(u)[0:m, 0:DV], RB(u)[0:m, 0:DV], ACT.Square,
                                           accum_out=ssq[0:m, c:c + 1]).then_inc(free(u), 1)
                        elif name == "norm":
                            act.wait_ge(s_ms, BEGUN + two(w, i) + 1)
                            act.activation(ms[:, :], ms[:, :], ACT.Sqrt).then_inc(s_sq, 1)

                def level_exp(act, w, i, l):
                    hs = LEVELS[l]
                    top = T if hs <= SLEN // 2 else SEQ
                    act.wait_ge(s_d, i * NL + (l + 1))
                    e = TB[:, 0:top].rearrange("p (n w) -> p n w", w=2 * hs)
                    act.activation(e[:, :, hs:2 * hs], e[:, :, hs:2 * hs], ACT.Exp, scale=1.0 / TAU)
                    act.activation(e[:, :, 0:hs], e[:, :, 0:hs], ACT.Exp, scale=-1.0 / TAU).then_inc(s_E, 1)
                run(act, None, window)

            @block.gpsimd
            def _(pool):
                st = Steps(pool, s_pool)
                for buf, x in ((cols[:, :, :], 0.0), (G[:, 0, :], 0.0), (me[:, :, :], 0.0), (KD[:, SEQ:T], 0.0), (ssq[:, :], 1.0), (ms[:, :], 1.0)):
                    pool.memset(buf, x)
                pool.memset(den[:, :], 1.0).then_inc(s_init, 1)

                def split_lo(w, i, l, h):
                    _, s, _, before = half(w, i, l, h)
                    r = half(w, i, l, h)[0]
                    pool.wait_ge(s_hi, before + 1)
                    wait(pool, s_used, before - (SPL - 1))
                    pool.tensor_tensor(Wl[:, s], raw[:, r], Wh[:, s].bitcast(F32), ALU.subtract).then_inc(s_lo, 1)
                pool.nop().then_inc(s_sum, BEGUN)
                split_lo("S", 0, 0, 0)

                def window(w, i):
                    hd = 1 if isB(w) else 0
                    for x in TIMELINE[w]:
                        if x[0] == "piece":
                            _, l, h, c = x
                            nxt = after(w, i, l, h, 1)
                            if c == 0 and nxt:
                                split_lo(*nxt)
                            continue
                        name = x[0]
                        n = USE[w].get(name)
                        if name.startswith("level") and int(name[5:]) < NL - 1:
                            l = int(name[5:])
                            if l == 0:
                                wait_use(pool, "A", i, USE["A"]["alpha"])
                                apart(pool)
                                pool.memset(AT[:, :], 0.0).then_inc(s_at0, 1)
                            else:
                                wait_use(pool, w, i, n - 1)
                            pool.wait_ge(s_E, i * NL + (l + 1))
                            top = T if LEVELS[l] <= SLEN // 2 else SEQ
                            pool.tensor_tensor(halves(KD[:, 0:top], l, 0), halves(K[1][:, 0:top], l, 0), halves(TB[:, 0:top], l, 0),
                                               ALU.mult).then_inc(s_ke, 1)
                        elif name == "masked":
                            wait_read(pool, w, i, "keys")
                            if isB(w):
                                pool.wait_ge(s_qd, i + 1)
                            else:
                                wait_read(pool, w, i, "interq")
                            pool.tensor_tensor(QM[:, :, :], mid(QD[:, SEQ:T], NSEQ), g.seqrow[:, :, :], ALU.mult)
                            pool.tensor_tensor(TB[0:NS, 0:SEQ].rearrange("p (b d) -> p b d", b=NSEQ), mid(KD[0:NS, SEQ:SEQ + P], NSEQ),
                                               bc(g.seqcol[:, :].unsqueeze(2), P), ALU.mult).then_inc(s_km, 1)
                        elif name in ("turn0", "turn1") and w == "B":
                            j = int(name[4])
                            wait_read(pool, w, i, name)
                            pool.tensor_tensor(M[:, j, :], M[:, j, :], G[:, j, :], ALU.add).then_inc(s_sum, 1)
                run(pool, None, window)

            @block.vector
            def _(dve):
                per = g.dve_per
                st = Steps(dve, s_dve, per=per)
                dve.nop().then_inc(s_ms, BEGUN)
                dve.nop().then_inc(s_gate, BEGUN)
                link, did = st.link, st.did

                def conv(kt):
                    z = Z[:, ZP:ZN].rearrange("p (b t) -> p b t", t=ZS)
                    dve.memset(Z[:, 0:W4 - 1], 0.0)
                    dve.tensor_copy(z[:, :, 0:W4 - 1], g.sconvT[:, bass.ds(kt, 1), :].rearrange("p k (b j) -> p (k b) j", j=W4 - 1))
                    dve.tensor_copy(g.pk[:, bass.ds(kt, 1), 0:W4 - 1].rearrange("p k j -> p (k j)"), Z[:, SEQ:ZP])
                    link(dve.tensor_copy(g.pk[:, bass.ds(kt, 1), W4 - 1:KEEP].rearrange("p k (b j) -> p (k b) j", j=W4 - 1),
                                         z[:, :, SLEN:ZS]))
                    col = lambda v: g.vec[:, bass.ds(v + kt, 1)]
                    link(dve.tensor_scalar(CV[:, 0:ZO], Z[:, 0:ZO], col(V_CW), col(V_CB), ALU.mult, ALU.add))
                    did(dve.scalar_tensor_tensor(CV[:, 0:ZO], Z[:, 1:1 + ZO], col(V_CW + KC), CV[:, 0:ZO], ALU.mult, ALU.add))

                def taps(kt):
                    col = lambda v: g.vec[:, bass.ds(v + kt, 1)]
                    dve.wait_ge(s_dve, st.value())
                    link(dve.scalar_tensor_tensor(CV[:, 0:ZO], Z[:, 2:2 + ZO], col(V_CW + 2 * KC), CV[:, 0:ZO], ALU.mult, ALU.add))
                    dve.scalar_tensor_tensor(CV[:, 0:ZO], Z[:, 3:3 + ZO], col(V_CW + 3 * KC), CV[:, 0:ZO], ALU.mult, ALU.add).then_inc(s_cv, 1)

                def silu(m, dst, f):
                    dve.wait_ge(s_th, m)
                    link(dve.tensor_scalar(Z[:, 0:ZO], Z[:, 0:ZO], 1.0, 0.5 * f, ALU.add, ALU.mult))
                    dve.tensor_tensor(dst[:, 0:SEQ], Z[:, 0:SEQ], CV[:, 0:SEQ], ALU.mult)
                    tail = lambda v: v[:, ZP:ZN].rearrange("p (b t) -> p b t", t=ZS)[:, :, 0:SLEN]
                    dve.tensor_tensor(seqs(dst), tail(Z), tail(CV), ALU.mult).then_inc(s_silu, 1)

                def window(w, i):
                    hd = 1 if isB(w) else 0
                    vw = DV if isB(w) else VX
                    q, k, v = Q[hd], K[hd], V[hd]
                    if w == "A":
                        st.turn(i)
                    for x in TIMELINE[w]:
                        if x[0] == "piece":
                            continue
                        name = x[0]
                        n = USE[w].get(name)
                        if name == "rows":
                            rows_stage()
                        elif name == "rows_t":
                            for b in range(2):
                                wait_use(dve, w, i, n + b)
                                src = RB(n + b)[:, :].rearrange("p (c r) -> p c r", r=P)
                                for r in range(3):
                                    ins = dve.tensor_copy(cols[:, 4 * b:4 * b + 4, r * H:(r + 1) * H], src[:, :, 32 * r:32 * r + H])
                                ins.then_inc(free(n + b), 1)
                            wait_use(dve, w, i, n + 2)
                            for r in range(3):
                                ins = dve.tensor_copy(cols[0:NS, NC, r * H:(r + 1) * H], RB(n + 2)[0:NS, 32 * r:32 * r + H])
                            ins.then_inc(free(n + 2), 1)
                            dve.wait_ge(free(n + 2), 1)
                        elif name in ("conv_q", "conv_k"):
                            wait_evacuated(dve, w, i, TILES[w].index(name[-1]))
                            conv((4 if name[-1] == "k" else 0) + (0 if w == "S" else i + 1))
                        elif name in ("taps_q", "taps_k"):
                            taps((4 if name[-1] == "k" else 0) + (0 if w == "S" else i + 1))
                        elif name in ("silu_q", "silu_k"):
                            isk = name[-1] == "k"
                            m = (0 if w == "S" else i * 2 + 2) + (2 if isk else 1)
                            silu(m, (K if isk else Q)[0], 1.0 if isk else QSCALE)
                        elif name == "select":
                            one = g.ident[0:H, bass.ds(i, 1)]
                            dve.tensor_scalar(TB[0:H, :], rows[0:H, :], one, None, ALU.mult)
                            dve.tensor_scalar(TB[32:32 + H, :], rows[32:32 + H, :], g.ident[32:32 + H, bass.ds(i + 32, 1)], None, ALU.mult)
                            dve.tensor_copy(walh[64:64 + RANK, :], wal[64:64 + RANK, bass.ds(i * DK, DK)]).then_inc(s_wah, 1)
                            dve.tensor_scalar(wcs[:, :], wcr[:, :], one, None, ALU.mult).then_inc(s_sel, 1)
                            link(dve.tensor_copy(hcol[:, :, :], cols[:, :, :].rearrange("p c (q h) -> p c q h", h=H)[:, :, :, bass.ds(i, 1)]
                                                 .rearrange("p c q h -> p c (q h)")))
                        elif name == "decay":
                            for b in range(2):
                                wait_use(dve, w, i, n + b)
                                for c in range(4 * b, 4 * b + 4):
                                    ins = dve.scalar_tensor_tensor(TA[:, c * P:(c + 1) * P], RB(n + b)[:, (c % 4) * P:(c % 4 + 1) * P],
                                                                   hcol[:, c, 0:1], g.cmask[:, :], ALU.add, ALU.min)
                                ins.then_inc(free(n + b), 1)
                            wait_use(dve, w, i, n + 2)
                            dve.scalar_tensor_tensor(TA[0:NS, SEQ:T], RB(n + 2)[0:NS, 0:NS], hcol[0:NS, NC, 0:1], g.cmask_s[:, :],
                                                     ALU.add, ALU.min).then_inc(s_warg, 1)
                            dve.tensor_copy(sdec[:, :], RB(n + 2)[:, NS:NS + 2 * NC]).then_inc(free(n + 2), 1)
                        elif name == "scores":
                            dve.wait_ge(s_wexp, i + 1)
                            for b in range(2):
                                wait_use(dve, w, i, n + b)
                                dve.tensor_tensor(AT[:, 512 * b:512 * b + 512], RB(n + b)[:, :], TA[:, 512 * b:512 * b + 512],
                                                  ALU.mult).then_inc(free(n + b), 1)
                            wait_use(dve, w, i, n + 2)
                            dve.tensor_tensor(AT[0:NS, SEQ:T], RB(n + 2)[0:NS, 0:NS], TA[0:NS, SEQ:T], ALU.mult).then_inc(free(n + 2), 1)
                        elif name == "interq":
                            did(dve.memset(V[0][:, :, DV:VX], 1.0))
                            did(dve.tensor_copy(ST[:, :, DV:VX], g.n0T[:, :].rearrange("p (b h) -> p b h", h=H)[:, :, bass.ds(i, 1)]))
                            for b, (c0, m) in enumerate(PARTS):
                                wait_use(dve, w, i, n + b)
                                dve.tensor_tensor(QD[:, c0:c0 + m], RB(n + b)[:, 0:m], q[:, c0:c0 + m], ALU.mult).then_inc(free(n + b), 1)
                        elif name == "keys" and not isB(w):
                            for b in range(2):
                                wait_use(dve, w, i, n + b)
                                dve.tensor_tensor(KD[:, 512 * b:512 * b + 512].rearrange("p (c d) -> p c d", d=P),
                                                  RB(n + b)[:, :].rearrange("p (c d) -> p c d", d=P),
                                                  bc(hcol[:, 4 * b:4 * b + 4, 1:2], P), ALU.mult).then_inc(free(n + b), 1)
                            wait_use(dve, w, i, n + 2)
                            dve.tensor_scalar(KD[0:NS, SEQ:SEQ + P], RB(n + 2)[0:NS, 0:P], hcol[0:NS, NC, 1:2], None,
                                              ALU.mult).then_inc(free(n + 2), 1)
                        elif name == "alpha":
                            wait_read(dve, w, i, "alpha")
                            link(dve.tensor_scalar(QD[:, :], QD[:, :], g.vec[:, bass.ds(V_AL + i, 1)], None, ALU.add))
                            dve.scalar_tensor_tensor(TB[:, :], QD[:, :], -1.0, QD[:, :], ALU.mult, ALU.min).then_inc(s_nab, 1)
                        elif name == "sums":
                            dve.wait_ge(s_ln, i * 2 + 2)
                            link(dve.scalar_tensor_tensor(TB[:, :], QD[:, :], 0.0, TB[:, :], ALU.min, ALU.subtract))
                            link(dve.tensor_tensor_scan(TA[:, :], g.reset[:, :], TB[:, :], 0.0, ALU.mult, ALU.add))
                            level_diff(0, i)
                        elif name.startswith("level"):
                            l = int(name[5:])
                            if l < NL - 1:
                                top = T if LEVELS[l] <= SLEN // 2 else SEQ
                                dve.wait_ge(s_E, i * NL + (l + 1))
                                dve.tensor_tensor(halves(QD[:, 0:top], l, 1), halves(q[:, 0:top], l, 1), halves(TB[:, 0:top], l, 1),
                                                  ALU.mult).then_inc(s_qe, 1)
                                dve.wait_ge(s_qe, i * (NL - 1) + (l + 1))
                                dve.wait_ge(s_ke, i * (NL - 1) + (l + 1))
                                if l < NL - 2:
                                    level_diff(l + 1, i)
                                else:
                                    e, b = chunks(TB), chunks(TA)
                                    did(dve.tensor_tensor(e, bc(b[:, :, P - 1:P], P), b, ALU.subtract))
                                    e, b = seqs(TB), seqs(TA)
                                    dve.tensor_tensor(e, bc(b[:, :, SLEN - 1:SLEN], SLEN), b, ALU.subtract).then_inc(s_d, 1)
                            if l == 0:
                                dve.wait_ge(s_at0, i + 1)
                            if l < NL - 1:
                                hs = LEVELS[l]
                                right = halves(g.lmask[:, l, :], l, 1).unsqueeze(1).to_broadcast([P, NC, HP // hs, hs])
                                wait_use(dve, w, i, n)
                                apart(dve)
                                dve.copy_predicated(AT[:, 0:SEQ].rearrange("p (c n w) -> p c n w", c=NC, w=2 * hs)[:, :, :, hs:2 * hs], right,
                                                    RB(n)[:, :].rearrange("p (c n w) -> p c n w", c=NC, w=hs)).then_inc(free(n), 1)
                            else:
                                c4 = lambda v: v.rearrange("p (c t) -> p c t", t=P)
                                for b in range(2):
                                    wait_use(dve, w, i, n + b)
                                    apart(dve)
                                    dve.copy_predicated(c4(AT[:, 512 * b:512 * b + 512]), mid(g.lmask[:, l, :], 4),
                                                        c4(RB(n + b)[:, :])).then_inc(free(n + b), 1)
                            if l >= NL - 3:
                                m = n + USES[name] - 1
                                wait_use(dve, w, i, m)
                                apart(dve)
                                dve.copy_predicated(AT[0:NS, SEQ:T], g.lmask[0:NS, l, 0:NS], RB(m)[0:NS, 0:NS]).then_inc(free(m), 1)
                            wait_read(dve, w, i, name)
                            if l == NL - 1:
                                dve.wait_ge(s_E, i * NL + NL)
                                dve.tensor_tensor(TB[:, :], k[:, :], TB[:, :], ALU.mult).then_inc(s_kt, 1)
                                did(dve.tensor_copy(sdec[:, 0:NC], chunks(TA)[:, :, P - 1:P].rearrange("p c t -> p (c t)")))
                                did(dve.tensor_copy(sdec[:, NC:2 * NC], seqs(TA)[:, :, SLEN - 1:SLEN].rearrange("p c t -> p (c t)")))
                                dve.tensor_tensor(QD[:, :], q[:, :], TA[:, :], ALU.mult).then_inc(s_qd, 1)
                        elif name in CHAIN:
                            c = CHAIN.index(name)
                            wait_use(dve, w, i, n)
                            if c == 0:
                                ins = dve.tensor_copy(SS[:, 0, 0:vw], RB(n)[:, 0:vw])
                            else:
                                wait_read_use(dve, w, i, USE[w][CHAIN[c - 1]])
                                if c == 1:
                                    dve.wait_ge(s_sts, BEGUN + two(w, i, 32))
                                ins = dve.scalar_tensor_tensor(SS[:, c % 2, 0:vw], SS[:, (c - 1) % 2, 0:vw], sdec[:, c:c + 1],
                                                               RB(n)[:, 0:vw], ALU.mult, ALU.add)
                            ins.then_inc(free(n), 1)
                            if c == NC - 1 and not isB(w):
                                wait_read_use(dve, w, i, n)
                                did(dve.tensor_copy(g.nout[:, bass.ds(i, 1)], SS[:, 1, DV:VX]))
                        elif name in SAMPLE:
                            b = SAMPLE.index(name)
                            wait_use(dve, w, i, n)
                            if b == 0:
                                dve.wait_ge(s_stl, two(w, i, 16) + 16)
                            dve.scalar_tensor_tensor(ST[:, b, 0:vw], ST[:, b, 0:vw], sdec[:, NC + b:NC + b + 1], RB(n)[:, 0:vw],
                                                     ALU.mult, ALU.add).then_inc(free(n), 1)
                            if b == NSEQ - 1 and not isB(w):
                                wait_read_use(dve, w, i, n)
                                did(dve.tensor_copy(g.nout[:, H:].rearrange("p (b h) -> p b h", h=H)[:, :, bass.ds(i, 1)], ST[:, :, DV:VX]))
                        elif name == "norm":
                            wait_read(dve, w, i, "sample_out")
                            if not isB(w):
                                d = v[:, 0:NC, DV:VX].rearrange("p c o -> p (c o)")
                                did(dve.scalar_tensor_tensor(den[:, 0:NC], d, -1.0, d, ALU.mult, ALU.max))
                                d = HS[0:NS, DV:VX]
                                link(dve.scalar_tensor_tensor(den[0:NS, NC:NT], d, -1.0, d, ALU.mult, ALU.max))
                                link(dve.tensor_tensor(den[:, :], den[:, :], hcol[:, :, 2:3].rearrange("p c o -> p (c o)"), ALU.max))
                                link(dve.reciprocal(den[:, :], den[:, :]))
                                link(dve.tensor_tensor(ms[:, :], ssq[:, :], den[:, :], ALU.mult))
                                link(dve.tensor_tensor(ms[:, :], ms[:, :], den[:, :], ALU.mult))
                                dve.tensor_scalar(ms[:, :], ms[:, :], 1.0 / DV, EPS, ALU.mult, ALU.add).then_inc(s_ms, 1)
                            else:
                                dve.tensor_scalar(ms[:, :], ssq[:, :], 1.0 / DV, EPS, ALU.mult, ALU.add).then_inc(s_ms, 1)
                            dve.wait_ge(s_sq, two(w, i) + 1)
                            link(dve.reciprocal(scl[:, :], ms[:, :]))
                            if not isB(w):
                                link(dve.tensor_tensor(scl[:, :], scl[:, :], den[:, :], ALU.mult))
                            dve.tensor_tensor(v[:, 0:NC, 0:DV], v[:, 0:NC, 0:DV], bc(scl[:, 0:NC].unsqueeze(2), DV), ALU.mult)
                            dve.tensor_scalar(HS[0:NS, 0:DV], HS[0:NS, 0:DV], scl[0:NS, NC:NT], None, ALU.mult).then_inc(s_hn, 1)
                        elif name in ("gate_r0", "gate_r1"):
                            j = int(name[-1])
                            wait_evacuated(dve, w, i, TILES[w].index(f"o{j}"))
                            dve.scalar_tensor_tensor(G[:, j, :], G[:, j, :], 1.0, TG[:, :], ALU.add, ALU.mult).then_inc(s_gr, 1)
                        elif name in ("gate0", "gate1"):
                            j = int(name[-1])
                            wait_evacuated(dve, w, i, TILES[w].index(f"g{j}"))
                            gain = g.vec[:, bass.ds(i * 2 + ((V_HB if isB(w) else V_HA) + j), 1)]
                            link(dve.tensor_scalar(TG[:, :], TG[:, :], 1.0, gain, ALU.add, ALU.mult))
                            if isB(w):
                                dve.wait_ge(s_gr, i * 2 + (j + 1))
                                ins = dve.tensor_tensor(G[:, j, :], G[:, j, :], TG[:, :], ALU.mult)
                            else:
                                ins = dve.scalar_tensor_tensor(G[:, j, :], G[:, j, :], 1.0, TG[:, :], ALU.add, ALU.mult)
                            ins.then_inc(s_gate, 1)
                        elif name in ("turn0", "turn1"):
                            j = int(name[-1])
                            dve.wait_ge(s_gate, BEGUN + two(w, i, 2) + (j + 1))
                            if not isB(w) and j == 0:
                                dve.wait_ge(s_mst, BEGUN + i * 16)
                            for b, (c0, m) in enumerate(PARTS):
                                wait_use(dve, w, i, n + b)
                                dst = G if isB(w) else M
                                dve.tensor_tensor(dst[:, j, c0:c0 + m], RB(n + b)[:, 0:m], G[:, j, c0:c0 + m], ALU.mult).then_inc(free(n + b), 1)
                            if w == "L":
                                wait_read(dve, w, i, name)
                                dve.tensor_tensor(M[:, j, :], M[:, j, :], G[:, j, :], ALU.add).then_inc(s_sum, 1)
                        elif name.startswith("ada") and name[3] != "_":
                            m = two(w, i, 4) + (int(name[3]) + 2 * KC)
                            wait_use(dve, w, i, n)
                            dve.tensor_scalar(g.ada[:, bass.ds(m, 1), :].rearrange("p o c -> p (o c)"), RB(n)[:, 0:NCOND],
                                              g.vec[:, bass.ds(m, 1)], None, ALU.add).then_inc(free(n), 1)
                    if per and w == "B" and st.n != per:
                        raise ValueError(f"set dve_per to {st.n}")

                def level_diff(l, i):
                    hs = LEVELS[l]
                    top = T if hs <= SLEN // 2 else SEQ
                    b = TA[:, 0:top].rearrange("p (n w) -> p n w", w=2 * hs)
                    dve.tensor_tensor(TB[:, 0:top].rearrange("p (n w) -> p n w", w=2 * hs), b, bc(b[:, :, hs - 1:hs], 2 * hs),
                                      ALU.subtract).then_inc(s_d, 1)

                def rows_stage():
                    I, X, LF, B_, MM = M[0:H, 0, :], M[0:H, 1, :], AT[0:H, :], QD[0:H, :], TA[0:H, :]
                    wait_evacuated(dve, "S", 0, 0)
                    dve.wait_ge(s_small, 64)
                    dve.wait_ge(s_init, 1)
                    did(dve.tensor_scalar(I, I, bif[:, 0:1], None, ALU.add))
                    link(dve.tensor_scalar(X, X, bif[:, 1:2], None, ALU.add))
                    dve.scalar_tensor_tensor(TB[0:H, :], X, -1.0, X, ALU.mult, ALU.min).then_inc(s_r1, 1)
                    dve.wait_ge(s_r2, 2)
                    link(dve.scalar_tensor_tensor(LF, X, 0.0, TB[0:H, :], ALU.min, ALU.subtract))
                    did(dve.tensor_tensor_scan(B_, g.reset[0:H, :], LF, 0.0, ALU.mult, ALU.add))
                    did(dve.tensor_tensor_scan(MM[:, 0:SEQ], LF[:, 0:SEQ], I[:, 0:SEQ], 0.0, ALU.add, ALU.max))
                    for b in range(NSEQ):
                        r = slice(SEQ + b * SLEN, SEQ + (b + 1) * SLEN)
                        did(dve.tensor_tensor_scan(MM[:, r], LF[:, r], I[:, r], m0[:, b:b + 1], ALU.add, ALU.max))
                    dve.wait_ge(s_dve, st.value())
                    ends = lambda v: (chunks(v)[:, :, P - 1:P].rearrange("p c t -> p (c t)"), seqs(v)[:, :, SLEN - 1:SLEN].rearrange("p c t -> p (c t)"))
                    for r, v in ((1, MM), (2, B_)):
                        for j, e in enumerate(ends(v)):
                            did(dve.tensor_copy(me[:, r, j * NC:(j + 1) * NC], e))
                    did(dve.tensor_copy(me[:, 0, NC:2 * NC], m0[:, :]))
                    dve.wait_ge(s_dve, st.value())
                    did(dve.tensor_copy(me[:, 0, 1:NC], me[:, 1, 0:NC - 1]))
                    did(dve.tensor_tensor(me[:, 3, :], me[:, 2, :], me[:, 1, :], ALU.subtract))
                    did(dve.tensor_tensor(rows[0:H, :], B_, MM, ALU.subtract))
                    did(dve.tensor_tensor(G[0:H, 0, :], I, B_, ALU.subtract))
                    dve.wait_ge(s_dve, st.value())
                    for f, col in ((chunks, slice(0, NC)), (seqs, slice(NC, 2 * NC))):
                        m = P if f is chunks else SLEN
                        did(dve.tensor_tensor(f(TB[0:H, :]), f(rows[0:H, :]), bc(me[:, 0, col].unsqueeze(2), m), ALU.add))
                        did(dve.tensor_tensor(f(VS[0:H, :]), f(G[0:H, 0, :]), bc(me[:, 3, col].unsqueeze(2), m), ALU.add))
                    dve.wait_ge(s_dve, st.value())
                    dve.tensor_tensor(me[:, 3, :], me[:, 3, :], me[:, 0, :], ALU.add).then_inc(s_r3, 1)
                run(dve, None, window)


NBLK = FT // 2


def ffn_phase(nc, g, a, loops=True):
    with ExitStack() as ctx:
        sb = lambda n, s, d=F32: ctx.enter_context(nc.sbuf_tensor(n, s, d))
        sem = lambda n: ctx.enter_context(nc.semaphore(n))
        RING = 4
        raw = g.raw
        Wh = sb("f_hi", [P, RING, 4, P], F32R)
        Wl = sb("f_lo", [P, RING, 4, P], F32R)
        X = sb("x_t", [P, KC, T])
        NXR = 4
        OT = sb("y_rows", [P, NXR, D])
        SQ, SQT, TH, SG, AC = (g.early[:, m, 0:T] for m in range(NEARLY))
        Ah = sb("act_hi", [P, 2, 2, T], F32R)
        Al = sb("act_lo", [P, 2, 2, T], F32R)
        small = sb("norm_small", [P, 4, NT])
        am = sb("norm2_mult", [P, KC, NCOND])
        stm = sb("sample_temp", [P, NS])
        co = OT[0:KEEP, 0, :]
        stn = sb("n_rows_out", [H * NCOND, P])
        fss = sb("final_small", [P, NT, 4])
        GF = SQT

        def mixed(m):
            return g.early[:, m, 0:T] if m < NEARLY else Ah[:, (m - NEARLY) // 2, (m - NEARLY) % 2, :].bitcast(F32)

        s_w = [sem(f"f_w_loaded{n}") for n in range(RING)]
        s_hi, s_lo, s_used = sem("f_hi_made"), sem("f_lo_made"), sem("f_used")
        s_piece = sem("f_pieces_full")
        s_pf = [sem(f"f_bank_free{n}") for n in range(4)]
        s_ml, s_xl = [sem(f"mix_loaded{m}") for m in range(NEARLY, KC)], [sem(f"x_loaded{m}") for m in range(4)]
        s_mh, s_mlo, s_mlv = sem("mix_hi"), sem("mix_lo"), sem("mix_lo_by_vector")
        s_sq, s_sum, s_ms, s_rt, s_rd, s_rb = sem("squares_summed"), sem("norm2_sums"), sem("norm2_ms"), sem("norm2_sqrt"), sem("norm2_rows"), sem("norm2_bcast")
        s_sql, s_row, s_rowc = sem("last_squares"), sem("norm2_row"), sem("norm2_row_copied")
        s_h, s_hh, s_hl = sem("h2_ready"), sem("h2_hi"), sem("h2_lo")
        s_th, s_ah, s_al = sem("tanh_ready"), sem("act_hi_made"), sem("act_lo_made")
        s_co, s_cc, s_out = sem("states_turned"), sem("states_copied"), sem("stored")
        s_gf = sem("final_gain")
        s_y = [sem(f"y_stored{m}") for m in range(NXR)]
        s_stm = sem("samples_gated")
        s_ft, s_fs, s_fm, s_fr, s_fo = sem("final_turned"), sem("final_ssq"), sem("final_ms"), sem("final_sqrt"), sem("final_rows")
        s_dve, s_pool = sem("f_dve_chain"), sem("f_pool_chain")

        w_out = a["w_out"][0].rearrange("(k p) n -> p k n", p=P)
        w_gate = a["w_ffn_gate"][0].rearrange("(k p) n -> p k n", p=P)
        w_up = a["w_ffn_up"][0].rearrange("(k p) n -> p k n", p=P)
        w_down = a["w_ffn_down"][0]
        LOOP = (NBLK - 1) // 2

        HALVES = {"out": 2, "proj": 8, "down": 4}
        PIECES = {"out": 3, "proj": 12, "down": 24}
        SIGNAL = {"out": 2, "proj": 8, "down": 22}

        class Place:
            def __init__(self, j, steps_before, in_turn):
                tot = lambda d, names: sum(d[x] for x in names)
                pre = ["out"] * KC + ["proj"]
                turn = ["proj", "down"] * 2
                n = lambda d: (tot(d, turn), tot(d, (pre if in_turn is not None else steps_before)) + tot(d, turn[:in_turn or 0]))
                self.j = j
                self.halves, self.pieces, self.fulls = n(HALVES), n(PIECES), n(SIGNAL)

            def half(self, k):
                per, base = self.halves
                s, turns = static(self.j, per, base + k, RING)
                return s, turns, self.j * per + (base + k)

            def piece(self, k):
                per, base = self.pieces
                return static(self.j, per, base + k, 4)

            def full(self, k):
                per, base = self.fulls
                return self.j * per + (base + k)

        def out_place(n):
            return Place(0, ["out"] * n, None)

        def run(engine, step):
            for n in range(KC):
                step("out", n, 0, out_place(n))
            step("norm2", 0, 0, None)
            step("proj", 0, 0, Place(0, ["out"] * KC, None))

            def turn(j):
                step("proj", j * 2 + 1, 1, Place(j, None, 0))
                step("down", j * 2, 0, Place(j, None, 1))
                step("proj", j * 2 + 2, 0, Place(j, None, 2))
                step("down", j * 2 + 1, 1, Place(j, None, 3))
            if loops:
                with engine.Fori(0, LOOP) as j:
                    turn(j)
            else:
                for j in range(LOOP):
                    turn(j)
            step("down", NBLK - 1, 0, Place(LOOP, None, 0))

        def source(kind, b, k):
            if kind == "out":
                return w_out[:, 4 * k:4 * k + 4, bass.ds(b * P, P)]
            if kind == "proj":
                t, h = k // 2, k % 2
                src = w_gate if t % 2 == 0 else w_up
                return src[:, 4 * h:4 * h + 4, bass.ds(b * (2 * P) + (t // 2) * P, P)]
            n0, f = k // 2, k % 2
            rows = w_down[bass.ds(b * (2 * P) + f * P, P), 512 * n0:512 * n0 + 512]
            return rows.rearrange("p (n c) -> p n c", c=P)

        def span(c):
            return c * PC, PC

        def ahead(split, pl, t):
            for k in (2 * t, 2 * t + 1):
                split(pl, k)

        def is_last(b):
            return isinstance(b, int) and b == NBLK - 1

        def wait_full(e, kind, pl, k):
            if kind == "down":
                nh, r = k // 12, k % 12
                if r == 11:
                    e.wait_ge(s_used, pl.half(2 * nh + 1)[2] + 1)
                else:
                    e.wait_ge(s_piece, pl.full(11 * nh + r) + 1)
            else:
                t, c = k // 3, k % 3
                if c == 2:
                    e.wait_ge(s_used, pl.half(2 * t + 1)[2] + 1)
                else:
                    e.wait_ge(s_piece, pl.full(2 * t + c) + 1)

        MISC = g.ps[4:8]
        ENDB = g.ps[4:8] + g.ps[0:4]
        NE = len(ENDB) // 2
        PARTS = [(0, 512), (512, 512), (SEQ, NS)]
        seqv = lambda v: v.rearrange("p (b t) -> p b t", t=SLEN)

        with nc.Block() as block:

            @block.sync
            def _(sp):
                for k in range(2):
                    sp.dma_start(raw[:, k], source("out", 0, k)).then_inc(s_w[k], 16)
                for m in range(NEARLY, KC):
                    sp.dma_start(mixed(m), g.mix_d[:, m, :]).then_inc(s_ml[m - NEARLY], 16)
                for k in range(2):
                    sp.dma_start(raw[:, 2 + k], source("out", 1, k)).then_inc(s_w[2 + k], 16)
                for m in range(4):
                    sp.dma_start(X[:, 2 * m:2 * m + 2, :], g.x_d[:, 2 * m:2 * m + 2, :]).then_inc(s_xl[m], 16)

                def step(kind, b, par, pl):
                    if kind == "norm2":
                        return
                    if kind == "out" and b == 1:
                        sp.wait_ge(s_cc, 2)
                        sp.dma_start(a["conv_p"].rearrange("o b j c -> (o b j) c"), co[0:W4 - 1, :]).then_inc(s_out, 16)
                        sp.dma_start(a["conv_s"].rearrange("o b j c -> (o b j) c"), co[W4 - 1:KEEP, :]).then_inc(s_out, 16)
                        sp.dma_start(a["n_p"].rearrange("o b h d -> (o b h) d"), stn[0:H, :]).then_inc(s_out, 16)
                        sp.dma_start(a["n_s"].rearrange("o b h d -> (o b h) d"), stn[H:H * NCOND, :]).then_inc(s_out, 16)
                    for k in range(HALVES[kind]):
                        if kind == "out" and b < 2:
                            continue
                        s, turns, before = pl.half(k)
                        wait(sp, s_lo, before - (RING - 1))
                        sp.dma_start(raw[:, s], source(kind, b, k)).then_inc(s_w[s], 16)
                run(sp, step)
                gf = a["g_final"].unsqueeze(0).to_broadcast([P, D])
                sp.wait_ge(s_hl, KC)
                sp.dma_start(GF[:, 0:D], gf).then_inc(s_gf, 16)
                for t in range(NT):
                    sp.wait_ge(s_fo, t + 1)
                    if t < NC:
                        sp.dma_start(a["y_prompt"][0, t * P:(t + 1) * P, :], OT[:, t % NXR, 0:D]).then_inc(s_y[t % NXR], 16)
                    else:
                        sp.dma_start(a["y_sample"].rearrange("b t d -> (b t) d"), OT[0:NS, t % NXR, 0:D]).then_inc(s_y[t % NXR], 16)
                sp.wait_ge(s_out, 16 * 4)
                for m in range(NXR):
                    sp.wait_ge(s_y[m], 16 * len(range(m, NT, NXR)))

            @block.tensor
            def _(pe):
                def tile3(pl, t, mix=False, first=False):
                    for h in range(2):
                        s, _, before = pl.half(2 * t + h)
                        pe.wait_ge(s_lo, before + 1)
                        if mix:
                            pe.wait_ge(s_mlo, len([m for m in range(4 * h + 4) if m % 3 == 1]))
                            pe.wait_ge(s_mlv, len([m for m in range(4 * h + 4) if m % 3 != 1]))
                        if first:
                            pe.wait_ge(s_hl, 4 * h + 4)
                        for c in range(NPC):
                            bnk, turns = pl.piece(3 * t + c)
                            if h == 0:
                                wait(pe, s_pf[bnk], turns)
                            c0, n = span(c)
                            for kk in range(4):
                                for m, (x, y) in enumerate(((Wh, g.Hh), (Wh, g.Hl), (Wl, g.Hh))):
                                    last = pe.matmul(g.ps[bnk][:, 0:n], x[:, s, kk, :], y[:, 4 * h + kk, c0:c0 + n],
                                                     start=(h == 0 and kk == 0 and m == 0), stop=(h == 1 and kk == 3 and m == 2))
                            if c == NPC - 1:
                                last.then_inc(s_used, 1)
                            elif h == 1:
                                last.then_inc(s_piece, 1)

                def step(kind, b, par, pl):
                    if kind == "out":
                        tile3(pl, 0, mix=(b == 0))
                    elif kind == "proj":
                        for t in range(4):
                            tile3(pl, t, first=(t == 0 and isinstance(b, int) and b == 0))
                    elif kind == "down":
                        pe.wait_ge(s_al, b * 6 + 6)
                        for nh in range(2):
                            sl = []
                            for f in range(2):
                                s, _, before = pl.half(2 * nh + f)
                                pe.wait_ge(s_lo, before + 1)
                                sl.append(s)
                            for r in range(12):
                                n, c = r // 3, r % 3
                                bnk, turns = pl.piece(12 * nh + r)
                                wait(pe, s_pf[bnk], turns)
                                c0, w = span(c)
                                for f in range(2):
                                    for m, (x, y) in enumerate(((Wh, Ah), (Wh, Al), (Wl, Ah))):
                                        last = pe.matmul(g.ps[bnk][:, 0:w], x[:, sl[f], n, :], y[:, par, f, c0:c0 + w],
                                                         start=(f == 0 and m == 0), stop=(f == 1 and m == 2))
                                if r == 11:
                                    last.then_inc(s_used, 2)
                                else:
                                    last.then_inc(s_piece, 1)
                    elif kind == "norm2":
                        pe.wait_ge(s_sq, KC - 1)
                        pe.wait_ge(s_sql, 1)
                        pe.wait_ge(s_cc, 2)
                        for b, (c0, m) in enumerate(PARTS):
                            pe.matmul(MISC[b][0:1, 0:m], g.ones[:, 0:1], SQ[:, c0:c0 + m], start=True, stop=False)
                            pe.matmul(MISC[b][0:1, 0:m], g.ones[:, 0:1], SG[:, c0:c0 + m], start=False, stop=True).then_inc(s_row, 1)
                        pe.wait_ge(s_rowc, len(PARTS))
                        for t in range(NT):
                            n = P if t < NC else NS
                            last = pe.transpose(MISC[3][0:n, 64 + 2 * t:65 + 2 * t], TH[0:1, t * P:t * P + n], g.ident[0:1, 0:1])
                        last.then_inc(s_sum, 1)
                        pe.wait_ge(s_rd, 1)
                        for b, (c0, m) in enumerate(PARTS):
                            n = P if b < 2 else NS
                            pe.matmul(MISC[b][:, 0:m], g.ones[0:n, :], SQ[0:n, c0:c0 + m], start=True, stop=True).then_inc(s_rb, 1)

                for half_ in range(2):
                    for k in range(4):
                        kk = 4 * half_ + k
                        last = pe.transpose(MISC[half_][0:KEEP, k * P:(k + 1) * P], g.pk[:, kk, :], g.ident[:, :])
                pe.transpose(MISC[2][0:H * NCOND, 0:P], g.nout[:, :], g.ident[:, :]).then_inc(s_co, 1)
                run(pe, step)
                lastp = Place(LOOP, None, 0)
                bnk, turns = lastp.piece(23)
                pe.wait_ge(s_pf[bnk], turns + 1)
                for t in range(NT):
                    n = P if t < NC else NS
                    for b in range(2):
                        if t >= NE and b == 0:
                            pe.wait_ge(s_fo, t - NE + 1)
                        for k in range(4):
                            last = pe.transpose(ENDB[2 * (t % NE) + b][0:n, k * P:(k + 1) * P], X[:, 4 * b + k, t * P:t * P + n], g.ident[:, :])
                        last.then_inc(s_ft, 1)

            @block.scalar
            def _(act):
                def hi(pl, k):
                    s, turns, before = pl.half(k)
                    act.wait_ge(s_w[s], turns * 16 + 16)
                    wait(act, s_used, before - (RING - 1))
                    act.activation(Wh[:, s], raw[:, s], ACT.Copy).then_inc(s_hi, 1)

                def step(kind, b, par, pl):
                    if kind == "out":
                        ahead(hi, pl, 1)
                    elif kind == "norm2":
                        for b, (c0, m) in enumerate(PARTS):
                            act.wait_ge(s_row, b + 1)
                            act.activation(TH[0:1, c0:c0 + m], MISC[b][0:1, 0:m], ACT.Copy).then_inc(s_rowc, 1)
                        act.wait_ge(s_ms, 1)
                        act.activation(small[:, 1, :], small[:, 0, :], ACT.Sqrt).then_inc(s_rt, 1)
                        for k in range(KC):
                            act.wait_ge(s_h, k + 1)
                            act.activation(g.Hh[:, k, :], (SQT, TH, SG)[k % 3][:, :], ACT.Copy).then_inc(s_hh, 1)
                    elif kind == "proj":
                        for t in range(4):
                            ahead(hi, pl, t + 1)
                            if t % 2:
                                up(b, t // 2, par, pl)
                            else:
                                gate(b, t // 2, pl)
                    else:
                        ahead(hi, pl, 1)
                        if not is_last(b):
                            ahead(hi, pl, 2)

                def gate(b, f, pl):
                    for c in range(NPC):
                        wait_full(act, "proj", pl, 6 * f + c)
                        bnk, _ = pl.piece(6 * f + c)
                        c0, w = span(c)
                        act.activation(TH[:, c0:c0 + w], g.ps[bnk][:, 0:w], ACT.Tanh, scale=0.5).then_inc(s_th, 1)

                def up(b, f, par, pl):
                    for c in range(NPC):
                        bnk, turns = pl.piece(6 * f + 3 + c)
                        act.wait_ge(s_pf[bnk], turns + 1)
                        c0, w = span(c)
                        act.activation(Ah[:, par, f, c0:c0 + w], AC[:, c0:c0 + w], ACT.Copy).then_inc(s_ah, 1)

                for m in range(KC):
                    if m == 2:
                        ahead(hi, out_place(0), 0)
                    if m == 0:
                        act.wait_ge(g.s_early, 16)
                    if m >= NEARLY:
                        act.wait_ge(s_ml[m - NEARLY], 16)
                    act.activation(g.Hh[:, m, :], mixed(m), ACT.Copy).then_inc(s_mh, 1)
                run(act, step)
                for t in range(NT + 1):
                    n = P if t < NC else NS
                    for b in range(2):
                        if t < NT:
                            act.wait_ge(s_ft, 2 * t + b + 1)
                            if 2 * t + b:
                                act.wait_ge(s_fs, 2 * t + b)
                            act.activation(TH[0:n, 0:512], ENDB[2 * (t % NE) + b][0:n, :], ACT.Square,
                                           accum_out=fss[0:n, t, b:b + 1]).then_inc(s_fs, 1)
                    if t:
                        act.wait_ge(s_fm, t)
                        act.activation(fss[:, t - 1, 2:3], fss[:, t - 1, 2:3], ACT.Sqrt).then_inc(s_fr, 1)

            @block.gpsimd
            def _(pool):
                def lo(pl, k):
                    s, _, before = pl.half(k)
                    pool.wait_ge(s_hi, before + 1)
                    wait(pool, s_used, before - (RING - 1))
                    pool.tensor_tensor(Wl[:, s], raw[:, s], Wh[:, s].bitcast(F32), ALU.subtract).then_inc(s_lo, 1)

                def squares(n):
                    bnk, turns = out_place(n).piece(2)
                    pool.wait_ge(s_pf[bnk], turns + 1)
                    if n == 0:
                        pool.tensor_tensor(SQ[:, :], X[:, 0, :], X[:, 0, :], ALU.mult).then_inc(s_sq, 1)
                    else:
                        pool.wait_ge(s_sq, n)
                        st.link(pool.tensor_tensor(SQT[:, :], X[:, n, :], X[:, n, :], ALU.mult))
                        pool.tensor_tensor(SQ[:, :], SQ[:, :], SQT[:, :], ALU.add).then_inc(s_sq, 1)

                def step(kind, b, par, pl):
                    if kind == "out":
                        ahead(lo, pl, 1)
                        if b:
                            squares(b - 1)
                    elif kind == "norm2":
                        for k in range(KC):
                            pool.wait_ge(s_hh, k + 1)
                            pool.tensor_tensor(g.Hl[:, k, :], (SQT, TH, SG)[k % 3][:, :], g.Hh[:, k, :].bitcast(F32), ALU.subtract).then_inc(s_hl, 1)
                    elif kind == "proj":
                        for t in range(4):
                            ahead(lo, pl, t + 1)
                            if t % 2:
                                n = b * 6 + 3 * (t // 2)
                                for c in range(NPC):
                                    pool.wait_ge(s_ah, n + (c + 1))
                                    c0, w = span(c)
                                    pool.tensor_tensor(Al[:, par, t // 2, c0:c0 + w], AC[:, c0:c0 + w],
                                                       Ah[:, par, t // 2, c0:c0 + w].bitcast(F32), ALU.subtract).then_inc(s_al, 1)
                    else:
                        ahead(lo, pl, 1)
                        if not is_last(b):
                            ahead(lo, pl, 2)
                st = Steps(pool, s_pool)
                ahead(lo, out_place(0), 0)
                for m in range(KC):
                    if m % 3 == 1:
                        pool.wait_ge(s_mh, m + 1)
                        pool.tensor_tensor(g.Hl[:, m, :], mixed(m), g.Hh[:, m, :].bitcast(F32), ALU.subtract).then_inc(s_mlo, 1)
                run(pool, step)

            @block.vector
            def _(dve):
                st = Steps(dve, s_dve)
                link, did = st.link, st.did

                def step(kind, b, par, pl):
                    if kind == "out":
                        if b % 2 == 0:
                            dve.wait_ge(s_xl[b // 2], 16)
                        for c in range(NPC):
                            if c == NPC - 1:
                                samples("out", pl, c, b, 2 * KC, b + 1)
                            add_prompt("out", pl, c, b, c, 2 * KC)
                    elif kind == "norm2":
                        dve.wait_ge(s_stm, 2 * KC)
                        bnk, turns = out_place(KC - 1).piece(NPC - 1)
                        dve.wait_ge(s_pf[bnk], turns + 1)
                        dve.tensor_tensor(SG[:, :], X[:, KC - 1, :], X[:, KC - 1, :], ALU.mult).then_inc(s_sql, 1)
                        dve.wait_ge(s_sum, 1)
                        sums = MISC[3][:, 64:64 + 2 * NT].rearrange("p (t o) -> p t o", o=2)
                        dve.tensor_scalar(small[:, 0, 0:NC], sums[:, 0:NC, 0], 1.0 / D, EPS, ALU.mult, ALU.add)
                        dve.tensor_scalar(small[0:NS, 0, NC:NT], sums[0:NS, NC:NT, 0], 1.0 / D, EPS, ALU.mult, ALU.add).then_inc(s_ms, 1)
                        link(dve.scalar_tensor_tensor(am[:, :, :], g.ada[:, 4 * KC:5 * KC, :], 1.0,
                                                      bc(g.vec[:, V_G2:V_G2 + KC].unsqueeze(2), NCOND), ALU.add, ALU.mult))
                        dve.wait_ge(s_rt, 1)
                        link(dve.reciprocal(small[:, 2, :], small[:, 1, :]))
                        did(dve.tensor_tensor(SQ[:, 0:SEQ].rearrange("p (c t) -> p c t", t=P), mid(g.ident[:, :], NC),
                                              bc(small[:, 2, 0:NC].unsqueeze(2), P), ALU.mult))
                        dve.tensor_scalar(SQ[0:NS, SEQ:T], g.ident[0:NS, 0:NS], small[0:NS, 2, NC:NT], None, ALU.mult).then_inc(s_rd, 1)
                        dve.wait_ge(s_rb, len(PARTS))
                        for k in range(KC):
                            t = (SQT, TH, SG)[k % 3]
                            if k >= 3:
                                dve.wait_ge(s_hl, k - 2)
                            for p in range(2):
                                st.did(dve.scalar_tensor_tensor(t[:, 512 * p:512 * p + 512], X[:, k, 512 * p:512 * p + 512], am[:, k, 0:1],
                                                                MISC[p][:, :], ALU.mult, ALU.mult))
                            v = seqv(t[:, SEQ:T])
                            link(dve.tensor_tensor(t[:, SEQ:T], X[:, k, SEQ:T], MISC[2][:, 0:NS], ALU.mult))
                            link(dve.tensor_tensor(v, v, bc(am[:, k, 1:NCOND].unsqueeze(2), SLEN), ALU.mult))
                            dve.tensor_scalar(t[:, 0:SEQ], t[:, 0:SEQ], g.ada[:, 3 * KC + k, 0:1], None, ALU.add)
                            dve.tensor_tensor(v, v, bc(g.ada[:, 3 * KC + k, 1:NCOND].unsqueeze(2), SLEN), ALU.add).then_inc(s_h, 1)
                    elif kind == "proj":
                        for f in range(2):
                            n = b * 6 + 3 * f
                            for c in range(NPC):
                                c0, w = span(c)
                                bnk, _ = pl.piece(6 * f + c)
                                dve.wait_ge(s_th, n + (c + 1))
                                dve.scalar_tensor_tensor(SG[:, c0:c0 + w], TH[:, c0:c0 + w], 1.0, g.ps[bnk][:, 0:w],
                                                         ALU.add, ALU.mult).then_inc(s_pf[bnk], 1)
                            for c in range(NPC):
                                c0, w = span(c)
                                bnk, _ = pl.piece(6 * f + 3 + c)
                                gb, gt = pl.piece(6 * f + c)
                                wait_full(dve, "proj", pl, 6 * f + 3 + c)
                                dve.wait_ge(s_pf[gb], gt + 1)
                                wait(dve, s_al, n - 3 + (c + 1))
                                dve.scalar_tensor_tensor(AC[:, c0:c0 + w], SG[:, c0:c0 + w], 0.5, g.ps[bnk][:, 0:w],
                                                         ALU.mult, ALU.mult).then_inc(s_pf[bnk], 1)
                    else:
                        for k in range(24):
                            n, c = 4 * (k // 12) + k % 12 // 3, k % 3
                            if c == NPC - 1:
                                samples("down", pl, k, n, 5 * KC, b * KC + (KC + n + 1))
                            add_prompt("down", pl, k, n, c, 5 * KC)

                def add_prompt(kind, pl, k, n, c, vec):
                    wait_full(dve, kind, pl, k)
                    bnk, _ = pl.piece(k)
                    c0, w = span(c)
                    m = min(w, SEQ - c0)
                    dve.scalar_tensor_tensor(X[:, n, c0:c0 + m], g.ps[bnk][:, 0:m], g.ada[:, vec + n, 0:1], X[:, n, c0:c0 + m],
                                             ALU.mult, ALU.add).then_inc(s_pf[bnk], 1)

                def samples(kind, pl, k, n, vec, count):
                    wait_full(dve, kind, pl, k)
                    bnk, _ = pl.piece(k)
                    wait(dve, s_stm, count * 2 - 2)
                    dve.tensor_tensor(seqv(stm[:, :]), seqv(g.ps[bnk][:, PC - NS:PC]), bc(g.ada[:, vec + n, 1:NCOND].unsqueeze(2), SLEN),
                                      ALU.mult).then_inc(s_stm, 1)
                    dve.wait_ge(s_stm, count * 2 - 1)
                    dve.tensor_tensor(X[:, n, SEQ:T], X[:, n, SEQ:T], stm[:, :], ALU.add).then_inc(s_stm, 1)

                def rows_out(t):
                    n = P if t < NC else NS
                    dve.wait_ge(s_fr, t + 1)
                    link(dve.reciprocal(fss[:, t, 3:4], fss[:, t, 2:3]))
                    if t == 0:
                        dve.wait_ge(s_out, 16 * 4)
                    if t >= NXR:
                        dve.wait_ge(s_y[t % NXR], 16 * (t // NXR))
                    for b in range(2):
                        ins = dve.scalar_tensor_tensor(OT[0:n, t % NXR, 512 * b:512 * b + 512], ENDB[2 * (t % NE) + b][0:n, :], fss[0:n, t, 3:4],
                                                       GF[0:n, 512 * b:512 * b + 512], ALU.mult, ALU.mult)
                    ins.then_inc(s_fo, 1)

                dve.memset(small[:, 0, :], 1.0)
                dve.memset(fss[:, :, :], 1.0)
                dve.wait_ge(s_co, 1)
                for b in range(2):
                    dve.tensor_copy(co[0:KEEP, 512 * b:512 * b + 512], MISC[b][0:KEEP, :])
                dve.tensor_copy(stn[:, :], MISC[2][0:H * NCOND, 0:P]).then_inc(s_cc, 2)
                for m in range(KC):
                    if m % 3 == 1:
                        continue
                    dve.wait_ge(s_mh, m + 1)
                    dve.tensor_tensor(g.Hl[:, m, :], mixed(m), g.Hh[:, m, :].bitcast(F32), ALU.subtract).then_inc(s_mlv, 1)
                run(dve, step)
                dve.wait_ge(s_gf, 16)
                for t in range(NT + 1):
                    if t < NT:
                        n = P if t < NC else NS
                        dve.wait_ge(s_fs, 2 * t + 2)
                        link(dve.tensor_tensor(fss[0:n, t, 2:3], fss[0:n, t, 0:1], fss[0:n, t, 1:2], ALU.add))
                        dve.tensor_scalar(fss[:, t, 2:3], fss[:, t, 2:3], 1.0 / D, EPS, ALU.mult, ALU.add).then_inc(s_fm, 1)
                    if t:
                        rows_out(t - 1)


class Shared:
    pass


def build(nc, a, outs, loops=True):
    a = dict(a, **outs)
    g = Shared()
    g.dve_per = DVE_PER
    g.x_d = nc.dram_tensor("x_scratch", (P, KC, T), F32, kind="Internal").ap()
    g.mix_d = nc.dram_tensor("mix_scratch", (P, KC, T), F32, kind="Internal").ap()
    with ExitStack() as ctx:
        sb = lambda n, s, d=F32: ctx.enter_context(nc.sbuf_tensor(n, s, d))
        g.ps = [ctx.enter_context(nc.psum_tensor(f"bank{n}", [P, 512], F32)) for n in range(8)]
        g.Hh = sb("h_hi", [P, KC, T], F32R)
        g.Hl = sb("h_lo", [P, KC, T], F32R)
        g.ident = sb("identity", [P, P])
        g.ones = sb("ones", [P, P])
        g.cmask = sb("causal", [P, P])
        g.cmask_s = sb("causal_samples", [NS, NS])
        g.lmask = sb("level_masks", [P, NL, P], U8)
        g.seqcol = sb("seq_columns", [NS, NSEQ])
        g.seqrow = sb("seq_rows", [P, NSEQ, NS])
        g.reset = sb("resets", [P, T], BF16)
        g.vec = sb("vectors", [P, P])
        g.cT = sb("c_t", [P, KC, NCOND])
        g.ada = sb("ada", [P, 6 * KC, NCOND])
        g.sconvT = sb("state_conv_t", [P, KC, NSEQ * (W4 - 1)])
        g.n0T = sb("state_n_t", [P, NSEQ * H])
        g.pk = sb("conv_keep", [P, KC, KEEP])
        g.nout = sb("n_out", [P, H * NCOND])
        g.early = sb("early", [P, NEARLY, ZN])
        g.s_early = ctx.enter_context(nc.semaphore("mix_loaded_early"))
        g.raw = sb("w_raw", [P, RAW, 4, P])
        g.s_w = [ctx.enter_context(nc.semaphore(f"w_loaded{n}")) for n in range(RAW)]
        setup_phase(nc, g, a)
        mixer_phase(nc, g, a, loops)
        ffn_phase(nc, g, a, loops)


DVE_PER = 34
LOOPS = True

_INS = ["x_prompt", "x_sample", "state_conv", "state_C", "state_n", "state_m", "state_S", "c_prompt", "c_sample",
        "g_norm1", "g_norm2", "w_ada", "b_ada", "w_in", "conv_w", "conv_b", "b_igate", "b_fgate", "g_head_a",
        "w_alpha", "b_alpha", "g_head_b", "w_out", "w_ffn_gate", "w_ffn_up", "w_ffn_down", "g_final"]
_OUTS = [("y_prompt", (1, SEQ, D)), ("y_sample", (NSEQ, SLEN, D)),
         ("conv_p", (1, 1, W4 - 1, 2 * QK)), ("C_p", (1, 1, H, DK, DV)), ("n_p", (1, 1, H, DK)), ("m_p", (1, 1, H)),
         ("S_p", (1, 1, H, DK, DV)),
         ("conv_s", (1, NSEQ, W4 - 1, 2 * QK)), ("C_s", (1, NSEQ, H, DK, DV)), ("n_s", (1, NSEQ, H, DK)), ("m_s", (1, NSEQ, H)),
         ("S_s", (1, NSEQ, H, DK, DV))]


def kernel(**inputs):
    import numpy as _np
    import concourse.bacc as _bacc
    from concourse.bass_utils import run_bass_kernel_spmd as _run

    nc = _bacc.Bacc("TRN2", target_bir_lowering=False, num_devices=1)
    arrays, args, outs = {}, {}, {}
    for name in _INS:
        x = _np.ascontiguousarray(inputs[name])
        arrays[f"in_{name}"] = x
        args[name] = nc.dram_tensor(f"in_{name}", x.shape, F32, kind="ExternalInput").ap()
    for name, shape in _OUTS:
        outs[name] = nc.dram_tensor(f"out_{name}", shape, F32, kind="ExternalOutput").ap()
    build(nc, args, outs, LOOPS)
    r = _run(nc, [arrays], core_ids=[0])
    return tuple(r.results[0][f"out_{name}"] for name, _ in _OUTS)
```
